# Optimizing a Trainium2 kernel written in Bass

```python
import math, functools
import jax, jax.numpy as jnp
from jax import lax
import numpy as np

D_MODEL = 1024
BATCH = 1
SEQ = 1024
DEPTH = 1

D_MIX = D_MODEL
N_ATT_HEADS = 8
HEAD_DIM = 64
D_ATT = N_ATT_HEADS * HEAD_DIM
D_POOL = D_MIX - D_ATT
POOL_WINDOWS = (2, 4, 8, 16)
N_POOL_GROUPS = len(POOL_WINDOWS)
POOL_GROUP = D_POOL // N_POOL_GROUPS
DILATED_BRANCHES = ((128, 1), (512, 4), (2048, 16))
MAX_DIL = 16
BLOCK = 128
ROPE_THETA = 10000.0
EPS = 1e-6
N_KEYS = 128
N_EXPERTS = N_KEYS * N_KEYS
PEER_HEADS = 8
PEER_KEY_DIM = 256
PEER_HALF = PEER_KEY_DIM // 2
PEER_TOPK = 16
PEER_CHUNK = 128

kernel_name = "hymba_dilated_pool_peer_block"

def _rmsnorm(x, g):
    xf = x.astype(jnp.float32)
    y = xf * lax.rsqrt(jnp.mean(xf * xf, axis=-1, keepdims=True) + EPS)
    return (y * g.astype(jnp.float32)).astype(x.dtype)

def _rope(x, pos):
    hd = x.shape[-1]
    freqs = ROPE_THETA ** (-jnp.arange(0, hd, 2, dtype=jnp.float32) / hd)
    ang = pos[:, None] * freqs[None, :]
    cos = jnp.cos(ang)[None, :, None, :]
    sin = jnp.sin(ang)[None, :, None, :]
    xf = x.astype(jnp.float32)
    x1, x2 = xf[..., : hd // 2], xf[..., hd // 2:]
    return jnp.concatenate([x1 * cos - x2 * sin, x2 * cos + x1 * sin], axis=-1)

def _dilated_branch(q, k, v, dil, n_back):
    B, H, Sp, hd = q.shape
    L = Sp // dil
    nb = L // BLOCK

    def to_blocks(t):
        t = t.reshape(B, H, L, dil, hd).transpose(0, 1, 3, 2, 4)
        return t.reshape(B, H, dil, nb, BLOCK, hd)

    def with_prev(t):
        prev = jnp.pad(t, ((0, 0), (0, 0), (0, 0), (1, 0), (0, 0), (0, 0)))[:, :, :, :nb]
        return jnp.concatenate([prev, t], axis=4)

    qb = to_blocks(q)
    kc = with_prev(to_blocks(k))
    vc = with_prev(to_blocks(v))
    s = jnp.einsum('bhrnqd,bhrnkd->bhrnqk', qb, kc)
    a = jnp.arange(BLOCK)[:, None]
    c = jnp.arange(2 * BLOCK)[None, :]
    dist = a - c + BLOCK
    kidx = jnp.arange(nb)[:, None, None] * BLOCK + c[None] - BLOCK
    valid = (dist >= 0) & (dist <= n_back) & (kidx >= 0)
    s = jnp.where(valid, s, -jnp.inf)
    m = jnp.max(s, axis=-1, keepdims=True)
    p = jnp.exp(s - m)
    l = jnp.sum(p, axis=-1, keepdims=True)
    o = jnp.einsum('bhrnqk,bhrnkd->bhrnqd', p, vc) / l
    lse = (m + jnp.log(l))[..., 0]
    o = o.reshape(B, H, dil, L, hd).transpose(0, 1, 3, 2, 4).reshape(B, H, Sp, hd)
    lse = lse.reshape(B, H, dil, L).transpose(0, 1, 3, 2).reshape(B, H, Sp)
    return o, lse

def _dilated_attention(q, k, v):
    B, H, S, hd = q.shape
    unit = MAX_DIL * BLOCK
    Sp = -(-S // unit) * unit
    pad = ((0, 0), (0, 0), (0, Sp - S), (0, 0))
    q = jnp.pad(q * (HEAD_DIM ** -0.5), pad)
    k = jnp.pad(k, pad)
    v = jnp.pad(v, pad)
    outs, lses = [], []
    for window, dil in DILATED_BRANCHES:
        o_i, lse_i = _dilated_branch(q, k, v, dil, window // dil)
        outs.append(o_i)
        lses.append(lse_i)
    wts = jax.nn.softmax(jnp.stack(lses, axis=0), axis=0)
    o = jnp.einsum('gbhs,gbhsd->bhsd', wts, jnp.stack(outs, axis=0))
    return o[:, :, :S]

def _trailing_mean_minus_self(x, w):
    S = x.shape[1]
    csum = jnp.pad(jnp.cumsum(x, axis=1), ((0, 0), (1, 0), (0, 0)))
    hi = csum[:, 1:]
    lo = jnp.pad(csum, ((0, 0), (w - 1, 0), (0, 0)))[:, :S]
    cnt = jnp.minimum(jnp.arange(S) + 1, w).astype(jnp.float32)
    return (hi - lo) / cnt[None, :, None] - x

def _pool_mixer(p, pool_w, pool_scale):
    B, S, _ = p.shape
    pg = p.astype(jnp.float32).reshape(B, S, N_POOL_GROUPS, POOL_GROUP)
    pooled = jnp.stack([_trailing_mean_minus_self(pg[:, :, g], w)
                        for g, w in enumerate(POOL_WINDOWS)], axis=2)
    y = jnp.einsum('bsgc,gcd->bsgd', pooled, pool_w.astype(jnp.float32))
    return y.reshape(B, S, D_POOL) * pool_scale.astype(jnp.float32)

def _peer(h, w_query, sub_keys, expert_u, expert_v):
    B, S, D = h.shape
    T = B * S
    ht = h.reshape(T, D)
    q = (ht @ w_query).astype(jnp.float32).reshape(T, PEER_HEADS, 2, PEER_HALF)
    s = jnp.einsum('thpc,hpnc->thpn', q, sub_keys.astype(jnp.float32))
    s_top, i_top = lax.top_k(s, PEER_TOPK)
    cand = (s_top[:, :, 0, :, None] + s_top[:, :, 1, None, :]).reshape(T, PEER_HEADS, -1)
    cand_idx = (i_top[:, :, 0, :, None] * N_KEYS + i_top[:, :, 1, None, :]).reshape(T, PEER_HEADS, -1)
    best, pos = lax.top_k(cand, PEER_TOPK)
    idx = jnp.take_along_axis(cand_idx, pos, axis=-1)
    gate = jax.nn.softmax(best, axis=-1)
    n_chunks = T // PEER_CHUNK
    xs = (ht.reshape(n_chunks, PEER_CHUNK, D),
          idx.reshape(n_chunks, PEER_CHUNK, PEER_HEADS * PEER_TOPK),
          gate.reshape(n_chunks, PEER_CHUNK, PEER_HEADS * PEER_TOPK))

    def chunk_fn(args):
        xc, ic, gc = args
        u = expert_u[ic]
        a = jnp.einsum('ckd,cd->ck', u.astype(jnp.float32), xc.astype(jnp.float32))
        act = jax.nn.gelu(a, approximate=False) * gc
        vsel = expert_v[ic]
        return jnp.einsum('ck,ckd->cd', act, vsel.astype(jnp.float32))

    y = lax.map(chunk_fn, xs)
    return y.reshape(B, S, D)

def setup_inputs(seed: int = 0) -> dict:
    key = jax.random.key(seed)
    ks = jax.random.split(key, 14)
    f32 = jnp.float32
    nrm = lambda k, shape, scale: (jax.random.normal(k, shape, f32) * scale)
    return {
        "x": nrm(ks[0], (BATCH, SEQ, D_MODEL), 1.0),
        "attn_norm_g": 1.0 + nrm(ks[1], (DEPTH, D_MODEL), 0.1),
        "w_in": nrm(ks[2], (DEPTH, D_MODEL, 3 * D_ATT + D_POOL), D_MODEL ** -0.5),
        "q_norm_g": 1.0 + nrm(ks[3], (DEPTH, HEAD_DIM), 0.1),
        "k_norm_g": 1.0 + nrm(ks[4], (DEPTH, HEAD_DIM), 0.1),
        "pool_w": nrm(ks[5], (DEPTH, N_POOL_GROUPS, POOL_GROUP, POOL_GROUP), POOL_GROUP ** -0.5),
        "pool_scale": 1.0 + nrm(ks[6], (DEPTH, D_POOL), 0.1),
        "w_out": nrm(ks[7], (DEPTH, D_MIX, D_MODEL), D_MIX ** -0.5),
        "ffn_norm_g": 1.0 + nrm(ks[8], (DEPTH, D_MODEL), 0.1),
        "peer_w_query": nrm(ks[9], (DEPTH, D_MODEL, PEER_HEADS * PEER_KEY_DIM), D_MODEL ** -0.5),
        "peer_sub_keys": nrm(ks[10], (DEPTH, PEER_HEADS, 2, N_KEYS, PEER_HALF), PEER_HALF ** -0.5),
        "peer_u": nrm(ks[11], (DEPTH, N_EXPERTS, D_MODEL), D_MODEL ** -0.5),
        "peer_v": nrm(ks[12], (DEPTH, N_EXPERTS, D_MODEL), (PEER_HEADS) ** -0.5),
    }

def reference(x, attn_norm_g, w_in, q_norm_g, k_norm_g, pool_w, pool_scale, w_out,
              ffn_norm_g, peer_w_query, peer_sub_keys, peer_u, peer_v):
    B, S, D = x.shape
    pos = jnp.arange(S, dtype=jnp.float32)
    for l in range(DEPTH):
        h = _rmsnorm(x, attn_norm_g[l])
        proj = h @ w_in[l]
        q, k, v, p = jnp.split(proj, [D_ATT, 2 * D_ATT, 3 * D_ATT], axis=-1)
        q = _rope(_rmsnorm(q.reshape(B, S, N_ATT_HEADS, HEAD_DIM), q_norm_g[l]), pos)
        k = _rope(_rmsnorm(k.reshape(B, S, N_ATT_HEADS, HEAD_DIM), k_norm_g[l]), pos)
        v = v.astype(jnp.float32).reshape(B, S, N_ATT_HEADS, HEAD_DIM)
        att = _dilated_attention(q.transpose(0, 2, 1, 3), k.transpose(0, 2, 1, 3),
                                 v.transpose(0, 2, 1, 3))
        att = att.transpose(0, 2, 1, 3).reshape(B, S, D_ATT)
        pool = _pool_mixer(p, pool_w[l], pool_scale[l])
        mixed = jnp.concatenate([att, pool], axis=-1).astype(x.dtype)
        x = x + (mixed @ w_out[l]).astype(x.dtype)
        h2 = _rmsnorm(x, ffn_norm_g[l])
        x = x + _peer(h2, peer_w_query[l], peer_sub_keys[l], peer_u[l], peer_v[l]).astype(x.dtype)
    return x


_drawn_inputs = setup_inputs


def setup_inputs(seed=0):
    import zlib

    import numpy as np

    out = dict(_drawn_inputs(seed))
    spreads = {}
    factors = {'q_norm_g': 3.092, 'k_norm_g': 3.566}
    for name, (base, spread) in spreads.items():
        noise = np.random.default_rng([zlib.crc32(name.encode()), seed]).standard_normal(out[name].shape)
        drawn = base * np.exp(spread * noise) if base else spread * noise
        out[name] = __import__('jax').numpy.asarray(drawn.astype(out[name].dtype))
    for name, factor in factors.items():
        out[name] = (out[name] * factor).astype(out[name].dtype)
    return out
```

```python
from contextlib import ExitStack

import numpy as np
import concourse.bass as bass
from concourse import mybir

F32 = mybir.dt.float32
F32R = mybir.dt.float32r
U32 = mybir.dt.uint32
ALU = mybir.AluOpType
ACT = mybir.ActivationFunctionType
AX = mybir.AxisListType
ds = bass.ds

P = 128
T = 1024
NT = T // P
D = 1024
KD = D // P
HALF = 512
HEADS = 8
HD = 64
DA = HEADS * HD
WINDOWS = (2, 4, 8, 16)
NG = len(WINDOWS)
PAD = max(WINDOWS)
EPS = 1e-6
KEYS = 128
PH = 8
TOPK = 16
NEG = -1e30
LOWEST = -3.0e38
RING = 4


def hold(eng, sem, value, passed):
    eng.wait_ge(sem, value)
    eng.sem_inc(passed, 1)


def banks(nc, ctx, name):
    return ctx.enter_context(nc.psum_tensor(name, [P, 8, HALF], F32))


def norm_and_transpose(nc, name, X, x_dram, gain_row, scratch, hT_hi, hT_lo, ident, ident_dram, spill, extra=None):
    with ExitStack() as ctx:
        sem = lambda n: ctx.enter_context(nc.semaphore(f"{name}_{n}"))
        ps = banks(nc, ctx, f"{name}_ps")
        stats = ctx.enter_context(nc.sbuf_tensor(f"{name}_stats", [P, 4, NT], F32))
        ssq, mean, root, rstd = (stats[:, i, :] for i in range(4))
        hn, gain, junk = scratch[:, 0:2048], scratch[:, 2048:3072], scratch[:, 3072:4096]
        x_in = [sem(f"x_in{i}") for i in range(NT)]
        consts_in, spilled, extra_in = sem("consts_in"), sem("spilled"), sem("extra_in")
        squares, mean_ready, root_ready, rstd_ready = sem("squares"), sem("mean"), sem("root"), sem("rstd")
        hn_ready, turned, hi_ready, lo_ready = sem("hn"), sem("turned"), sem("hi"), sem("lo")
        block = ctx.enter_context(nc.Block())

        @block.sync
        def _(sp):
            if x_dram is not None:
                for tt in range(NT):
                    sp.dma_start(X[:, tt, :], x_dram[tt * P:(tt + 1) * P, :]).then_inc(x_in[tt], 16)
                sp.dma_start(ident[:, :], ident_dram).then_inc(consts_in, 16)
            sp.dma_start(gain, gain_row.partition_broadcast(P)).then_inc(consts_in, 16)
            if extra is not None:
                sp.dma_start(*extra).then_inc(extra_in, 16)
                sp.wait_ge(extra_in, 16)
            if spill is not None:
                sp.dma_start(spill.rearrange("(n p) d -> p n d", p=P), X[:, :, :]).then_inc(spilled, 16)
                sp.wait_ge(spilled, 16)

        @block.scalar
        def _(act):
            for tt in range(NT):
                if x_dram is not None:
                    act.wait_ge(x_in[tt], 16)
                if tt:
                    act.wait_ge(squares, tt)
                act.activation(junk, X[:, tt, :], ACT.Square, accum_out=ssq[:, tt:tt + 1]).then_inc(squares, 1)
            act.wait_ge(mean_ready, 1)
            act.activation(root, mean, ACT.Sqrt).then_inc(root_ready, 1)
            for tt in range(NT):
                act.wait_ge(turned, tt + 1)
                act.activation(hT_hi[:, :, tt * P:(tt + 1) * P],
                               ps[:, 2 * (tt % 2):2 * (tt % 2) + 2, :].rearrange("p b (k t) -> p (b k) t", t=P),
                               ACT.Copy).then_inc(hi_ready, 1)

        @block.vector
        def _(dve):
            dve.wait_ge(squares, NT)
            dve.tensor_scalar(mean, ssq, 1.0 / D, EPS, ALU.mult, ALU.add).then_inc(mean_ready, 1)
            dve.wait_ge(root_ready, 1)
            dve.reciprocal(rstd, root).then_inc(rstd_ready, 1)
            dve.wait_ge(rstd_ready, 1)
            dve.wait_ge(consts_in, 32 if x_dram is not None else 16)

            def scale_tile(tt):
                if tt >= 2:
                    dve.wait_ge(turned, tt - 1)
                dve.scalar_tensor_tensor(out=hn[:, (tt % 2) * D:(tt % 2 + 1) * D], in0=X[:, tt, :],
                                         scalar=rstd[:, tt:tt + 1], in1=gain, op0=ALU.mult,
                                         op1=ALU.mult).then_inc(hn_ready, 1)

            scale_tile(0)
            for tt in range(NT):
                if tt + 1 < NT:
                    scale_tile(tt + 1)
                dve.wait_ge(hi_ready, tt + 1)
                dve.tensor_tensor(hT_lo[:, :, tt * P:(tt + 1) * P],
                                  ps[:, 2 * (tt % 2):2 * (tt % 2) + 2, :].rearrange("p b (k t) -> p (b k) t", t=P),
                                  hT_hi[:, :, tt * P:(tt + 1) * P].bitcast(F32), ALU.subtract).then_inc(lo_ready, 1)

        @block.tensor
        def _(pe):
            pe.wait_ge(consts_in, 32 if x_dram is not None else 16)
            for tt in range(NT):
                pe.wait_ge(hn_ready, tt + 1)
                if tt >= 2:
                    pe.wait_ge(lo_ready, tt - 1)
                for k in range(KD):
                    ins = pe.transpose(ps[:, 2 * (tt % 2) + k // 4, (k % 4) * P:(k % 4 + 1) * P],
                                       hn[:, (tt % 2) * D + k * P:(tt % 2) * D + (k + 1) * P], ident[:, :])
                ins.then_inc(turned, 1)


class Weights:

    def __init__(self, nc, ctx, name):
        sem = lambda n: ctx.enter_context(nc.semaphore(f"{name}_{n}"))
        self.raw = ctx.enter_context(nc.sbuf_tensor(f"{name}_raw", [P, RING, HALF], F32))
        self.hi = ctx.enter_context(nc.sbuf_tensor(f"{name}_hi", [P, RING, HALF], F32R))
        self.lo = ctx.enter_context(nc.sbuf_tensor(f"{name}_lo", [P, RING, HALF], F32R))
        self.landed = [sem(f"landed{i}") for i in range(RING)]
        self.hi_ready, self.lo_ready, self.used = sem("hi_ready"), sem("lo_ready"), sem("used")


def product3(pe, out, left, right, first, last):
    (lh, ll), (rh, rl) = left, right
    pe.matmul(out, lh, rh, start=first, stop=False)
    pe.matmul(out, lh, rl, start=False, stop=False)
    return pe.matmul(out, ll, rh, start=False, stop=last)


def load_weights(eng, W, source, chunks):
    with eng.Fori(0, chunks) as c:
        for k in range(KD):
            eng.wait_ge(W.lo_ready, c * KD + k + 1)
            eng.dma_start(W.raw[:, k % RING, :], source[k * P:(k + 1) * P, ds(c * HALF, HALF)]).then_inc(
                W.landed[k % RING], 16)


def split_hi(act, W, c):
    for k in range(KD):
        act.wait_ge(W.landed[k % RING], 16 * (2 * c + k // RING + 1))
        act.wait_ge(W.used, c * KD + k + 1)
        act.activation(W.hi[:, k % RING, :], W.raw[:, k % RING, :], ACT.Copy).then_inc(W.hi_ready, 1)


def split_lo(eng, W, c):
    for k in range(KD):
        eng.wait_ge(W.hi_ready, c * KD + k + 1)
        eng.tensor_tensor(W.lo[:, k % RING, :], W.raw[:, k % RING, :],
                          W.hi[:, k % RING, :].bitcast(F32), ALU.subtract).then_inc(W.lo_ready, 1)


def wait_bank(eng, W, bank_done, c, b):
    if b < 7:
        eng.wait_ge(bank_done, c * 7 + b + 1)
    else:
        eng.wait_ge(W.used, RING + (c + 1) * KD)


def weight_chunk(pe, W, ps, c, free, bank_done, operands):
    for k in range(KD):
        pe.wait_ge(W.lo_ready, RING + c * KD + k + 1)
        for b in range(8):
            if k == 0:
                free(b)
            left, right = operands(k, b)
            ins = product3(pe, ps[:, b, :], left, right, k == 0, k == KD - 1)
            if k == KD - 1 and b < 7:
                ins.then_inc(bank_done, 1)
        ins.then_inc(W.used, 1)


def token_operands(W, hT_hi, hT_lo):
    return lambda k, b: ((hT_hi[:, k, b * P:(b + 1) * P], hT_lo[:, k, b * P:(b + 1) * P]),
                         (W.hi[:, k % RING, :], W.lo[:, k % RING, :]))


def channel_operands(W, hT_hi, hT_lo):
    def at(k, b):
        n, t = (b % 4) * P, (b // 4) * HALF
        return ((W.hi[:, k % RING, n:n + P], W.lo[:, k % RING, n:n + P]),
                (hT_hi[:, k, t:t + HALF], hT_lo[:, k, t:t + HALF]))
    return at


def project_inputs(nc, w_in, hT_hi, hT_lo, QKV, poolT):
    with ExitStack() as ctx:
        sem = lambda n: ctx.enter_context(nc.semaphore(f"pi_{n}"))
        ps = banks(nc, ctx, "pi_ps")
        W = Weights(nc, ctx, "pi_w")
        bank_done, even_free, odd_free, zeroed = sem("bank_done"), sem("even_free"), sem("odd_free"), sem("zeroed")
        block = ctx.enter_context(nc.Block())

        def channel_slot(b):
            return poolT[:, b % 4, PAD + (b // 4) * HALF:PAD + (b // 4 + 1) * HALF]

        @block.sync
        def _(sp):
            load_weights(sp, W, w_in, 4)

        @block.scalar
        def _(act):
            with act.Fori(0, 3) as c:
                split_hi(act, W, c)
                for b in range(0, 8, 2):
                    wait_bank(act, W, bank_done, c, b)
                    act.activation(QKV[:, b, ds(c * HALF, HALF)], ps[:, b, :], ACT.Copy).then_inc(even_free, 1)
            split_hi(act, W, 3)
            for b in range(0, 8, 2):
                wait_bank(act, W, bank_done, 3, b)
                act.activation(channel_slot(b), ps[:, b, :], ACT.Copy).then_inc(even_free, 1)

        @block.vector
        def _(dve):
            dve.sem_inc(W.lo_ready, RING)
            dve.memset(poolT[:, :, 0:PAD], 0.0).then_inc(zeroed, 1)
            with dve.Fori(0, 3) as c:
                split_lo(dve, W, c)
                for b in range(1, 8, 2):
                    wait_bank(dve, W, bank_done, c, b)
                    dve.tensor_copy(QKV[:, b, ds(c * HALF, HALF)], ps[:, b, :]).then_inc(odd_free, 1)
            split_lo(dve, W, 3)
            for b in range(1, 8, 2):
                wait_bank(dve, W, bank_done, 3, b)
                dve.tensor_copy(channel_slot(b), ps[:, b, :]).then_inc(odd_free, 1)

        @block.tensor
        def _(pe):
            pe.sem_inc(W.used, RING)
            pe.sem_inc(even_free, 4)
            pe.sem_inc(odd_free, 4)

            def free(c):
                return lambda b: pe.wait_ge((even_free, odd_free)[b % 2], c * 4 + b // 2 + 1)

            with pe.Fori(0, 3) as c:
                weight_chunk(pe, W, ps, c, free(c), bank_done, token_operands(W, hT_hi, hT_lo))
            weight_chunk(pe, W, ps, 3, free(3), bank_done, channel_operands(W, hT_hi, hT_lo))


def prepare_heads(nc, QKV, QT, cos, sin, gains, ident, consts):
    NH = 2 * HEADS
    with ExitStack() as ctx:
        sem = lambda n: ctx.enter_context(nc.semaphore(f"ph_{n}"))
        sb = lambda n, s: ctx.enter_context(nc.sbuf_tensor(f"ph_{n}", s, F32))
        ps = banks(nc, ctx, "ph_ps")
        square = sb("square", [P, 2, 2 * DA])
        stats = sb("stats", [P, 3, NT, NH])
        normed, turnc, turns = sb("normed", [P, 2 * DA]), sb("turnc", [P, 2 * DA]), sb("turns", [P, 2 * DA])
        consts_in, squared, summed = sem("consts_in"), sem("squared"), sem("summed")
        mean_ready, root_ready, rstd_ready = sem("mean"), sem("root"), sem("rstd")
        normed_ready, gained, cos_ready = sem("normed_r"), sem("gained"), sem("cos")
        sin_ready, rotated, turned, QT_ready = sem("sin"), sem("rotated"), sem("turned"), sem("QT")
        block = ctx.enter_context(nc.Block())
        heads = lambda ap: ap.rearrange("p (h d) -> p h d", d=HD)
        halves = lambda ap: ap.rearrange("p (h s d) -> p h s d", s=2, d=HD // 2)

        @block.sync
        def _(sp):
            for to, source in consts:
                sp.dma_start(to, source).then_inc(consts_in, 16)

        @block.scalar
        def _(act):
            for tt in range(NT):
                if tt >= 2:
                    act.wait_ge(summed, tt - 1)
                act.activation(square[:, tt % 2, :], QKV[:, tt, 0:2 * DA], ACT.Square).then_inc(squared, 1)
            act.wait_ge(mean_ready, 1)
            act.activation(stats[:, 1], stats[:, 0], ACT.Sqrt).then_inc(root_ready, 1)
            with act.Fori(0, NT) as tt:
                act.wait_ge(turned, tt + 2)
                act.activation(QT[:, 0:4, ds(tt * P, P)], ps[:, 0, :].rearrange("p (a t) -> p a t", t=P),
                               ACT.Copy, scale=HD ** -0.5).then_inc(QT_ready, 1)
                act.activation(QT[:, 4:8, ds(tt * P, P)], ps[:, 1, :].rearrange("p (a t) -> p a t", t=P),
                               ACT.Copy).then_inc(QT_ready, 1)

        @block.gpsimd
        def _(pool):
            pool.wait_ge(consts_in, 16 * len(consts))
            with pool.Fori(0, NT) as tt:
                pool.wait_ge(gained, tt + 1)
                pool.wait_ge(rotated, tt + 1)
                s = sin[:, ds(tt, 1), :].broadcast_to([P, NH, HD // 2])
                x, o = halves(normed[:, :]), halves(turns[:, :])
                pool.tensor_tensor(o[:, :, 0, :], x[:, :, 1, :], s, ALU.mult).then_inc(sin_ready, 1)
                pool.tensor_tensor(o[:, :, 1, :], x[:, :, 0, :], s, ALU.mult).then_inc(sin_ready, 1)

        @block.vector
        def _(dve):
            for tt in range(NT):
                dve.wait_ge(squared, tt + 1)
                dve.tensor_reduce(stats[:, 2, tt, :], heads(square[:, tt % 2, :]), AX.X, ALU.add).then_inc(summed, 1)
            dve.wait_ge(summed, NT)
            dve.tensor_scalar(stats[:, 0], stats[:, 2], 1.0 / HD, EPS, ALU.mult, ALU.add).then_inc(mean_ready, 1)
            dve.wait_ge(root_ready, 1)
            dve.reciprocal(stats[:, 2], stats[:, 1]).then_inc(rstd_ready, 1)
            dve.wait_ge(rstd_ready, 1)
            dve.wait_ge(consts_in, 16 * len(consts))
            dve.sem_inc(rotated, 1)
            with dve.Fori(0, NT) as tt:
                dve.wait_ge(rotated, tt + 1)
                dve.tensor_tensor(heads(turnc[:, :]), heads(QKV[:, ds(tt, 1), 0:2 * DA].rearrange("p a n -> p (a n)")),
                                  stats[:, 2, ds(tt, 1), :].rearrange("p a h -> p h a").broadcast_to([P, NH, HD]),
                                  ALU.mult).then_inc(normed_ready, 1)
                dve.wait_ge(normed_ready, tt + 1)
                dve.tensor_tensor(normed[:, :].rearrange("p (a h d) -> p a h d", a=2, d=HD),
                                  turnc[:, :].rearrange("p (a h d) -> p a h d", a=2, d=HD),
                                  gains[:, :, :].unsqueeze(2).broadcast_to([P, 2, HEADS, HD]),
                                  ALU.mult).then_inc(gained, 1)
                dve.wait_ge(gained, tt + 1)
                dve.tensor_tensor(turnc[:, :].rearrange("p (h d) -> p h d", d=HD // 2),
                                  normed[:, :].rearrange("p (h d) -> p h d", d=HD // 2),
                                  cos[:, ds(tt, 1), :].broadcast_to([P, 2 * NH, HD // 2]), ALU.mult).then_inc(cos_ready, 1)
                dve.wait_ge(cos_ready, tt + 1)
                dve.wait_ge(sin_ready, 2 * tt + 2)
                dve.wait_ge(turned, tt + 1)
                out, c, s = halves(square[:, 0, :]), halves(turnc[:, :]), halves(turns[:, :])
                dve.tensor_tensor(out[:, :, 0, :], c[:, :, 0, :], s[:, :, 0, :], ALU.subtract)
                dve.tensor_tensor(out[:, :, 1, :], c[:, :, 1, :], s[:, :, 1, :], ALU.add).then_inc(rotated, 1)

        @block.tensor
        def _(pe):
            pe.sem_inc(turned, 1)
            pe.sem_inc(QT_ready, 2)
            with pe.Fori(0, NT) as tt:
                pe.wait_ge(rotated, tt + 2)
                pe.wait_ge(QT_ready, 2 * tt + 2)
                for pair in range(8):
                    ins = pe.transpose(ps[:, pair // 4, (pair % 4) * P:(pair % 4 + 1) * P],
                                       square[:, 0, pair * P:(pair + 1) * P], ident[:, :])
                ins.then_inc(turned, 1)


def attend(nc, QKV, QT, O, poolT, inv_count, mask_dram, ident):
    stage = QKV[:, 0:2, 0:T]
    pooled = QKV[:, 4:8, 0:T]
    UNITS = 2 * NT
    with ExitStack() as ctx:
        sem = lambda n: ctx.enter_context(nc.semaphore(f"at_{n}"))
        sb = lambda n, s: ctx.enter_context(nc.sbuf_tensor(f"at_{n}", s, F32))
        ps = banks(nc, ctx, "at_ps")
        mask, masked, probs, probsT = sb("mask", [P, T]), sb("masked", [P, 2, T]), sb("probs", [P, 2, T]), sb("probsT", [P, 2, T])
        small = sb("small", [P, 4, 2])
        windows = sb("windows", [P, 2, PAD + T])
        mask_in, staged, scores_ready, masked_ready = sem("mask_in"), sem("staged"), sem("scores"), sem("masked_r")
        negmax_ready, probs_ready, turned = sem("negmax"), sem("probs_r"), sem("turned")
        left_ready, right_ready, pv_done = sem("left"), sem("right"), sem("pv")
        inv_ready, out_ready, pair_done, pool_step = sem("inv"), sem("out"), sem("pair"), sem("pool_step")
        passed = sem("passed")
        block = ctx.enter_context(nc.Block())
        scores = lambda u: ps[:, 2 * (u % 2):2 * (u % 2) + 2, :].rearrange("p b n -> p (b n)")
        psT = ps[:, 4:6, :].rearrange("p b n -> p (b n)")
        psO = lambda u: ps[:, 6 + u % 2, 0:HD]
        cols = lambda u: (u % NT + 1) * P

        def rights(u):
            return sum(cols(w) > HALF for w in range(u + 1))

        @block.sync
        def _(sp):
            sp.dma_start(mask[:, :], mask_dram).then_inc(mask_in, 16)
            with sp.Fori(0, HEADS // 2) as pair:
                sp.wait_ge(pair_done, pair + 1)
                sp.dma_start(stage[:, 0, :], QT[:, ds(pair, 1), :].rearrange("p a t -> p (a t)")).then_inc(staged, 16)
                sp.dma_start(stage[:, 1, :], QT[:, ds(pair + 4, 1), :].rearrange("p a t -> p (a t)")).then_inc(staged, 16)

        @block.tensor
        def _(pe):
            pe.sem_inc(pair_done, 1)
            with pe.Fori(0, HEADS // 2) as pair:
                pe.wait_ge(staged, 32 * pair + 32)
                for step in range(UNITS + 2):
                    if step < UNITS:
                        u, rows = step, slice((step // NT) * HD, (step // NT + 1) * HD)
                        if u >= 2:
                            pe.wait_ge(masked_ready, UNITS * pair + u - 1)
                        for c0 in range(0, cols(u), HALF):
                            c1 = min(c0 + HALF, cols(u))
                            ins = pe.matmul(scores(u)[:, c0:c1], stage[rows, 0, (u % NT) * P:(u % NT + 1) * P],
                                            stage[rows, 1, c0:c1], start=True, stop=True)
                        ins.then_inc(scores_ready, 1)
                        if u == UNITS - 1:
                            pe.wait_ge(scores_ready, UNITS * (pair + 1))
                            pe.sem_inc(pair_done, 1)
                    if 0 < step <= UNITS:
                        u = step - 1
                        pe.wait_ge(probs_ready, UNITS * pair + u + 1)
                        if u >= 1:
                            pe.wait_ge(left_ready, UNITS * pair + u)
                            if cols(u - 1) > HALF:
                                pe.wait_ge(right_ready, NT * pair + rights(u - 1))
                        for b in range(u % NT + 1):
                            ins = pe.transpose(psT[:, b * P:(b + 1) * P], probs[:, u % 2, b * P:(b + 1) * P], ident[:, :])
                        ins.then_inc(turned, 1)
                    if step >= 2:
                        u = step - 2
                        pe.wait_ge(left_ready, UNITS * pair + u + 1)
                        if cols(u) > HALF:
                            pe.wait_ge(right_ready, NT * pair + rights(u))
                        if u >= 2:
                            pe.wait_ge(out_ready, UNITS * pair + u - 1)
                        n = u % NT + 1
                        for b in range(n):
                            ins = pe.matmul(psO(u), probsT[:, u % 2, b * P:(b + 1) * P],
                                            QKV[:, b, ds(2 * DA + pair * 2 * HD + (u // NT) * HD, HD)],
                                            start=b == 0, stop=b == n - 1)
                        ins.then_inc(pv_done, 1)

        @block.scalar
        def _(act):
            with act.Fori(0, HEADS // 2) as pair:
                for step in range(UNITS + 1):
                    if step < UNITS:
                        u, n = step, cols(step)
                        act.wait_ge(negmax_ready, UNITS * pair + u + 1)
                        if u >= 2:
                            act.wait_ge(turned, UNITS * pair + u - 1)
                            act.wait_ge(inv_ready, UNITS * pair + u - 1)
                        act.activation(probs[:, u % 2, 0:n], masked[:, u % 2, 0:n], ACT.Exp,
                                       bias=small[:, 1, u % 2:u % 2 + 1],
                                       accum_out=small[:, 2, u % 2:u % 2 + 1]).then_inc(probs_ready, 1)
                    if step >= 1:
                        u = step - 1
                        act.wait_ge(turned, UNITS * pair + u + 1)
                        if u >= 2:
                            act.wait_ge(pv_done, UNITS * pair + u - 1)
                        n = min(cols(u), HALF)
                        act.activation(probsT[:, u % 2, 0:n], psT[:, 0:n], ACT.Copy).then_inc(left_ready, 1)

        @block.vector
        def _(dve):
            dve.wait_ge(mask_in, 16)
            with dve.Fori(0, HEADS // 2) as pair:
                for step in range(UNITS + 2):
                    if step < UNITS:
                        u, n = step, cols(step)
                        if u >= 2:
                            dve.wait_ge(probs_ready, UNITS * pair + u - 1)
                        hold(dve, scores_ready, UNITS * pair + u + 1, passed)
                        dve.tensor_tensor_reduce(masked[:, u % 2, 0:n], scores(u)[:, 0:n], mask[:, T - n:T],
                                                 1.0, LOWEST, ALU.add, ALU.max,
                                                 small[:, 0, u % 2:u % 2 + 1]).then_inc(masked_ready, 1)
                        dve.wait_ge(masked_ready, UNITS * pair + u + 1)
                        dve.tensor_scalar(small[:, 1, u % 2:u % 2 + 1], small[:, 0, u % 2:u % 2 + 1], -1.0, None,
                                          ALU.mult).then_inc(negmax_ready, 1)
                    if 0 < step <= UNITS:
                        u = step - 1
                        if cols(u) > HALF:
                            dve.wait_ge(turned, UNITS * pair + u + 1)
                            if u >= 2:
                                dve.wait_ge(pv_done, UNITS * pair + u - 1)
                            dve.tensor_copy(probsT[:, u % 2, HALF:cols(u)], psT[:, HALF:cols(u)]).then_inc(right_ready, 1)
                    if step >= 2:
                        u = step - 2
                        slot = slice(u % 2, u % 2 + 1)
                        if u < UNITS:
                            dve.wait_ge(pv_done, UNITS * pair + u + 1)
                            dve.wait_ge(inv_ready, UNITS * pair + u + 1)
                            dve.tensor_scalar(O[:, u % NT, ds(pair * 2 * HD + (u // NT) * HD, HD)], psO(u),
                                              small[:, 3, slot], None, ALU.mult).then_inc(out_ready, 1)
                    if 0 < step <= UNITS:
                        u = step - 1
                        slot = slice(u % 2, u % 2 + 1)
                        dve.wait_ge(probs_ready, UNITS * pair + u + 1)
                        dve.reciprocal(small[:, 3, slot], small[:, 2, slot]).then_inc(inv_ready, 1)

        @block.gpsimd
        def _(pool):
            pool.memset(windows[:, :, 0:PAD], 0.0).then_inc(pool_step, 1)
            n = 1

            def step(ins):
                nonlocal n
                ins.then_inc(pool_step, 1)
                n += 1
                pool.wait_ge(pool_step, n)

            pool.wait_ge(pool_step, 1)
            for g, w in enumerate(WINDOWS):
                source, reach = poolT[:, g, :], 1
                while reach < w:
                    to = windows[:, reach.bit_length() % 2, :]
                    step(pool.tensor_tensor(to[:, PAD:], source[:, PAD:], source[:, PAD - reach:PAD + T - reach], ALU.add))
                    source, reach = to, 2 * reach
                step(pool.tensor_tensor(pooled[:, g, 0:PAD], source[:, PAD:2 * PAD], inv_count[:, g, :], ALU.mult))
                step(pool.tensor_scalar(pooled[:, g, PAD:T], source[:, 2 * PAD:], 1.0 / w, None, ALU.mult))
                step(pool.tensor_tensor(pooled[:, g, :], pooled[:, g, :], poolT[:, g, PAD:], ALU.subtract))
    return pooled


def mix(nc, O, pooled, pool_w, pool_scale, mixT_hi, mixT_lo, ident):
    with ExitStack() as ctx:
        sem = lambda n: ctx.enter_context(nc.semaphore(f"mx_{n}"))
        sb = lambda n, s: ctx.enter_context(nc.sbuf_tensor(f"mx_{n}", s, F32))
        ps = banks(nc, ctx, "mx_ps")
        w, scale, scaled = sb("w", [P, NG, P]), sb("scale", [P, NG]), sb("scaled", [P, 8, HALF])
        w_in, pooled_done, scaled_ready = sem("w_in"), sem("pooled_done"), sem("scaled")
        hi_ready, lo_ready, turned, oT_hi, oT_lo = sem("hi"), sem("lo"), sem("turned"), sem("oT_hi"), sem("oT_lo")
        block = ctx.enter_context(nc.Block())
        at = lambda m, n: m[:, NG + n // 2, (n % 2) * HALF:(n % 2 + 1) * HALF]
        att = lambda m, tt: m[:, 0:4, tt * P:(tt + 1) * P]
        turned_ps = lambda tt: ps[:, tt, :].rearrange("p (k t) -> p k t", t=P)

        @block.sync
        def _(sp):
            sp.dma_start(w[:, :, :], pool_w.rearrange("g c d -> c g d")).then_inc(w_in, 16)
            sp.dma_start(scale[:, :], pool_scale).then_inc(w_in, 16)

        @block.tensor
        def _(pe):
            pe.wait_ge(w_in, 32)
            for n in range(8):
                pe.matmul(ps[:, n, :], w[:, n // 2, :], pooled[:, n // 2, (n % 2) * HALF:(n % 2 + 1) * HALF],
                          start=True, stop=True).then_inc(pooled_done, 1)
            for tt in range(NT):
                pe.wait_ge(scaled_ready, tt + 1)
                for k in range(4):
                    ins = pe.transpose(ps[:, tt, k * P:(k + 1) * P], O[:, tt, k * P:(k + 1) * P], ident[:, :])
                ins.then_inc(turned, 1)

        @block.scalar
        def _(act):
            act.wait_ge(w_in, 32)
            for n in range(8):
                act.wait_ge(pooled_done, n + 1)
                act.activation(scaled[:, n, :], ps[:, n, :], ACT.Copy, scale=scale[:, n // 2:n // 2 + 1]).then_inc(scaled_ready, 1)
                act.wait_ge(scaled_ready, n + 1)
                act.activation(at(mixT_hi, n), scaled[:, n, :], ACT.Copy).then_inc(hi_ready, 1)
            for tt in range(NT):
                act.wait_ge(turned, tt + 1)
                act.activation(att(mixT_hi, tt), turned_ps(tt), ACT.Copy).then_inc(oT_hi, 1)

        @block.vector
        def _(dve):
            for n in range(8):
                dve.wait_ge(hi_ready, n + 1)
                dve.tensor_tensor(at(mixT_lo, n), scaled[:, n, :], at(mixT_hi, n).bitcast(F32), ALU.subtract).then_inc(lo_ready, 1)
            for tt in range(NT):
                dve.wait_ge(oT_hi, tt + 1)
                dve.tensor_tensor(att(mixT_lo, tt), turned_ps(tt), att(mixT_hi, tt).bitcast(F32), ALU.subtract).then_inc(oT_lo, 1)


def project_output(nc, w_out, mixT_hi, mixT_lo, X):
    with ExitStack() as ctx:
        sem = lambda n: ctx.enter_context(nc.semaphore(f"po_{n}"))
        ps = banks(nc, ctx, "po_ps")
        W = Weights(nc, ctx, "po_w")
        bank_done, added = sem("bank_done"), sem("added")
        block = ctx.enter_context(nc.Block())
        chunks = D // HALF

        @block.sync
        def _(sp):
            load_weights(sp, W, w_out, chunks)

        @block.scalar
        def _(act):
            with act.Fori(0, chunks) as c:
                split_hi(act, W, c)

        @block.vector
        def _(dve):
            dve.sem_inc(W.lo_ready, RING)
            with dve.Fori(0, chunks) as c:
                split_lo(dve, W, c)
                for b in range(8):
                    wait_bank(dve, W, bank_done, c, b)
                    x = X[:, b, ds(c * HALF, HALF)]
                    dve.tensor_tensor(x, ps[:, b, :], x, ALU.add).then_inc(added, 1)

        @block.tensor
        def _(pe):
            pe.sem_inc(W.used, RING)
            pe.sem_inc(added, 8)
            with pe.Fori(0, chunks) as c:
                weight_chunk(pe, W, ps, c, lambda b: pe.wait_ge(added, 8 * c + b + 1), bank_done,
                             token_operands(W, mixT_hi, mixT_lo))


def retrieve(nc, w_query, sub_keys, hT_hi, hT_lo, hT_spill, scores, picks, iota, ident):
    HC = 2
    CHUNKS = PH // HC
    LISTS = NT * HC
    with ExitStack() as ctx:
        sem = lambda n: ctx.enter_context(nc.semaphore(f"rt_{n}"))
        sb = lambda n, s, dt=F32: ctx.enter_context(nc.sbuf_tensor(f"rt_{n}", s, dt))
        ps = banks(nc, ctx, "rt_ps")
        W = Weights(nc, ctx, "rt_w")
        queryT, keysT = sb("queryT", [P, 2 * HC, T]), sb("keysT", [P, 2 * PH, KEYS])
        top, top_i = sb("top", [P, NT, 2 * HC, TOPK]), sb("top_i", [P, NT, 2 * HC, TOPK], U32)
        best, best_i = sb("best", [P, NT, HC, TOPK]), sb("best_i", [P, NT, HC, TOPK], U32)
        rest, cand = sb("rest", [P, 2 * HC, KEYS]), sb("cand", [P, 2, HC, TOPK * TOPK])
        rest2 = sb("rest2", [P, HC, TOPK * TOPK])
        match = sb("match", [P, LISTS // 2, TOPK, TOPK])
        ab, ab_i = sb("ab", [P, 2, NT, HC, TOPK]), sb("ab_i", [P, 2, NT, HC, TOPK], U32)
        topf, total = sb("topf", [P, NT, 2 * HC, TOPK]), sb("total", [P, 2, NT, PH])
        raw_keys = match[:, :, :, :].rearrange("p a b c -> p (a b c)").rearrange("p (n c) -> p n c", c=P)
        bank_done, keys_in, keys_turned, keys_ready = sem("bank_done"), sem("keys_in"), sem("keys_turned"), sem("keys")
        query_ready, scored, scores_ready, spilled = sem("query"), sem("scored"), sem("scores_r"), sem("spilled")
        scores_free, passed = sem("scores_free"), sem("passed")
        dec, shifted, exped, normed = sem("decode"), sem("shifted"), sem("exped"), sem("normed")
        block = ctx.enter_context(nc.Block())

        @block.sync
        def _(sp):
            sp.dma_start(raw_keys[:, 0:PH, :], sub_keys[0:PH * KEYS, :].rearrange("(g n) c -> n g c", n=KEYS)).then_inc(keys_in, 16)
            load_weights(sp, W, w_query, CHUNKS)
            sp.dma_start(hT_spill[0], hT_hi[:, :, :].bitcast(F32)).then_inc(spilled, 16)
            sp.dma_start(hT_spill[1], hT_lo[:, :, :].bitcast(F32)).then_inc(spilled, 16)
            sp.wait_ge(spilled, 32)

        @block.tensor
        def _(pe):
            for n in range(2 * PH // 4):
                pe.wait_ge(keys_in, 16 * (n // 2 + 1))
                for g in range(4):
                    ins = pe.transpose(ps[:, n, g * P:(g + 1) * P], raw_keys[:, (n % 2) * 4 + g, :], ident[:, :])
                ins.then_inc(keys_turned, 1)
            pe.wait_ge(keys_ready, 4)
            pe.sem_inc(W.used, RING)
            pe.sem_inc(scores_ready, 8)
            with pe.Fori(0, CHUNKS) as c:
                weight_chunk(pe, W, ps, c, lambda b: pe.wait_ge(scores_ready, 8 * c + b + 1), bank_done,
                             channel_operands(W, hT_hi, hT_lo))
                for tt in range(NT):
                    pe.wait_ge(query_ready, 8 * c + max(4 * (tt // 4) + 4, tt + 1))
                    for g in range(2 * HC):
                        ins = pe.matmul(ps[:, tt, g * KEYS:(g + 1) * KEYS], queryT[:, g, tt * P:(tt + 1) * P],
                                        keysT[:, ds(c * 2 * HC + g, 1), :].rearrange("p a n -> p (a n)"),
                                        start=True, stop=True)
                    ins.then_inc(scored, 1)

        @block.scalar
        def _(act):
            for n in range(2 * PH // 4):
                act.wait_ge(keys_turned, n + 1)
                act.activation(keysT[:, 4 * n:4 * n + 4, :], ps[:, n, :].rearrange("p (g c) -> p g c", c=P),
                               ACT.Copy).then_inc(keys_ready, 1)
                if n == 1:
                    act.dma_start(raw_keys[:, 0:PH, :],
                                  sub_keys[PH * KEYS:2 * PH * KEYS, :].rearrange("(g n) c -> n g c", n=KEYS)).then_inc(keys_in, 16)

            def chunk(c, buffer):
                split_hi(act, W, c)
                for b in range(8):
                    wait_bank(act, W, bank_done, c, b)
                    act.activation(queryT[:, b % 4, (b // 4) * HALF:(b // 4 + 1) * HALF], ps[:, b, :],
                                   ACT.Copy).then_inc(query_ready, 1)
                for tt in range(NT):
                    act.wait_ge(scored, 8 * c + tt + 1)
                    act.wait_ge(scores_free, 8 * c + tt + 1)
                    act.activation(scores[:, buffer, tt, :, :], ps[:, tt, :].rearrange("p (g n) -> p g n", n=KEYS),
                                   ACT.Copy).then_inc(scores_ready, 1)

            with act.Fori(0, CHUNKS // 2) as cc:
                chunk(2 * cc, 0)
                chunk(2 * cc + 1, 1)
            act.wait_ge(shifted, CHUNKS)
            act.activation(picks[:, :, 2, :], picks[:, :, 2, :], ACT.Exp).then_inc(exped, 1)

        @block.gpsimd
        def _(pool):
            pool.sem_inc(W.lo_ready, RING)
            with pool.Fori(0, CHUNKS) as c:
                split_lo(pool, W, c)

        @block.vector
        def _(dve):
            dve.sem_inc(scores_free, 2 * NT)

            def search_keys(c, buffer, tt):
                hold(dve, scores_ready, 8 * c + tt + 1 + 8, passed)
                s = scores[:, buffer, tt, :, :]
                for g in range(4):
                    dve.max(top[:, tt, g, 0:8], s[:, g, :])
                dve.drain()
                for g in range(4):
                    dve.match_replace(rest[:, g, :], top[:, tt, g, 0:8], s[:, g, :], LOWEST)
                for g in range(4):
                    ins = dve.max_index(top_i[:, tt, g, 0:8], top[:, tt, g, 0:8], s[:, g, :])
                ins.then_inc(scores_free, 1)
                dve.drain()
                for g in range(4):
                    dve.max(top[:, tt, g, 8:16], rest[:, g, :])
                dve.drain()
                for g in range(4):
                    dve.max_index(top_i[:, tt, g, 8:16], top[:, tt, g, 8:16], rest[:, g, :])

            def search_pairs(tt):
                sums = cand[:, tt % 2, :, :]
                for h in range(HC):
                    dve.tensor_tensor(sums[:, h, :].rearrange("p (a b) -> p a b", b=TOPK),
                                      top[:, tt, 2 * h, :].unsqueeze(2).broadcast_to([P, TOPK, TOPK]),
                                      top[:, tt, 2 * h + 1, :].unsqueeze(1).broadcast_to([P, TOPK, TOPK]), ALU.add)
                dve.drain()
                for h in range(HC):
                    dve.max(best[:, tt, h, 0:8], sums[:, h, :])
                dve.drain()
                for h in range(HC):
                    dve.match_replace(rest2[:, h, :], best[:, tt, h, 0:8], sums[:, h, :], LOWEST)
                for h in range(HC):
                    dve.max_index(best_i[:, tt, h, 0:8], best[:, tt, h, 0:8], sums[:, h, :])
                dve.drain()
                for h in range(HC):
                    dve.max(best[:, tt, h, 8:16], rest2[:, h, :])
                dve.drain()
                for h in range(HC):
                    dve.max_index(best_i[:, tt, h, 8:16], best[:, tt, h, 8:16], rest2[:, h, :])

            STEPS = 4 + 2 * (2 * 3)

            def decode(c):
                count = 0

                def step(ins):
                    nonlocal count
                    count += 1
                    ins.then_inc(dec, 1)
                    dve.wait_ge(dec, STEPS * c + count)

                dve.drain()
                dve.tensor_tensor(picks[:, :, 2, ds(c * HC * TOPK, HC * TOPK)].rearrange("p t (h r) -> p t h r", r=TOPK),
                                  best[:, :, :, :],
                                  best[:, :, :, 0:1].broadcast_to([P, NT, HC, TOPK]), ALU.subtract).then_inc(shifted, 1)
                step(dve.tensor_scalar(ab_i[:, 0], best_i[:, :, :, :], 4, None, ALU.logical_shift_right))
                step(dve.tensor_scalar(ab_i[:, 1], best_i[:, :, :, :], TOPK - 1, None, ALU.bitwise_and))
                step(dve.tensor_copy(ab[:, :, :, :, :].rearrange("p a t h r -> p (a t h r)"),
                                     ab_i[:, :, :, :, :].rearrange("p a t h r -> p (a t h r)")))
                step(dve.tensor_copy(topf[:, :, :, :], top_i[:, :, :, :]))
                for part in range(2):
                    for half in range(2):
                        tts = slice(half * NT // 2, (half + 1) * NT // 2)
                        position = ab[:, part, tts, :, :].rearrange("p t h r -> p (t h) r")
                        step(dve.tensor_tensor(match[:, :, :, :], position.unsqueeze(3).broadcast_to([P, LISTS // 2, TOPK, TOPK]),
                                               iota[:, 0:TOPK].unsqueeze(1).unsqueeze(1).broadcast_to([P, LISTS // 2, TOPK, TOPK]),
                                               ALU.is_equal))
                        lists = topf[:, tts, :, :].rearrange("p t (h q) a -> p (t h) q a", q=2)[:, :, part, :]
                        step(dve.tensor_tensor(match[:, :, :, :], match[:, :, :, :],
                                               lists.unsqueeze(2).broadcast_to([P, LISTS // 2, TOPK, TOPK]), ALU.mult))
                        out = picks[:, tts, part, ds(c * HC * TOPK, HC * TOPK)].rearrange("p t (h r) -> p t h r", r=TOPK)
                        step(dve.tensor_reduce(out, match[:, :, :, :].rearrange("p (t h) r a -> p t h r a", h=HC), AX.X, ALU.add))
                assert count == STEPS

            with dve.Fori(0, CHUNKS // 2) as cc:
                for half in range(2):
                    c = 2 * cc + half
                    for tt in range(NT):
                        search_keys(c, half, tt)
                        search_pairs(tt)
                    decode(c)
            gates = picks[:, :, 2, :].rearrange("p t (h r) -> p t h r", r=TOPK)
            dve.wait_ge(exped, 1)
            dve.tensor_reduce(total[:, 0, :, :], gates, AX.X, ALU.add).then_inc(normed, 1)
            dve.wait_ge(normed, 1)
            dve.reciprocal(total[:, 1, :, :], total[:, 0, :, :]).then_inc(normed, 1)
            dve.wait_ge(normed, 2)
            dve.tensor_tensor(gates, gates, total[:, 1, :, :].unsqueeze(3).broadcast_to([P, NT, PH, TOPK]),
                              ALU.mult).then_inc(normed, 1)


def spread_gates(nc, picks, iota, ident, gates):
    BLOCK = 4
    SLOTS = 4
    BLOCKS = P // BLOCK
    with ExitStack() as ctx:
        sem = lambda n: ctx.enter_context(nc.semaphore(f"sg_{n}"))
        sb = lambda n, s: ctx.enter_context(nc.sbuf_tensor(f"sg_{n}", s, F32))
        ps = banks(nc, ctx, "sg_ps")
        picksT = sb("picksT", [P, 3, T])
        rows, columns = sb("rows", [P, SLOTS, BLOCK, KEYS]), sb("columns", [P, SLOTS, BLOCK, KEYS])
        tile = [sb(f"tile{b}", [P, KEYS, P]) for b in range(2)]
        turned, picks_ready, rows_ready, columns_ready = sem("turned"), sem("picks"), sem("rows_r"), sem("columns_r")
        spread, tile_ready = sem("spread"), sem("tile_r")
        written = [sem("written0"), sem("written1")]
        block = ctx.enter_context(nc.Block())

        @block.tensor
        def _(pe):
            for n in range(6):
                for q in range(4):
                    tt = (n % 2) * 4 + q
                    ins = pe.transpose(ps[:, n, q * P:(q + 1) * P], picks[:, tt, n // 2, :], ident[:, :])
                ins.then_inc(turned, 1)
            pe.wait_ge(picks_ready, 6)
            pe.sem_inc(tile_ready, SLOTS)
            with pe.Fori(0, NT * BLOCKS // SLOTS) as n:
                for s in range(SLOTS):
                    pe.wait_ge(rows_ready, n * SLOTS + s + 1)
                    pe.wait_ge(columns_ready, n * SLOTS + s + 1)
                    pe.wait_ge(tile_ready, n * SLOTS + s + 1)
                    for q in range(BLOCK):
                        ins = pe.matmul(ps[:, s, q * KEYS:(q + 1) * KEYS], columns[:, s, q, :], rows[:, s, q, :],
                                        start=True, stop=True)
                    ins.then_inc(spread, 1)

        @block.vector
        def _(dve):
            for n in range(1, 6, 2):
                dve.wait_ge(turned, n + 1)
                dve.tensor_copy(picksT[:, n // 2, HALF:T], ps[:, n, :]).then_inc(picks_ready, 1)
            dve.wait_ge(picks_ready, 6)
            dve.sem_inc(spread, SLOTS)
            with dve.Fori(0, NT * BLOCKS // SLOTS) as n:
                for s in range(SLOTS):
                    dve.wait_ge(spread, n * SLOTS + s + 1)
                    for q in range(BLOCK):
                        t = (n * SLOTS + s) * BLOCK + q
                        ins = dve.tensor_scalar(rows[:, s, q, :], iota[:, :], picksT[:, 0, ds(t, 1)],
                                                picksT[:, 2, ds(t, 1)], ALU.is_equal, ALU.mult)
                    ins.then_inc(rows_ready, 1)
                    for q in range(BLOCK):
                        t = (n * SLOTS + s) * BLOCK + q
                        ins = dve.tensor_scalar(columns[:, s, q, :], iota[:, :], picksT[:, 1, ds(t, 1)], None, ALU.is_equal)
                    ins.then_inc(columns_ready, 1)

        @block.scalar
        def _(act):
            for n in range(0, 6, 2):
                act.wait_ge(turned, n + 1)
                act.activation(picksT[:, n // 2, 0:HALF], ps[:, n, :], ACT.Copy).then_inc(picks_ready, 1)
            with act.Fori(0, NT // 2) as pair:
                for b in range(2):
                    act.wait_ge(written[b], 16 * pair + 16)
                    with act.Fori(0, BLOCKS // SLOTS) as n:
                        for s in range(SLOTS):
                            done = (2 * pair + b) * BLOCKS + n * SLOTS + s + 1
                            act.wait_ge(spread, done + SLOTS)
                            act.activation(tile[b][:, :, ds((n * SLOTS + s) * BLOCK, BLOCK)],
                                           ps[:, s, :].rearrange("p (t i) -> p i t", i=KEYS), ACT.Copy).then_inc(tile_ready, 1)

        @block.sync
        def _(sp):
            for b in range(2):
                sp.sem_inc(written[b], 16)
            with sp.Fori(0, NT // 2) as pair:
                for b in range(2):
                    sp.wait_ge(tile_ready, SLOTS + (2 * pair + b + 1) * BLOCKS)
                    sp.dma_start(gates[:, :, ds((2 * pair + b) * P, P)].rearrange("i j t -> j i t"),
                                 tile[b][:, :, :]).then_inc(written[b], 16)
            for b in range(2):
                sp.wait_ge(written[b], 16 * (NT // 2 + 1))


def mix_experts(nc, u, v, gates, hT_spill, x_spill, X, ident, out):
    G = 2
    GROUPS = KEYS // G
    UNITS = 16
    OUT_BANKS = 4
    with ExitStack() as ctx:
        sem = lambda n: ctx.enter_context(nc.semaphore(f"me_{n}"))
        sb = lambda n, s, dt=F32: ctx.enter_context(nc.sbuf_tensor(f"me_{n}", s, dt))
        ps = banks(nc, ctx, "me_ps")
        hT = [sb("hT_hi", [P, KD, T], F32R), sb("hT_lo", [P, KD, T], F32R)]
        u_raw, v_raw, gate = sb("u_raw", [P, G, D]), sb("v_raw", [P, G, D]), sb("gate", [P, G, T])
        uT_hi, uT_lo = sb("uT_hi", [P, G, KD, P], F32R), sb("uT_lo", [P, G, KD, P], F32R)
        v_hi, v_lo = sb("v_hi", [P, G, D], F32R), sb("v_lo", [P, G, D], F32R)
        act_hi, act_lo = sb("act_hi", [P, G, T], F32R), sb("act_lo", [P, G, T], F32R)
        hidden = sb("hidden", [P, 2, HALF])
        hT_in, x_in, stored = sem("hT_in"), sem("x_in"), sem("stored")
        u_in, v_in, gate_in = ([sem(f"{n}{b}") for b in range(G)] for n in ("u_in", "v_in", "gate_in"))
        u_turned, uT_hi_ready, uT_lo_ready = sem("u_turned"), sem("uT_hi_r"), sem("uT_lo_r")
        v_hi_ready, v_lo_ready = sem("v_hi_r"), sem("v_lo_r")
        hidden_done, gelu_done, gated = sem("hidden_done"), sem("gelu"), sem("gated")
        act_hi_ready, act_lo_ready = sem("act_hi_r"), sem("act_lo_r")
        unit_done, added = sem("unit_done"), sem("added")
        block = ctx.enter_context(nc.Block())
        uT_ps = ps[:, 0:2, :].rearrange("p b (k e) -> p (b k) e", e=P)

        @block.sync
        def _(sp):
            def load(n, b):
                rows = lambda w: w[ds(n * KEYS, KEYS), :]
                sp.dma_start(u_raw[:, b, :], rows(u)).then_inc(u_in[b], 16)
                sp.dma_start(gate[:, b, :], gates[ds(n, 1), :, :].rearrange("a j t -> (a j) t")).then_inc(gate_in[b], 16)
                sp.dma_start(v_raw[:, b, :], rows(v)).then_inc(v_in[b], 16)

            for b in range(G):
                sp.dma_start(u_raw[:, b, :], u[b * KEYS:(b + 1) * KEYS, :]).then_inc(u_in[b], 16)
            for half in range(2):
                sp.dma_start(hT[half][:, :, :].bitcast(F32), hT_spill[half]).then_inc(hT_in, 16)
            for b in range(G):
                sp.dma_start(gate[:, b, :], gates[b]).then_inc(gate_in[b], 16)
                sp.dma_start(v_raw[:, b, :], v[b * KEYS:(b + 1) * KEYS, :]).then_inc(v_in[b], 16)
            sp.dma_start(X[:, :, :], x_spill.rearrange("(n p) d -> p n d", p=P)).then_inc(x_in, 16)
            with sp.Fori(1, GROUPS) as g:
                for b in range(G):
                    n = g * G + b
                    sp.wait_ge(u_turned, n - 1)
                    sp.dma_start(u_raw[:, b, :], u[ds(n * KEYS, KEYS), :]).then_inc(u_in[b], 16)
                    sp.wait_ge(gated, 2 * (n - 1))
                    sp.dma_start(gate[:, b, :], gates[ds(n, 1), :, :].rearrange("a j t -> (a j) t")).then_inc(gate_in[b], 16)
                    sp.wait_ge(v_lo_ready, n - 1)
                    sp.dma_start(v_raw[:, b, :], v[ds(n * KEYS, KEYS), :]).then_inc(v_in[b], 16)
            for tt in range(NT):
                sp.wait_ge(added, OUT_BANKS + UNITS * (GROUPS - 1) + 2 * tt + 2)
                sp.dma_start(out[tt * P:(tt + 1) * P, :], X[:, tt, :]).then_inc(stored, 16)
            sp.wait_ge(stored, 16 * NT)

        @block.tensor
        def _(pe):
            def turn(n, g, b):
                pe.wait_ge(u_in[b], 16 * (g + 1))
                pe.wait_ge(uT_lo_ready, n + 1)
                for k in range(KD):
                    ins = pe.transpose(uT_ps[:, k, :], u_raw[:, b, k * P:(k + 1) * P], ident[:, :])
                ins.then_inc(u_turned, 1)

            def hidden_products(n, b):
                pe.wait_ge(uT_lo_ready, n + 2)
                for half in range(2):
                    pe.wait_ge(gelu_done, 2 * n + half + 1)
                    t = slice(half * HALF, (half + 1) * HALF)
                    for k in range(KD):
                        ins = product3(pe, ps[:, 2 + half, :], (uT_hi[:, b, k, :], uT_lo[:, b, k, :]),
                                       (hT[0][:, k, t], hT[1][:, k, t]), k == 0, k == KD - 1)
                    ins.then_inc(hidden_done, 1)

            def output_part(g, unit, b):
                tt, d = unit // 2, slice((unit % 2) * HALF, (unit % 2 + 1) * HALF)
                return product3(pe, ps[:, 4 + unit % OUT_BANKS, :],
                                (act_hi[:, b, tt * P:(tt + 1) * P], act_lo[:, b, tt * P:(tt + 1) * P]),
                                (v_hi[:, b, d], v_lo[:, b, d]), b == 0, b == G - 1)

            def outputs(g):
                pe.wait_ge(v_lo_ready, g * G + 1)
                pe.wait_ge(act_lo_ready, 2 * (g * G) + 2 + 2)
                for unit in range(OUT_BANKS):
                    pe.wait_ge(added, UNITS * g + unit + 1)
                    output_part(g, unit, 0)
                pe.wait_ge(v_lo_ready, g * G + 2)
                for unit in range(UNITS):
                    if unit % 8 == 0:
                        pe.wait_ge(act_lo_ready, 2 * (g * G + 1) + unit // 8 + 1 + 2)
                    if unit >= OUT_BANKS:
                        pe.wait_ge(added, UNITS * g + unit + 1)
                        output_part(g, unit, 0)
                    output_part(g, unit, 1).then_inc(unit_done, 1)

            def group(g, last):
                turn(g * G + 1, g, 1)
                hidden_products(g * G, 0)
                if not last:
                    turn(g * G + 2, g + 1, 0)
                hidden_products(g * G + 1, 1)
                outputs(g)

            pe.sem_inc(uT_lo_ready, 1)
            pe.sem_inc(gelu_done, 2)
            pe.sem_inc(added, OUT_BANKS)
            pe.sem_inc(unit_done, UNITS)
            turn(0, 0, 0)
            pe.wait_ge(hT_in, 32)
            with pe.Fori(0, GROUPS - 1) as g:
                group(g, False)
            group(GROUPS - 1, True)

        @block.scalar
        def _(act):
            copy = lambda o, i: act.activation(o, i, ACT.Copy)

            def u_hi(n, b):
                act.wait_ge(u_turned, n + 1)
                copy(uT_hi[:, b, :, :], uT_ps).then_inc(uT_hi_ready, 1)

            def tile(g, b):
                n = g * G + b
                act.wait_ge(v_in[b], 16 * (g + 1))
                act.wait_ge(unit_done, UNITS * (g + 1))
                copy(v_hi[:, b, :], v_raw[:, b, :]).then_inc(v_hi_ready, 1)
                for half in range(2):
                    t = slice(half * HALF, (half + 1) * HALF)
                    act.wait_ge(hidden_done, 2 * n + half + 1)
                    act.wait_ge(act_lo_ready, 2 * n + half + 1)
                    act.activation(hidden[:, half, :], ps[:, 2 + half, :], ACT.Gelu).then_inc(gelu_done, 1)
                    act.wait_ge(gated, 2 * n + half + 1)
                    copy(act_hi[:, b, t], hidden[:, half, :]).then_inc(act_hi_ready, 1)

            u_hi(0, 0)
            with act.Fori(0, GROUPS - 1) as g:
                u_hi(g * G + 1, 1)
                tile(g, 0)
                u_hi(g * G + 2, 0)
                tile(g, 1)
            u_hi(KEYS - 1, 1)
            tile(GROUPS - 1, 0)
            tile(GROUPS - 1, 1)

        @block.vector
        def _(dve):
            def u_lo(n, b):
                dve.wait_ge(uT_hi_ready, n + 1)
                dve.tensor_tensor(uT_lo[:, b, :, :], uT_ps, uT_hi[:, b, :, :].bitcast(F32), ALU.subtract).then_inc(uT_lo_ready, 1)

            def tile(g, b):
                n = g * G + b
                dve.wait_ge(v_hi_ready, n + 1)
                dve.tensor_tensor(v_lo[:, b, :], v_raw[:, b, :], v_hi[:, b, :].bitcast(F32), ALU.subtract).then_inc(v_lo_ready, 1)
                for half in range(2):
                    t = slice(half * HALF, (half + 1) * HALF)
                    if half == 0:
                        dve.wait_ge(gate_in[b], 16 * (g + 1))
                    dve.wait_ge(gelu_done, 2 * n + half + 1 + 2)
                    dve.tensor_tensor(hidden[:, half, :], hidden[:, half, :], gate[:, b, t], ALU.mult).then_inc(gated, 1)
                    dve.wait_ge(act_hi_ready, 2 * n + half + 1)
                    dve.tensor_tensor(act_lo[:, b, t], hidden[:, half, :], act_hi[:, b, t].bitcast(F32),
                                      ALU.subtract).then_inc(act_lo_ready, 1)

            def add_outputs(g):
                for unit in range(UNITS):
                    dve.wait_ge(unit_done, UNITS * (g + 1) + unit + 1)
                    x = X[:, unit // 2, (unit % 2) * HALF:(unit % 2 + 1) * HALF]
                    dve.tensor_tensor(x, ps[:, 4 + unit % OUT_BANKS, :], x, ALU.add).then_inc(added, 1)

            dve.sem_inc(act_lo_ready, 2)
            u_lo(0, 0)
            dve.wait_ge(x_in, 16)
            with dve.Fori(0, GROUPS - 1) as g:
                u_lo(g * G + 1, 1)
                tile(g, 0)
                u_lo(g * G + 2, 0)
                tile(g, 1)
                add_outputs(g)
            u_lo(KEYS - 1, 1)
            tile(GROUPS - 1, 0)
            tile(GROUPS - 1, 1)
            add_outputs(GROUPS - 1)


def hybrid_block(nc, x, w_in, pool_w, w_out, w_query, sub_keys, u, v, attn_g, q_g, k_g, pool_scale, ffn_g,
                 ident_d, cos_d, sin_d, mask_d, inv_count_d, iota_d, out):
    x_spill = nc.dram_tensor("x_spill", (T, D), F32).ap()
    hT_spill = nc.dram_tensor("hT_spill", (2, P, KD, T), F32).ap()
    gates = nc.dram_tensor("gates", (KEYS, KEYS, T), F32).ap()
    with ExitStack() as whole:
        sb = lambda ctx, n, s, dt=F32: ctx.enter_context(nc.sbuf_tensor(n, s, dt))
        ident = sb(whole, "ident", [P, P])
        X = sb(whole, "X", [P, NT, D])
        with ExitStack() as mixing:
            QKV = sb(mixing, "QKV", [P, NT, 3 * DA])
            poolT = sb(mixing, "poolT", [P, NG, PAD + T])
            O = sb(mixing, "O", [P, NT, DA])
            with ExitStack() as ctx:
                hT = [sb(ctx, f"hT1_{n}", [P, KD, T], F32R) for n in ("hi", "lo")]
                scratch = O[:, :, :].rearrange("p n d -> p (n d)")
                norm_and_transpose(nc, "n1", X, x, attn_g, scratch, *hT, ident, ident_d, None)
                project_inputs(nc, w_in, *hT, QKV, poolT)
            with ExitStack() as ctx:
                QT = sb(ctx, "QT", [P, 8, T])
                inv_count = sb(ctx, "inv_count", [P, NG, PAD])
                with ExitStack() as inner:
                    cos, sin = sb(inner, "cos", [P, NT, HD // 2]), sb(inner, "sin", [P, NT, HD // 2])
                    gains = sb(inner, "gains", [P, 2, HD])
                    consts = [(cos[:, :, :], cos_d.rearrange("(n p) d -> p n d", p=P)),
                              (sin[:, :, :], sin_d.rearrange("(n p) d -> p n d", p=P)),
                              (gains[:, 0, :], q_g.partition_broadcast(P)), (gains[:, 1, :], k_g.partition_broadcast(P)),
                              (inv_count[:, :, :], inv_count_d)]
                    prepare_heads(nc, QKV, QT, cos, sin, gains, ident, consts)
                pooled = attend(nc, QKV, QT, O, poolT, inv_count, mask_d, ident)
            with ExitStack() as ctx:
                mixT = [sb(ctx, f"mixT_{n}", [P, KD, T], F32R) for n in ("hi", "lo")]
                mix(nc, O, pooled, pool_w, pool_scale, *mixT, ident)
                project_output(nc, w_out, *mixT, X)
        picks = sb(whole, "picks", [P, NT, 3, KEYS])
        iota = sb(whole, "iota", [P, KEYS])
        with ExitStack() as ctx:
            hT = [sb(ctx, f"hT2_{n}", [P, KD, T], F32R) for n in ("hi", "lo")]
            with ExitStack() as inner:
                scratch = sb(inner, "scratch", [P, 4 * D])
                norm_and_transpose(nc, "n2", X, None, ffn_g, scratch[:, :], *hT, ident, None, x_spill, (iota[:, :], iota_d))
            scores = X[:, :, :].rearrange("p n d -> p (n d)").rearrange("p (b t g n) -> p b t g n", b=2, t=NT, g=4)
            retrieve(nc, w_query, sub_keys, *hT, hT_spill, scores, picks, iota, ident)
        spread_gates(nc, picks, iota, ident, gates)
        mix_experts(nc, u, v, gates, hT_spill, x_spill, X, ident, out)


def constants():
    freqs = np.float32(10000.0) ** (-np.arange(0, HD, 2, dtype=np.float32) / np.float32(HD))
    angle = np.arange(T, dtype=np.float32)[:, None] * freqs[None, :].astype(np.float32)
    back = np.arange(P)[:, None] - np.arange(T)[None, :] + (T - P)
    count = sum(((back >= 0) & (back <= window) & (back % dil == 0)).astype(np.int64)
                for window, dil in ((128, 1), (512, 4), (2048, 16)))
    mask = np.where(count > 0, np.log(np.maximum(count, 1)), NEG).astype(np.float32)
    t = np.arange(PAD)
    inv = np.stack([1.0 / np.minimum(t + 1, w) for w in WINDOWS]).astype(np.float32)
    return {
        "ident": np.eye(P, dtype=np.float32), "cos": np.cos(angle), "sin": np.sin(angle), "mask": mask,
        "inv_count": np.ascontiguousarray(np.broadcast_to(inv, (P, NG, PAD))),
        "iota": np.ascontiguousarray(np.broadcast_to(np.arange(KEYS, dtype=np.float32), (P, KEYS))),
    }


def kernel(**inputs):
    import concourse.bacc as bacc
    from concourse.bass_utils import run_bass_kernel_spmd

    shapes = {
        "x": (T, D), "w_in": (D, 3 * DA + NG * P), "pool_w": (NG, P, P), "w_out": (D, D),
        "peer_w_query": (D, PH * 2 * P), "peer_sub_keys": (PH * 2 * KEYS, P),
        "peer_u": (KEYS * KEYS, D), "peer_v": (KEYS * KEYS, D),
        "attn_norm_g": (D,), "q_norm_g": (HD,), "k_norm_g": (HD,), "pool_scale": (NG * P,), "ffn_norm_g": (D,),
    }
    nc = bacc.Bacc("TRN2", target_bir_lowering=False, num_devices=1)
    arrays = {f"in_{n}": np.ascontiguousarray(inputs[n]).reshape(s) for n, s in shapes.items()}
    arrays["in_pool_scale"] = np.ascontiguousarray(arrays["in_pool_scale"].reshape(NG, P).T)
    arrays |= {f"const_{n}": a for n, a in constants().items()}
    args = [nc.dram_tensor(n, a.shape, mybir.dt.from_np(a.dtype), kind="ExternalInput").ap() for n, a in arrays.items()]
    out = nc.dram_tensor("out", (T, D), F32, kind="ExternalOutput").ap()
    hybrid_block(nc, *args, out)
    r = run_bass_kernel_spmd(nc, [arrays], core_ids=[0])
    return r.results[0]["out"].reshape(1, T, D)
```

```python
from contextlib import ExitStack

import numpy as np
import concourse.bass as bass
from concourse import mybir

F32 = mybir.dt.float32
F32R = mybir.dt.float32r
U32 = mybir.dt.uint32
ALU = mybir.AluOpType
ACT = mybir.ActivationFunctionType
AX = mybir.AxisListType
ds = bass.ds

P = 128
T = 1024
NT = T // P
D = 1024
KD = D // P
HALF = 512
HEADS = 8
HD = 64
DA = HEADS * HD
WINDOWS = (2, 4, 8, 16)
NG = len(WINDOWS)
PAD = max(WINDOWS)
EPS = 1e-6
KEYS = 128
PH = 8
TOPK = 16
NEG = -1e30
LOWEST = -3.0e38
RING = 4


def hold(eng, sem, value, passed):
    eng.wait_ge(sem, value)
    eng.sem_inc(passed, 1)


def banks(nc, ctx, name):
    return ctx.enter_context(nc.psum_tensor(name, [P, 8, HALF], F32))


def norm_and_transpose(nc, name, X, x_dram, gain_row, scratch, hT_hi, hT_lo, ident, ident_dram, spill, extra=None):
    with ExitStack() as ctx:
        sem = lambda n: nc.alloc_semaphore(f"{name}_{n}")
        ps = banks(nc, ctx, f"{name}_ps")
        stats = ctx.enter_context(nc.sbuf_tensor(f"{name}_stats", [P, 4, NT], F32))
        ssq, mean, root, rstd = (stats[:, i, :] for i in range(4))
        hn, gain, junk = scratch[:, 0:2048], scratch[:, 2048:3072], scratch[:, 3072:4096]
        x_in = [sem(f"x_in{i}") for i in range(NT)]
        consts_in, spilled, extra_in = sem("consts_in"), sem("spilled"), sem("extra_in")
        squares, mean_ready, root_ready, rstd_ready = sem("squares"), sem("mean"), sem("root"), sem("rstd")
        hn_ready, turned, hi_ready, lo_ready = sem("hn"), sem("turned"), sem("hi"), sem("lo")
        block = ctx.enter_context(nc.Block())

        @block.sync
        def _(sp):
            if x_dram is not None:
                for tt in range(NT):
                    sp.dma_start(X[:, tt, :], x_dram[tt * P:(tt + 1) * P, :]).then_inc(x_in[tt], 16)
                sp.dma_start(ident[:, :], ident_dram).then_inc(consts_in, 16)
            sp.dma_start(gain, gain_row.partition_broadcast(P)).then_inc(consts_in, 16)
            if extra is not None:
                sp.dma_start(*extra).then_inc(extra_in, 16)
                sp.wait_ge(extra_in, 16)
            if spill is not None:
                sp.dma_start(spill.rearrange("(n p) d -> p n d", p=P), X[:, :, :]).then_inc(spilled, 16)
                sp.wait_ge(spilled, 16)

        @block.scalar
        def _(act):
            for tt in range(NT):
                if x_dram is not None:
                    act.wait_ge(x_in[tt], 16)
                if tt:
                    act.wait_ge(squares, tt)
                act.activation(junk, X[:, tt, :], ACT.Square, accum_out=ssq[:, tt:tt + 1]).then_inc(squares, 1)
            act.wait_ge(mean_ready, 1)
            act.activation(root, mean, ACT.Sqrt).then_inc(root_ready, 1)
            for tt in range(NT):
                act.wait_ge(turned, tt + 1)
                act.activation(hT_hi[:, :, tt * P:(tt + 1) * P],
                               ps[:, 2 * (tt % 2):2 * (tt % 2) + 2, :].rearrange("p b (k t) -> p (b k) t", t=P),
                               ACT.Copy).then_inc(hi_ready, 1)

        @block.vector
        def _(dve):
            dve.wait_ge(squares, NT)
            dve.tensor_scalar(mean, ssq, 1.0 / D, EPS, ALU.mult, ALU.add).then_inc(mean_ready, 1)
            dve.wait_ge(root_ready, 1)
            dve.reciprocal(rstd, root).then_inc(rstd_ready, 1)
            dve.wait_ge(rstd_ready, 1)
            dve.wait_ge(consts_in, 32 if x_dram is not None else 16)

            def scale_tile(tt):
                if tt >= 2:
                    dve.wait_ge(turned, tt - 1)
                dve.scalar_tensor_tensor(out=hn[:, (tt % 2) * D:(tt % 2 + 1) * D], in0=X[:, tt, :],
                                         scalar=rstd[:, tt:tt + 1], in1=gain, op0=ALU.mult,
                                         op1=ALU.mult).then_inc(hn_ready, 1)

            scale_tile(0)
            for tt in range(NT):
                if tt + 1 < NT:
                    scale_tile(tt + 1)
                dve.wait_ge(hi_ready, tt + 1)
                dve.tensor_tensor(hT_lo[:, :, tt * P:(tt + 1) * P],
                                  ps[:, 2 * (tt % 2):2 * (tt % 2) + 2, :].rearrange("p b (k t) -> p (b k) t", t=P),
                                  hT_hi[:, :, tt * P:(tt + 1) * P].bitcast(F32), ALU.subtract).then_inc(lo_ready, 1)

        @block.tensor
        def _(pe):
            pe.wait_ge(consts_in, 32 if x_dram is not None else 16)
            for tt in range(NT):
                pe.wait_ge(hn_ready, tt + 1)
                if tt >= 2:
                    pe.wait_ge(lo_ready, tt - 1)
                for k in range(KD):
                    ins = pe.transpose(ps[:, 2 * (tt % 2) + k // 4, (k % 4) * P:(k % 4 + 1) * P],
                                       hn[:, (tt % 2) * D + k * P:(tt % 2) * D + (k + 1) * P], ident[:, :])
                ins.then_inc(turned, 1)


class Weights:

    def __init__(self, nc, ctx, name):
        sem = lambda n: nc.alloc_semaphore(f"{name}_{n}")
        self.raw = ctx.enter_context(nc.sbuf_tensor(f"{name}_raw", [P, RING, HALF], F32))
        self.hi = ctx.enter_context(nc.sbuf_tensor(f"{name}_hi", [P, RING, HALF], F32R))
        self.lo = ctx.enter_context(nc.sbuf_tensor(f"{name}_lo", [P, RING, HALF], F32R))
        self.landed = [sem(f"landed{i}") for i in range(RING)]
        self.hi_ready, self.lo_ready, self.used = sem("hi_ready"), sem("lo_ready"), sem("used")


def product3(pe, out, left, right, first, last):
    (lh, ll), (rh, rl) = left, right
    pe.matmul(out, lh, rh, start=first, stop=False)
    pe.matmul(out, lh, rl, start=False, stop=False)
    return pe.matmul(out, ll, rh, start=False, stop=last)


def load_weights(eng, W, source, chunks):
    with eng.Fori(0, chunks) as c:
        for k in range(KD):
            eng.wait_ge(W.lo_ready, c * KD + k + 1)
            eng.dma_start(W.raw[:, k % RING, :], source[k * P:(k + 1) * P, ds(c * HALF, HALF)]).then_inc(
                W.landed[k % RING], 16)


HEAD = range(RING - 1)
REST = range(RING - 1, KD)


def split_hi(act, W, c, slices=range(KD)):
    for k in slices:
        act.wait_ge(W.landed[k % RING], 16 * (2 * c + k // RING + 1))
        act.wait_ge(W.used, c * KD + k + 1)
        act.activation(W.hi[:, k % RING, :], W.raw[:, k % RING, :], ACT.Copy).then_inc(W.hi_ready, 1)


def split_lo(eng, W, c, slices=range(KD)):
    for k in slices:
        eng.wait_ge(W.hi_ready, c * KD + k + 1)
        eng.tensor_tensor(W.lo[:, k % RING, :], W.raw[:, k % RING, :],
                          W.hi[:, k % RING, :].bitcast(F32), ALU.subtract).then_inc(W.lo_ready, 1)


def wait_bank(eng, W, bank_done, c, b):
    if b < 7:
        eng.wait_ge(bank_done, c * 7 + b + 1)
    else:
        eng.wait_ge(W.used, RING + (c + 1) * KD)


def weight_chunk(pe, W, ps, c, free, bank_done, operands):
    for k in range(KD):
        pe.wait_ge(W.lo_ready, RING + c * KD + k + 1)
        for b in range(8):
            if k == 0:
                free(b)
            left, right = operands(k, b)
            ins = product3(pe, ps[:, b, :], left, right, k == 0, k == KD - 1)
            if k == KD - 1 and b < 7:
                ins.then_inc(bank_done, 1)
        ins.then_inc(W.used, 1)


def token_operands(W, hT_hi, hT_lo):
    return lambda k, b: ((hT_hi[:, k, b * P:(b + 1) * P], hT_lo[:, k, b * P:(b + 1) * P]),
                         (W.hi[:, k % RING, :], W.lo[:, k % RING, :]))


def channel_operands(W, hT_hi, hT_lo):
    def at(k, b):
        n, t = (b % 4) * P, (b // 4) * HALF
        return ((W.hi[:, k % RING, n:n + P], W.lo[:, k % RING, n:n + P]),
                (hT_hi[:, k, t:t + HALF], hT_lo[:, k, t:t + HALF]))
    return at


def project_inputs(nc, w_in, hT_hi, hT_lo, QKV, poolT):
    with ExitStack() as ctx:
        sem = lambda n: nc.alloc_semaphore(f"pi_{n}")
        ps = banks(nc, ctx, "pi_ps")
        W = Weights(nc, ctx, "pi_w")
        bank_done, even_free, odd_free, zeroed = sem("bank_done"), sem("even_free"), sem("odd_free"), sem("zeroed")
        block = ctx.enter_context(nc.Block())

        def channel_slot(b):
            return poolT[:, b % 4, PAD + (b // 4) * HALF:PAD + (b // 4 + 1) * HALF]

        @block.sync
        def _(sp):
            load_weights(sp, W, w_in, 4)

        @block.scalar
        def _(act):
            split_hi(act, W, 0, HEAD)
            with act.Fori(0, 3) as c:
                split_hi(act, W, c, REST)
                split_hi(act, W, c + 1, HEAD)
                for b in range(0, 8, 2):
                    wait_bank(act, W, bank_done, c, b)
                    act.activation(QKV[:, b, ds(c * HALF, HALF)], ps[:, b, :], ACT.Copy).then_inc(even_free, 1)
            split_hi(act, W, 3, REST)
            for b in range(0, 8, 2):
                wait_bank(act, W, bank_done, 3, b)
                act.activation(channel_slot(b), ps[:, b, :], ACT.Copy).then_inc(even_free, 1)

        @block.vector
        def _(dve):
            dve.sem_inc(W.lo_ready, RING)
            dve.memset(poolT[:, :, 0:PAD], 0.0).then_inc(zeroed, 1)
            split_lo(dve, W, 0, HEAD)
            with dve.Fori(0, 3) as c:
                split_lo(dve, W, c, REST)
                split_lo(dve, W, c + 1, HEAD)
                for b in range(1, 8, 2):
                    wait_bank(dve, W, bank_done, c, b)
                    dve.tensor_copy(QKV[:, b, ds(c * HALF, HALF)], ps[:, b, :]).then_inc(odd_free, 1)
            split_lo(dve, W, 3, REST)
            for b in range(1, 8, 2):
                wait_bank(dve, W, bank_done, 3, b)
                dve.tensor_copy(channel_slot(b), ps[:, b, :]).then_inc(odd_free, 1)

        @block.tensor
        def _(pe):
            pe.sem_inc(W.used, RING)
            pe.sem_inc(even_free, 4)
            pe.sem_inc(odd_free, 4)

            def free(c):
                return lambda b: pe.wait_ge((even_free, odd_free)[b % 2], c * 4 + b // 2 + 1)

            with pe.Fori(0, 3) as c:
                weight_chunk(pe, W, ps, c, free(c), bank_done, token_operands(W, hT_hi, hT_lo))
            weight_chunk(pe, W, ps, 3, free(3), bank_done, channel_operands(W, hT_hi, hT_lo))


def prepare_heads(nc, QKV, QT, cos, sin, gains, ident, consts):
    NH = 2 * HEADS
    with ExitStack() as ctx:
        sem = lambda n: nc.alloc_semaphore(f"ph_{n}")
        sb = lambda n, s: ctx.enter_context(nc.sbuf_tensor(f"ph_{n}", s, F32))
        ps = banks(nc, ctx, "ph_ps")
        square = sb("square", [P, 2, 2 * DA])
        stats = sb("stats", [P, 3, NT, NH])
        normed, turnc, turns = sb("normed", [P, 2 * DA]), sb("turnc", [P, 2 * DA]), sb("turns", [P, 2 * DA])
        consts_in, squared, summed = sem("consts_in"), sem("squared"), sem("summed")
        mean_ready, root_ready, rstd_ready = sem("mean"), sem("root"), sem("rstd")
        normed_ready, gained, cos_ready = sem("normed_r"), sem("gained"), sem("cos")
        sin_ready, rotated, turned, QT_ready = sem("sin"), sem("rotated"), sem("turned"), sem("QT")
        block = ctx.enter_context(nc.Block())
        heads = lambda ap: ap.rearrange("p (h d) -> p h d", d=HD)
        halves = lambda ap: ap.rearrange("p (h s d) -> p h s d", s=2, d=HD // 2)

        @block.sync
        def _(sp):
            for to, source in consts:
                sp.dma_start(to, source).then_inc(consts_in, 16)

        @block.scalar
        def _(act):
            for tt in range(NT):
                if tt >= 2:
                    act.wait_ge(summed, tt - 1)
                act.activation(square[:, tt % 2, :], QKV[:, tt, 0:2 * DA], ACT.Square).then_inc(squared, 1)
            act.wait_ge(mean_ready, 1)
            act.activation(stats[:, 1], stats[:, 0], ACT.Sqrt).then_inc(root_ready, 1)
            with act.Fori(0, NT) as tt:
                act.wait_ge(turned, tt + 2)
                act.activation(QT[:, 0:4, ds(tt * P, P)], ps[:, 0, :].rearrange("p (a t) -> p a t", t=P),
                               ACT.Copy, scale=HD ** -0.5).then_inc(QT_ready, 1)
                act.activation(QT[:, 4:8, ds(tt * P, P)], ps[:, 1, :].rearrange("p (a t) -> p a t", t=P),
                               ACT.Copy).then_inc(QT_ready, 1)

        @block.gpsimd
        def _(pool):
            pool.wait_ge(consts_in, 16 * len(consts))
            with pool.Fori(0, NT) as tt:
                pool.wait_ge(gained, tt + 1)
                pool.wait_ge(rotated, tt + 1)
                s = sin[:, ds(tt, 1), :].broadcast_to([P, NH, HD // 2])
                x, o = halves(normed[:, :]), halves(turns[:, :])
                pool.tensor_tensor(o[:, :, 0, :], x[:, :, 1, :], s, ALU.mult).then_inc(sin_ready, 1)
                pool.tensor_tensor(o[:, :, 1, :], x[:, :, 0, :], s, ALU.mult).then_inc(sin_ready, 1)

        @block.vector
        def _(dve):
            for tt in range(NT):
                dve.wait_ge(squared, tt + 1)
                dve.tensor_reduce(stats[:, 2, tt, :], heads(square[:, tt % 2, :]), AX.X, ALU.add).then_inc(summed, 1)
            dve.wait_ge(summed, NT)
            dve.tensor_scalar(stats[:, 0], stats[:, 2], 1.0 / HD, EPS, ALU.mult, ALU.add).then_inc(mean_ready, 1)
            dve.wait_ge(root_ready, 1)
            dve.reciprocal(stats[:, 2], stats[:, 1]).then_inc(rstd_ready, 1)
            dve.wait_ge(rstd_ready, 1)
            dve.wait_ge(consts_in, 16 * len(consts))
            dve.sem_inc(rotated, 1)
            with dve.Fori(0, NT) as tt:
                dve.wait_ge(rotated, tt + 1)
                dve.tensor_tensor(heads(turnc[:, :]), heads(QKV[:, ds(tt, 1), 0:2 * DA].rearrange("p a n -> p (a n)")),
                                  stats[:, 2, ds(tt, 1), :].rearrange("p a h -> p h a").broadcast_to([P, NH, HD]),
                                  ALU.mult).then_inc(normed_ready, 1)
                dve.wait_ge(normed_ready, tt + 1)
                dve.tensor_tensor(normed[:, :].rearrange("p (a h d) -> p a h d", a=2, d=HD),
                                  turnc[:, :].rearrange("p (a h d) -> p a h d", a=2, d=HD),
                                  gains[:, :, :].unsqueeze(2).broadcast_to([P, 2, HEADS, HD]),
                                  ALU.mult).then_inc(gained, 1)
                dve.wait_ge(gained, tt + 1)
                dve.tensor_tensor(turnc[:, :].rearrange("p (h d) -> p h d", d=HD // 2),
                                  normed[:, :].rearrange("p (h d) -> p h d", d=HD // 2),
                                  cos[:, ds(tt, 1), :].broadcast_to([P, 2 * NH, HD // 2]), ALU.mult).then_inc(cos_ready, 1)
                dve.wait_ge(cos_ready, tt + 1)
                dve.wait_ge(sin_ready, 2 * tt + 2)
                dve.wait_ge(turned, tt + 1)
                out, c, s = halves(square[:, 0, :]), halves(turnc[:, :]), halves(turns[:, :])
                dve.tensor_tensor(out[:, :, 0, :], c[:, :, 0, :], s[:, :, 0, :], ALU.subtract)
                dve.tensor_tensor(out[:, :, 1, :], c[:, :, 1, :], s[:, :, 1, :], ALU.add).then_inc(rotated, 1)

        @block.tensor
        def _(pe):
            pe.sem_inc(turned, 1)
            pe.sem_inc(QT_ready, 2)
            with pe.Fori(0, NT) as tt:
                pe.wait_ge(rotated, tt + 2)
                pe.wait_ge(QT_ready, 2 * tt + 2)
                for pair in range(8):
                    ins = pe.transpose(ps[:, pair // 4, (pair % 4) * P:(pair % 4 + 1) * P],
                                       square[:, 0, pair * P:(pair + 1) * P], ident[:, :])
                ins.then_inc(turned, 1)


def attend(nc, QKV, QT, OT, inv_sum, poolT, inv_count, mask_dram, ident):
    stage = [QKV[:, 0:2, 0:T], QKV[:, 2:4, 0:T]]
    pooled = QKV[:, 4:8, 0:T]
    UNITS = 2 * NT
    tile = lambda u: (NT - 1 - u % NT // 2, u % NT // 2)[u % 2]
    with ExitStack() as ctx:
        sem = lambda n: nc.alloc_semaphore(f"at_{n}")
        sb = lambda n, s: ctx.enter_context(nc.sbuf_tensor(f"at_{n}", s, F32))
        ps = banks(nc, ctx, "at_ps")
        mask, masked, probs, probsT = sb("mask", [P, T]), sb("masked", [P, 2, T]), sb("probs", [P, 2, T]), sb("probsT", [P, 2, T])
        values = sb("values", [P, 2, NT, P])
        small = sb("small", [P, 3, 2])
        windows = sb("windows", [P, 2, PAD + T])
        mask_in, staged = sem("mask_in"), [sem("staged0"), sem("staged1")]
        scores_ready, masked_ready = sem("scores"), sem("masked_r")
        negmax_ready, probs_ready, turned = sem("negmax"), sem("probs_r"), sem("turned")
        left_ready, right_ready, pv_done = sem("left"), sem("right"), sem("pv")
        inv_ready, out_ready, pair_done, pool_step = sem("inv"), sem("out"), sem("pair"), sem("pool_step")
        passed = sem("passed")
        block = ctx.enter_context(nc.Block())
        scores = lambda u: ps[:, 2 * (u % 2):2 * (u % 2) + 2, :].rearrange("p b n -> p (b n)")
        psT = ps[:, 4:6, :].rearrange("p b n -> p (b n)")
        psO = lambda u: ps[:, 6 + u % 2, 0:P]
        cols = lambda u: (tile(u) + 1) * P

        def rights(u):
            return sum(cols(w) > HALF for w in range(u + 1))

        @block.sync
        def _(sp):
            sp.dma_start(mask[:, :], mask_dram).then_inc(mask_in, 16)
            with sp.Fori(0, HEADS // 4) as two:
                for s in range(2):
                    pair = 2 * two + s
                    sp.wait_ge(pair_done, pair + 1)
                    sp.dma_start(stage[s][:, 0, :], QT[:, ds(pair, 1), :].rearrange("p a t -> p (a t)")).then_inc(staged[s], 16)
                    sp.dma_start(stage[s][:, 1, :], QT[:, ds(pair + 4, 1), :].rearrange("p a t -> p (a t)")).then_inc(staged[s], 16)
                    sp.dma_start(values[:, s, :, :], QKV[:, :, ds(2 * DA + pair * P, P)]).then_inc(staged[s], 16)

        @block.tensor
        def _(pe):
            def one_pair(two, s):
                pair = 2 * two + s
                pe.wait_ge(staged[s], 48 * two + 48)
                for step in range(UNITS + 2):
                    if step < UNITS:
                        u, rows = step, slice((step // NT) * HD, (step // NT + 1) * HD)
                        if u >= 2:
                            pe.wait_ge(masked_ready, UNITS * pair + u - 1)
                        for c0 in range(0, cols(u), HALF):
                            c1 = min(c0 + HALF, cols(u))
                            ins = pe.matmul(scores(u)[:, c0:c1], stage[s][rows, 0, tile(u) * P:(tile(u) + 1) * P],
                                            stage[s][rows, 1, c0:c1], start=True, stop=True)
                        ins.then_inc(scores_ready, 1)
                    if 0 < step <= UNITS:
                        u = step - 1
                        pe.wait_ge(probs_ready, UNITS * pair + u + 1)
                        if u >= 1:
                            pe.wait_ge(left_ready, UNITS * pair + u)
                            if cols(u - 1) > HALF:
                                pe.wait_ge(right_ready, NT * pair + rights(u - 1))
                        for b in range(tile(u) + 1):
                            ins = pe.transpose(psT[:, b * P:(b + 1) * P], probs[:, u % 2, b * P:(b + 1) * P], ident[:, :])
                        ins.then_inc(turned, 1)
                    if step >= 2:
                        u = step - 2
                        pe.wait_ge(left_ready, UNITS * pair + u + 1)
                        if cols(u) > HALF:
                            pe.wait_ge(right_ready, NT * pair + rights(u))
                        if u >= 2:
                            pe.wait_ge(out_ready, UNITS * pair + u - 1)
                        n = tile(u) + 1
                        for b in range(n):
                            ins = pe.matmul(psO(u), values[:, s, b, :], probsT[:, u % 2, b * P:(b + 1) * P],
                                            start=b == 0, stop=b == n - 1)
                        ins.then_inc(pv_done, 1)
                pe.wait_ge(pv_done, UNITS * (pair + 1))
                pe.sem_inc(pair_done, 1)

            pe.sem_inc(pair_done, 2)
            with pe.Fori(0, HEADS // 4) as two:
                for s in range(2):
                    one_pair(two, s)

        @block.scalar
        def _(act):
            with act.Fori(0, HEADS // 2) as pair:
                for step in range(UNITS + 1):
                    if step < UNITS:
                        u, n = step, cols(step)
                        act.wait_ge(negmax_ready, UNITS * pair + u + 1)
                        if u >= 2:
                            act.wait_ge(turned, UNITS * pair + u - 1)
                            act.wait_ge(inv_ready, UNITS * pair + u - 1)
                        act.activation(probs[:, u % 2, 0:n], masked[:, u % 2, 0:n], ACT.Exp,
                                       bias=small[:, 1, u % 2:u % 2 + 1],
                                       accum_out=small[:, 2, u % 2:u % 2 + 1]).then_inc(probs_ready, 1)
                    if step >= 1:
                        u = step - 1
                        act.wait_ge(turned, UNITS * pair + u + 1)
                        if u >= 2:
                            act.wait_ge(pv_done, UNITS * pair + u - 1)
                        n = min(cols(u), HALF)
                        act.activation(probsT[:, u % 2, 0:n], psT[:, 0:n], ACT.Copy).then_inc(left_ready, 1)

        @block.vector
        def _(dve):
            dve.wait_ge(mask_in, 16)
            with dve.Fori(0, HEADS // 2) as pair:
                for step in range(UNITS + 2):
                    if step < UNITS:
                        u, n = step, cols(step)
                        if u >= 2:
                            dve.wait_ge(probs_ready, UNITS * pair + u - 1)
                        hold(dve, scores_ready, UNITS * pair + u + 1, passed)
                        dve.tensor_tensor_reduce(masked[:, u % 2, 0:n], scores(u)[:, 0:n], mask[:, T - n:T],
                                                 1.0, LOWEST, ALU.add, ALU.max,
                                                 small[:, 0, u % 2:u % 2 + 1]).then_inc(masked_ready, 1)
                        dve.wait_ge(masked_ready, UNITS * pair + u + 1)
                        dve.tensor_scalar(small[:, 1, u % 2:u % 2 + 1], small[:, 0, u % 2:u % 2 + 1], -1.0, None,
                                          ALU.mult).then_inc(negmax_ready, 1)
                    if 0 < step <= UNITS:
                        u = step - 1
                        if cols(u) > HALF:
                            dve.wait_ge(turned, UNITS * pair + u + 1)
                            if u >= 2:
                                dve.wait_ge(pv_done, UNITS * pair + u - 1)
                            dve.tensor_copy(probsT[:, u % 2, HALF:cols(u)], psT[:, HALF:cols(u)]).then_inc(right_ready, 1)
                    if step >= 2:
                        u = step - 2
                        rows = slice((u // NT) * HD, (u // NT + 1) * HD)
                        dve.wait_ge(pv_done, UNITS * pair + u + 1)
                        dve.tensor_copy(OT[rows, ds(pair, 1), tile(u) * P:(tile(u) + 1) * P].rearrange("p a t -> p (a t)"),
                                        psO(u)[rows, :]).then_inc(out_ready, 1)
                    if 0 < step <= UNITS:
                        u = step - 1
                        dve.wait_ge(probs_ready, UNITS * pair + u + 1)
                        dve.reciprocal(inv_sum[:, tile(u), ds(2 * pair + u // NT, 1)], small[:, 2, u % 2:u % 2 + 1]).then_inc(inv_ready, 1)

        @block.gpsimd
        def _(pool):
            pool.memset(windows[:, :, 0:PAD], 0.0).then_inc(pool_step, 1)
            n = 1

            def step(ins):
                nonlocal n
                ins.then_inc(pool_step, 1)
                n += 1
                pool.wait_ge(pool_step, n)

            pool.wait_ge(pool_step, 1)
            for g, w in enumerate(WINDOWS):
                source, reach = poolT[:, g, :], 1
                while reach < w:
                    to = windows[:, reach.bit_length() % 2, :]
                    step(pool.tensor_tensor(to[:, PAD:], source[:, PAD:], source[:, PAD - reach:PAD + T - reach], ALU.add))
                    source, reach = to, 2 * reach
                step(pool.tensor_tensor(pooled[:, g, 0:PAD], source[:, PAD:2 * PAD], inv_count[:, g, :], ALU.mult))
                step(pool.tensor_scalar(pooled[:, g, PAD:T], source[:, 2 * PAD:], 1.0 / w, None, ALU.mult))
                step(pool.tensor_tensor(pooled[:, g, :], pooled[:, g, :], poolT[:, g, PAD:], ALU.subtract))
    return pooled


def mix(nc, OT, inv_sum, pooled, pool_w, pool_scale, mixT_hi, mixT_lo, ident):
    with ExitStack() as ctx:
        sem = lambda n: nc.alloc_semaphore(f"mx_{n}")
        sb = lambda n, s: ctx.enter_context(nc.sbuf_tensor(f"mx_{n}", s, F32))
        ps = banks(nc, ctx, "mx_ps")
        inv = sb("inv", [P, 2, HEADS, HD])
        inv_ready, divided = sem("inv"), sem("divided")
        w, scale, scaled = sb("w", [P, NG, P]), sb("scale", [P, NG]), sb("scaled", [P, 8, HALF])
        w_in, pooled_done, scaled_ready = sem("w_in"), sem("pooled_done"), sem("scaled")
        hi_ready, lo_ready, turned, oT_hi, oT_lo = sem("hi"), sem("lo"), sem("turned"), sem("oT_hi"), sem("oT_lo")
        block = ctx.enter_context(nc.Block())
        at = lambda m, n: m[:, NG + n // 2, (n % 2) * HALF:(n % 2 + 1) * HALF]
        att = lambda m, tt: m[:, 0:4, tt * P:(tt + 1) * P]
        turned_ps = lambda tt: ps[:, tt, :].rearrange("p (k t) -> p k t", t=P)

        @block.sync
        def _(sp):
            sp.dma_start(w[:, :, :], pool_w.rearrange("g c d -> c g d")).then_inc(w_in, 16)
            sp.dma_start(scale[:, :], pool_scale).then_inc(w_in, 16)

        @block.tensor
        def _(pe):
            pe.wait_ge(w_in, 32)
            for n in range(8):
                pe.matmul(ps[:, n, :], w[:, n // 2, :], pooled[:, n // 2, (n % 2) * HALF:(n % 2 + 1) * HALF],
                          start=True, stop=True).then_inc(pooled_done, 1)
            for tt in range(NT):
                pe.wait_ge(scaled_ready, tt + 1)
                pe.wait_ge(inv_ready, tt + 1)
                for k in range(4):
                    ins = pe.transpose(ps[:, tt, k * P:(k + 1) * P],
                                       inv[:, tt % 2, 2 * k:2 * k + 2, :].rearrange("p h d -> p (h d)"), ident[:, :])
                ins.then_inc(turned, 1)

        @block.scalar
        def _(act):
            act.wait_ge(w_in, 32)
            for n in range(8):
                act.wait_ge(pooled_done, n + 1)
                act.activation(scaled[:, n, :], ps[:, n, :], ACT.Copy, scale=scale[:, n // 2:n // 2 + 1]).then_inc(scaled_ready, 1)
                act.wait_ge(scaled_ready, n + 1)
                act.activation(at(mixT_hi, n), scaled[:, n, :], ACT.Copy).then_inc(hi_ready, 1)
            for tt in range(NT):
                act.wait_ge(divided, tt + 1)
                act.activation(att(mixT_hi, tt), att(OT, tt), ACT.Copy).then_inc(oT_hi, 1)

        @block.vector
        def _(dve):
            for n in range(8):
                dve.wait_ge(hi_ready, n + 1)
                dve.tensor_tensor(at(mixT_lo, n), scaled[:, n, :], at(mixT_hi, n).bitcast(F32), ALU.subtract).then_inc(lo_ready, 1)
            def divide(tt):
                dve.wait_ge(turned, tt + 1)
                dve.tensor_tensor(att(OT, tt), att(OT, tt), turned_ps(tt), ALU.mult).then_inc(divided, 1)

            divide(0)
            for tt in range(NT):
                if tt + 1 < NT:
                    divide(tt + 1)
                dve.wait_ge(oT_hi, tt + 1)
                dve.tensor_tensor(att(mixT_lo, tt), att(OT, tt), att(mixT_hi, tt).bitcast(F32), ALU.subtract).then_inc(oT_lo, 1)

        @block.gpsimd
        def _(pool):
            for tt in range(NT):
                if tt >= 2:
                    pool.wait_ge(turned, tt - 1)
                pool.tensor_copy(inv[:, tt % 2, :, :], inv_sum[:, tt, :].unsqueeze(2).broadcast_to([P, HEADS, HD])).then_inc(inv_ready, 1)


def project_output(nc, w_out, mixT_hi, mixT_lo, X):
    with ExitStack() as ctx:
        sem = lambda n: nc.alloc_semaphore(f"po_{n}")
        ps = banks(nc, ctx, "po_ps")
        W = Weights(nc, ctx, "po_w")
        bank_done, added = sem("bank_done"), sem("added")
        block = ctx.enter_context(nc.Block())
        chunks = D // HALF

        @block.sync
        def _(sp):
            load_weights(sp, W, w_out, chunks)

        @block.scalar
        def _(act):
            with act.Fori(0, chunks) as c:
                split_hi(act, W, c)

        @block.vector
        def _(dve):
            dve.sem_inc(W.lo_ready, RING)

            def add_banks(c):
                for b in range(8):
                    wait_bank(dve, W, bank_done, c, b)
                    x = X[:, b, ds(c * HALF, HALF)]
                    dve.tensor_tensor(x, ps[:, b, :], x, ALU.add).then_inc(added, 1)

            split_lo(dve, W, 0, HEAD)
            with dve.Fori(0, chunks - 1) as c:
                split_lo(dve, W, c, REST)
                split_lo(dve, W, c + 1, HEAD)
                add_banks(c)
            split_lo(dve, W, chunks - 1, REST)
            add_banks(chunks - 1)

        @block.tensor
        def _(pe):
            pe.sem_inc(W.used, RING)
            pe.sem_inc(added, 8)
            with pe.Fori(0, chunks) as c:
                weight_chunk(pe, W, ps, c, lambda b: pe.wait_ge(added, 8 * c + b + 1), bank_done,
                             token_operands(W, mixT_hi, mixT_lo))


class EarlyTiles:

    def __init__(self, nc, ctx, name, u, hidden_dram, first, hT, ps, ident, u_raw, uT_f, uT_hi, uT_lo, hidden):
        sem = lambda n: nc.alloc_semaphore(f"{name}_{n}")
        self.u, self.hidden_dram, self.first, self.hT, self.ps, self.ident = u, hidden_dram, first, hT, ps, ident
        self.u_raw, self.uT_f, self.uT_hi, self.uT_lo, self.hidden = u_raw, uT_f, uT_hi, uT_lo, hidden
        self.u_in, self.stored = [sem("u_in0"), sem("u_in1")], [sem("stored0"), sem("stored1")]
        self.turned, self.copied, self.lo_ready = sem("turned"), sem("copied"), sem("lo_ready")
        self.hidden_done, self.gelu_done = sem("hidden_done"), sem("gelu_done")
        self.uT_ps = ps[:, 0:2, :].rearrange("p b (k e) -> p (b k) e", e=P)

    def load(self, sp, pair, s, landed=None):
        m = 2 * pair + s
        sp.wait_ge(self.turned, m + 1)
        sp.dma_start(self.u_raw[:, s, :], self.u[ds((m + self.first) * KEYS, KEYS), :]).then_inc(
            landed or self.u_in[s], 16)

    def credit_tensor(self, pe):
        pe.sem_inc(self.turned, 2)
        pe.sem_inc(self.copied, 2)
        pe.sem_inc(self.gelu_done, 2)

    def credit_sync(self, sp):
        for s in range(2):
            sp.sem_inc(self.stored[s], 16)

    def turn(self, pe, pair, s):
        m = 2 * pair + s
        pe.wait_ge(self.u_in[s], 16 * (pair + 1))
        pe.wait_ge(self.copied, 2 * m + 2)
        for k in range(KD):
            ins = pe.transpose(self.uT_ps[:, k, :], self.u_raw[:, s, k * P:(k + 1) * P], self.ident[:, :])
        ins.then_inc(self.turned, 1)

    def products(self, pe, pair, s, between=None):
        m = 2 * pair + s
        pe.wait_ge(self.lo_ready, m + 1)
        for half in range(2):
            pe.wait_ge(self.gelu_done, 2 * m + half + 1)
            t = slice(half * HALF, (half + 1) * HALF)
            for k in range(KD):
                ins = product3(pe, self.ps[:, 2 + half, :], (self.uT_hi[:, s, k, :], self.uT_lo[:, s, k, :]),
                               (self.hT[0][:, k, t], self.hT[1][:, k, t]), k == 0, k == KD - 1)
                if k == KD - 1:
                    ins.then_inc(self.hidden_done, 1)
                if between is not None:
                    between(half * KD + k)

    def copy(self, act, pair, s):
        m = 2 * pair + s
        act.wait_ge(self.turned, m + 1 + 2)
        act.activation(self.uT_f[:, s, :, :], self.uT_ps, ACT.Copy).then_inc(self.copied, 1)
        act.activation(self.uT_hi[:, s, :, :], self.uT_ps, ACT.Copy).then_inc(self.copied, 1)

    def gelu(self, act, pair, s, half):
        m = 2 * pair + s
        act.wait_ge(self.hidden_done, 2 * m + half + 1)
        if half == 0:
            act.wait_ge(self.stored[s], 16 * (pair + 1))
        act.activation(self.hidden[:, s, half * HALF:(half + 1) * HALF], self.ps[:, 2 + half, :],
                       ACT.Gelu).then_inc(self.gelu_done, 1)

    def store(self, act, pair, s):
        m = 2 * pair + s
        act.wait_ge(self.gelu_done, 2 * m + 2 + 2)
        act.dma_start(self.hidden_dram[ds(m + self.first, 1), :, :].rearrange("a j t -> (a j) t"),
                      self.hidden[:, s, :]).then_inc(self.stored[s], 16)

    def split(self, pool, pair, s, piece=None):
        m = 2 * pair + s
        k = slice(0, KD) if piece is None else slice(piece * KD // 4, (piece + 1) * KD // 4)
        if not piece:
            pool.wait_ge(self.copied, 2 * m + 2 + 2)
        ins = pool.tensor_tensor(self.uT_lo[:, s, k, :], self.uT_f[:, s, k, :], self.uT_hi[:, s, k, :].bitcast(F32),
                                 ALU.subtract)
        if piece is None or piece == 3:
            ins.then_inc(self.lo_ready, 1)

    def finish(self, eng, pairs):
        for s in range(2):
            eng.wait_ge(self.stored[s], 16 * (pairs + 1))


def retrieve(nc, w_query, sub_keys, hT_hi, hT_lo, W, scores, picks, iota, ident, u, hidden_dram, early_pairs):
    HC = 2
    CHUNKS = PH // HC
    LISTS = NT * HC
    with ExitStack() as ctx:
        sem = lambda n: nc.alloc_semaphore(f"rt_{n}")
        sb = lambda n, s, dt=F32: ctx.enter_context(nc.sbuf_tensor(f"rt_{n}", s, dt))
        ps = banks(nc, ctx, "rt_ps")
        queryT, keysT = sb("queryT", [P, 2 * HC, T]), sb("keysT", [P, 2 * PH, KEYS])
        top, top_i = sb("top", [P, NT, 2 * HC, TOPK]), sb("top_i", [P, NT, 2 * HC, TOPK], U32)
        best, best_i = sb("best", [P, NT, HC, TOPK]), sb("best_i", [P, NT, HC, TOPK], U32)
        rest, cand = sb("rest", [P, 2 * HC, KEYS]), sb("cand", [P, 2, HC, TOPK * TOPK])
        rest2 = sb("rest2", [P, HC, TOPK * TOPK])
        match = sb("match", [P, LISTS // 2, TOPK, TOPK])
        ab, ab_i = sb("ab", [P, 2, NT, HC, TOPK]), sb("ab_i", [P, 2, NT, HC, TOPK], U32)
        topf, total = sb("topf", [P, NT, 2 * HC, TOPK]), sb("total", [P, 2, NT, PH])
        raw_keys = match[:, :, :, :].rearrange("p a b c -> p (a b c)").rearrange("p (n c) -> p n c", c=P)
        early = EarlyTiles(nc, ctx, "re", u, hidden_dram, 0, (hT_hi, hT_lo), ps, ident,
                           W.raw[:, :, :].rearrange("p (s a) n -> p s (a n)", s=2),
                           queryT[:, 0:2, :].rearrange("p s (k e) -> p s k e", e=P),
                           W.hi[:, :, :].rearrange("p (s a) (k e) -> p s (a k) e", s=2, e=P),
                           W.lo[:, :, :].rearrange("p (s a) (k e) -> p s (a k) e", s=2, e=P), queryT[:, 2:4, :])
        bank_done, keys_in, keys_turned, keys_ready = sem("bank_done"), sem("keys_in"), sem("keys_turned"), sem("keys")
        query_ready, scored, scores_ready = sem("query"), sem("scored"), sem("scores_r")
        scores_free, passed = sem("scores_free"), sem("passed")
        dec, shifted, exped, normed = sem("decode"), sem("shifted"), sem("exped"), sem("normed")
        block = ctx.enter_context(nc.Block())

        @block.sync
        def _(sp):
            sp.dma_start(raw_keys[:, 0:PH, :], sub_keys[0:PH * KEYS, :].rearrange("(g n) c -> n g c", n=KEYS)).then_inc(keys_in, 16)
            load_weights(sp, W, w_query, CHUNKS)
            early.credit_sync(sp)
            sp.wait_ge(W.lo_ready, RING + CHUNKS * KD)
            with sp.Fori(0, early_pairs) as pair:
                for s in range(2):
                    early.load(sp, pair, s)

        @block.tensor
        def _(pe):
            for n in range(2 * PH // 4):
                pe.wait_ge(keys_in, 16 * (n // 2 + 1))
                for g in range(4):
                    ins = pe.transpose(ps[:, n, g * P:(g + 1) * P], raw_keys[:, (n % 2) * 4 + g, :], ident[:, :])
                ins.then_inc(keys_turned, 1)
            pe.wait_ge(keys_ready, 4)
            pe.sem_inc(W.used, RING)
            pe.sem_inc(scores_ready, 8)
            with pe.Fori(0, CHUNKS) as c:
                weight_chunk(pe, W, ps, c, lambda b: pe.wait_ge(scores_ready, 8 * c + b + 1), bank_done,
                             channel_operands(W, hT_hi, hT_lo))
                for tt in range(NT):
                    pe.wait_ge(query_ready, 8 * c + max(4 * (tt // 4) + 4, tt + 1))
                    for g in range(2 * HC):
                        ins = pe.matmul(ps[:, tt, g * KEYS:(g + 1) * KEYS], queryT[:, g, tt * P:(tt + 1) * P],
                                        keysT[:, ds(c * 2 * HC + g, 1), :].rearrange("p a n -> p (a n)"),
                                        start=True, stop=True)
                    ins.then_inc(scored, 1)
            pe.wait_ge(scores_ready, 8 * (CHUNKS + 1))
            early.credit_tensor(pe)
            early.turn(pe, 0, 0)
            with pe.Fori(0, early_pairs - 1) as pair:
                early.turn(pe, pair, 1)
                early.products(pe, pair, 0)
                early.turn(pe, pair + 1, 0)
                early.products(pe, pair, 1)
            early.turn(pe, early_pairs - 1, 1)
            early.products(pe, early_pairs - 1, 0)
            early.products(pe, early_pairs - 1, 1)

        @block.scalar
        def _(act):
            for n in range(2 * PH // 4):
                act.wait_ge(keys_turned, n + 1)
                act.activation(keysT[:, 4 * n:4 * n + 4, :], ps[:, n, :].rearrange("p (g c) -> p g c", c=P),
                               ACT.Copy).then_inc(keys_ready, 1)
                if n == 1:
                    act.dma_start(raw_keys[:, 0:PH, :],
                                  sub_keys[PH * KEYS:2 * PH * KEYS, :].rearrange("(g n) c -> n g c", n=KEYS)).then_inc(keys_in, 16)

            def chunk(c, buffer, last=False):
                split_hi(act, W, c, REST)
                if not last:
                    split_hi(act, W, c + 1, HEAD)
                for b in range(8):
                    wait_bank(act, W, bank_done, c, b)
                    act.activation(queryT[:, b % 4, (b // 4) * HALF:(b // 4 + 1) * HALF], ps[:, b, :],
                                   ACT.Copy).then_inc(query_ready, 1)
                for tt in range(NT):
                    act.wait_ge(scored, 8 * c + tt + 1)
                    act.wait_ge(scores_free, 8 * c + tt + 1)
                    act.activation(scores[:, buffer, tt, :, :], ps[:, tt, :].rearrange("p (g n) -> p g n", n=KEYS),
                                   ACT.Copy).then_inc(scores_ready, 1)

            split_hi(act, W, 0, HEAD)
            with act.Fori(0, CHUNKS // 2 - 1) as cc:
                chunk(2 * cc, 0)
                chunk(2 * cc + 1, 1)
            chunk(CHUNKS - 2, 0)
            chunk(CHUNKS - 1, 1, last=True)

            def tile(pair, s):
                for half in range(2):
                    early.gelu(act, pair, s, half)
                early.store(act, pair, s)

            early.copy(act, 0, 0)
            with act.Fori(0, early_pairs - 1) as pair:
                early.copy(act, pair, 1)
                tile(pair, 0)
                early.copy(act, pair + 1, 0)
                tile(pair, 1)
            early.copy(act, early_pairs - 1, 1)
            tile(early_pairs - 1, 0)
            tile(early_pairs - 1, 1)
            early.finish(act, early_pairs)
            act.wait_ge(shifted, CHUNKS)
            act.activation(picks[:, :, 2, :], picks[:, :, 2, :], ACT.Exp).then_inc(exped, 1)

        @block.gpsimd
        def _(pool):
            pool.sem_inc(W.lo_ready, RING)
            with pool.Fori(0, CHUNKS) as c:
                split_lo(pool, W, c)
            with pool.Fori(0, early_pairs) as pair:
                for s in range(2):
                    early.split(pool, pair, s)

        @block.vector
        def _(dve):
            dve.sem_inc(scores_free, 2 * NT)

            def search_keys(c, buffer, tt):
                hold(dve, scores_ready, 8 * c + tt + 1 + 8, passed)
                s = scores[:, buffer, tt, :, :]
                for g in range(4):
                    dve.max(top[:, tt, g, 0:8], s[:, g, :])
                dve.drain()
                for g in range(4):
                    dve.match_replace(rest[:, g, :], top[:, tt, g, 0:8], s[:, g, :], LOWEST)
                for g in range(4):
                    ins = dve.max_index(top_i[:, tt, g, 0:8], top[:, tt, g, 0:8], s[:, g, :])
                ins.then_inc(scores_free, 1)
                dve.drain()
                for g in range(4):
                    dve.max(top[:, tt, g, 8:16], rest[:, g, :])
                dve.drain()
                for g in range(4):
                    dve.max_index(top_i[:, tt, g, 8:16], top[:, tt, g, 8:16], rest[:, g, :])

            def search_pairs(tt):
                sums = cand[:, tt % 2, :, :]
                for h in range(HC):
                    dve.tensor_tensor(sums[:, h, :].rearrange("p (a b) -> p a b", b=TOPK),
                                      top[:, tt, 2 * h, :].unsqueeze(2).broadcast_to([P, TOPK, TOPK]),
                                      top[:, tt, 2 * h + 1, :].unsqueeze(1).broadcast_to([P, TOPK, TOPK]), ALU.add)
                dve.drain()
                for h in range(HC):
                    dve.max(best[:, tt, h, 0:8], sums[:, h, :])
                dve.drain()
                for h in range(HC):
                    dve.match_replace(rest2[:, h, :], best[:, tt, h, 0:8], sums[:, h, :], LOWEST)
                for h in range(HC):
                    dve.max_index(best_i[:, tt, h, 0:8], best[:, tt, h, 0:8], sums[:, h, :])
                dve.drain()
                for h in range(HC):
                    dve.max(best[:, tt, h, 8:16], rest2[:, h, :])
                dve.drain()
                for h in range(HC):
                    dve.max_index(best_i[:, tt, h, 8:16], best[:, tt, h, 8:16], rest2[:, h, :])

            STEPS = 4 + 2 * (2 * 3)

            def decode(c):
                count = 0

                def step(ins):
                    nonlocal count
                    count += 1
                    ins.then_inc(dec, 1)
                    dve.wait_ge(dec, STEPS * c + count)

                dve.drain()
                dve.tensor_tensor(picks[:, :, 2, ds(c * HC * TOPK, HC * TOPK)].rearrange("p t (h r) -> p t h r", r=TOPK),
                                  best[:, :, :, :],
                                  best[:, :, :, 0:1].broadcast_to([P, NT, HC, TOPK]), ALU.subtract).then_inc(shifted, 1)
                step(dve.tensor_scalar(ab_i[:, 0], best_i[:, :, :, :], 4, None, ALU.logical_shift_right))
                step(dve.tensor_scalar(ab_i[:, 1], best_i[:, :, :, :], TOPK - 1, None, ALU.bitwise_and))
                step(dve.tensor_copy(ab[:, :, :, :, :].rearrange("p a t h r -> p (a t h r)"),
                                     ab_i[:, :, :, :, :].rearrange("p a t h r -> p (a t h r)")))
                step(dve.tensor_copy(topf[:, :, :, :], top_i[:, :, :, :]))
                for part in range(2):
                    for half in range(2):
                        tts = slice(half * NT // 2, (half + 1) * NT // 2)
                        position = ab[:, part, tts, :, :].rearrange("p t h r -> p (t h) r")
                        step(dve.tensor_tensor(match[:, :, :, :], position.unsqueeze(3).broadcast_to([P, LISTS // 2, TOPK, TOPK]),
                                               iota[:, 0:TOPK].unsqueeze(1).unsqueeze(1).broadcast_to([P, LISTS // 2, TOPK, TOPK]),
                                               ALU.is_equal))
                        lists = topf[:, tts, :, :].rearrange("p t (h q) a -> p (t h) q a", q=2)[:, :, part, :]
                        step(dve.tensor_tensor(match[:, :, :, :], match[:, :, :, :],
                                               lists.unsqueeze(2).broadcast_to([P, LISTS // 2, TOPK, TOPK]), ALU.mult))
                        out = picks[:, tts, part, ds(c * HC * TOPK, HC * TOPK)].rearrange("p t (h r) -> p t h r", r=TOPK)
                        step(dve.tensor_reduce(out, match[:, :, :, :].rearrange("p (t h) r a -> p t h r a", h=HC), AX.X, ALU.add))
                assert count == STEPS

            with dve.Fori(0, CHUNKS // 2) as cc:
                for half in range(2):
                    c = 2 * cc + half
                    for tt in range(NT):
                        search_keys(c, half, tt)
                        search_pairs(tt)
                    decode(c)
            gates = picks[:, :, 2, :].rearrange("p t (h r) -> p t h r", r=TOPK)
            dve.wait_ge(exped, 1)
            dve.tensor_reduce(total[:, 0, :, :], gates, AX.X, ALU.add).then_inc(normed, 1)
            dve.wait_ge(normed, 1)
            dve.reciprocal(total[:, 1, :, :], total[:, 0, :, :]).then_inc(normed, 1)
            dve.wait_ge(normed, 2)
            dve.tensor_tensor(gates, gates, total[:, 1, :, :].unsqueeze(3).broadcast_to([P, NT, PH, TOPK]),
                              ALU.mult).then_inc(normed, 1)


def turn_picks(nc, picks, picksT, W, ident):
    with ExitStack() as ctx:
        sem = lambda n: nc.alloc_semaphore(f"tp_{n}")
        ps = banks(nc, ctx, "tp_ps")
        turned, hi_ready, hi_copied = sem("turned"), sem("hi"), sem("hi_copied")
        block = ctx.enter_context(nc.Block())

        @block.tensor
        def _(pe):
            for n in range(6):
                for q in range(4):
                    tt = (n % 2) * 4 + q
                    ins = pe.transpose(ps[:, n, q * P:(q + 1) * P], picks[:, tt, n // 2, :], ident[:, :])
                ins.then_inc(turned, 1)

        @block.scalar
        def _(act):
            for n in range(4):
                act.wait_ge(turned, n + 1)
                act.activation(picksT[:, n // 2, (n % 2) * HALF:(n % 2 + 1) * HALF], ps[:, n, :], ACT.Copy)

        @block.vector
        def _(dve):
            for half in range(2):
                t, gate = slice(half * HALF, (half + 1) * HALF), ps[:, 4 + half, :]
                dve.wait_ge(turned, 5 + half)
                dve.tensor_copy(W.hi[:, half, :], gate).then_inc(hi_ready, 1)
                dve.wait_ge(hi_ready, half + 1)
                dve.tensor_tensor(picksT[:, 3, t], gate, W.hi[:, half, :].bitcast(F32), ALU.subtract)
                dve.tensor_copy(picksT[:, 2, t], W.hi[:, half, :].bitcast(F32)).then_inc(hi_copied, 1)


def spread_gates(nc, ctx, picksT, iota, ident, gates, W, X, hT, u, hidden_dram, first, early_pairs, last_part,
                 written, late_u_in):
    BATCH = 4
    PART = 64
    SLOTS = 4
    BATCHES = PART // BATCH
    PER_TILE = 8
    assert T // PART == early_pairs and BATCHES == 2 * PER_TILE
    sem = lambda n: nc.alloc_semaphore(f"sg_{n}")
    sb = lambda n, s, dt=F32: ctx.enter_context(nc.sbuf_tensor(f"sg_{n}", s, dt))
    ps = banks(nc, ctx, "sg_ps")
    flat = X[:, :, :].rearrange("p n d -> p (n d)")
    slots = lambda a: flat[:, a * 2 * D:(a + 1) * 2 * D].rearrange("p (s d) -> p s d", s=2)
    early = EarlyTiles(nc, ctx, "se", u, hidden_dram, first, hT, ps, ident,
                       W.raw[:, :, :].rearrange("p (s a) n -> p s (a n)", s=2),
                       slots(0).rearrange("p s (k e) -> p s k e", e=P),
                       W.hi[:, :, :].rearrange("p (s a) (k e) -> p s (a k) e", s=2, e=P),
                       W.lo[:, :, :].rearrange("p (s a) (k e) -> p s (a k) e", s=2, e=P), slots(1))
    rows = sb("rows", [P, 2, BATCH, KEYS])
    column_hot, row_hi, row_lo = (sb(n, [P, 2, BATCH, KEYS], F32R) for n in ("columns", "row_hi", "row_lo"))
    part = [sb("part", [P, KEYS, PART])[:, :, :],
            last_part[:, :, :].rearrange("p a n -> p (a n)").rearrange("p (i t) -> p i t", t=PART)]
    columns_ready, rows_ready, hi_ready, lo_ready = sem("columns_r"), sem("rows_r"), sem("hi"), sem("lo")
    spread, copied = sem("spread"), sem("copied")
    pool_passed = sem("pool_passed")
    block = ctx.enter_context(nc.Block())

    @block.tensor
    def _(pe):
        pe.sem_inc(copied, SLOTS)
        early.credit_tensor(pe)

        def batch(part_i, j):
            n = part_i * BATCHES + j
            pe.wait_ge(hi_ready, n + 1)
            pe.wait_ge(lo_ready, n + 1)
            pe.wait_ge(copied, n + 1)
            for q in range(BATCH):
                out = ps[:, 4 + j % SLOTS, q * KEYS:(q + 1) * KEYS]
                pe.matmul(out, column_hot[:, j % 2, q, :], row_hi[:, j % 2, q, :], start=True, stop=False)
                ins = pe.matmul(out, column_hot[:, j % 2, q, :], row_lo[:, j % 2, q, :], start=False, stop=True)
            ins.then_inc(spread, 1)

        def between(pair, s):
            return lambda step: step % 2 and batch(pair, s * PER_TILE + step // 2)

        early.turn(pe, 0, 0)
        with pe.Fori(0, early_pairs - 1) as pair:
            early.turn(pe, pair, 1)
            early.products(pe, pair, 0, between(pair, 0))
            early.turn(pe, pair + 1, 0)
            early.products(pe, pair, 1, between(pair, 1))
        early.turn(pe, early_pairs - 1, 1)
        early.products(pe, early_pairs - 1, 0, between(early_pairs - 1, 0))
        early.products(pe, early_pairs - 1, 1, between(early_pairs - 1, 1))

    @block.vector
    def _(dve):
        dve.sem_inc(spread, 2)
        with dve.Fori(0, early_pairs) as pair:
            for j in range(BATCHES):
                n = pair * BATCHES + j
                index = iota[:, :].unsqueeze(1).broadcast_to([P, BATCH, KEYS])
                of = lambda a: picksT[:, a, ds(n * BATCH, BATCH)].unsqueeze(2).broadcast_to([P, BATCH, KEYS])
                dve.wait_ge(spread, n + 1)
                dve.tensor_tensor(rows[:, j % 2, :, :], index, of(0), ALU.is_equal).then_inc(rows_ready, 1)
                dve.tensor_tensor(column_hot[:, j % 2, :, :], index, of(1), ALU.is_equal).then_inc(columns_ready, 1)
                dve.wait_ge(rows_ready, n + 1)
                dve.tensor_tensor(row_hi[:, j % 2, :, :], rows[:, j % 2, :, :], of(2), ALU.mult).then_inc(hi_ready, 1)

    @block.gpsimd
    def _(pool):
        early.split(pool, 0, 0)

        def row_los(pair, splits):
            for j in range(BATCHES):
                n = pair * BATCHES + j
                hold(pool, rows_ready, n + 1, pool_passed)
                pool.tensor_tensor(row_lo[:, j % 2, :, :], rows[:, j % 2, :, :],
                                   picksT[:, 3, ds(n * BATCH, BATCH)].unsqueeze(2).broadcast_to([P, BATCH, KEYS]),
                                   ALU.mult).then_inc(lo_ready, 1)
                if j in splits:
                    early.split(pool, *splits[j])

        second = lambda pair: {1 + i: (pair, 1, i) for i in range(4)}
        first_of = lambda pair: {PER_TILE + 1 + i: (pair, 0, i) for i in range(4)}
        with pool.Fori(0, early_pairs - 1) as pair:
            row_los(pair, second(pair) | first_of(pair + 1))
        row_los(early_pairs - 1, second(early_pairs - 1))

    @block.scalar
    def _(act):
        def copy_out(pair, b, j):
            n = pair * BATCHES + j
            act.wait_ge(spread, n + 1 + 2)
            act.activation(part[b][:, :, j * BATCH:(j + 1) * BATCH],
                           ps[:, 4 + j % SLOTS, :].rearrange("p (t i) -> p i t", i=KEYS), ACT.Copy).then_inc(copied, 1)

        def tile(pair, b, s):
            for half in range(2):
                for j in range(PER_TILE // 2):
                    copy_out(pair, b, s * PER_TILE + half * PER_TILE // 2 + j)
                early.gelu(act, pair, s, half)
            early.store(act, pair, s)

        def both(two, b, last=False):
            pair = 2 * two + b
            act.wait_ge(written[b], 16 * two + 16)
            early.copy(act, pair, 1)
            tile(pair, b, 0)
            if not last:
                early.copy(act, pair + 1, 0)
            tile(pair, b, 1)

        early.copy(act, 0, 0)
        with act.Fori(0, early_pairs // 2 - 1) as two:
            both(two, 0)
            both(two, 1)
        both(early_pairs // 2 - 1, 0)
        both(early_pairs // 2 - 1, 1, last=True)

    @block.sync
    def _(sp):
        early.credit_sync(sp)
        for b in range(2):
            sp.sem_inc(written[b], 16)

        def store_part(n, b):
            sp.wait_ge(copied, SLOTS + (n + 1) * BATCHES)
            sp.dma_start(gates[ds(n, 1), :, :, :].rearrange("q j i t -> (q j) i t"), part[b]).then_inc(written[b], 16)

        for s in range(2):
            early.load(sp, 0, s)
        with sp.Fori(0, early_pairs // 2 - 1) as two:
            for b in range(2):
                n = 2 * two + b
                for s in range(2):
                    early.load(sp, n + 1, s)
                store_part(n, b)
        for s in range(2):
            early.load(sp, early_pairs - 1, s)
        store_part(early_pairs - 2, 0)
        for s in range(2):
            early.load(sp, early_pairs, s, late_u_in[s])
        store_part(early_pairs - 1, 1)
        sp.wait_ge(written[0], 16 + 16 * (early_pairs // 2))
    return early.stored


def gates_of(gates, i):
    return gates[:, :, ds(i, 1), :].rearrange("q j i t -> j q (i t)")


def mix_late_experts(nc, u, v, gates, hT, x_spill, X, ident, first, W, part_written, u_in, hidden_stored, spread_pairs,
                     hidden_dram, ee_raw, ee_in):
    G = 2
    TILES = KEYS - first
    GROUPS = TILES // G
    UNITS = 16
    OUT_BANKS = 4
    with ExitStack() as ctx:
        sem = lambda n: nc.alloc_semaphore(f"me_{n}")
        sb = lambda n, s, dt=F32: ctx.enter_context(nc.sbuf_tensor(f"me_{n}", s, dt))
        ps = banks(nc, ctx, "me_ps")
        v_raw, gate = sb("v_raw", [P, G, D]), sb("gate", [P, G, T])
        u_raw = W.raw[:, :, :].rearrange("p (s a) n -> p s (a n)", s=2)
        uT_hi, uT_lo = (w[:, :, :].rearrange("p (s a) (k e) -> p s (a k) e", s=2, e=P) for w in (W.hi, W.lo))
        v_hi, v_lo = sb("v_hi", [P, G, D], F32R), sb("v_lo", [P, G, D], F32R)
        act_hi, act_lo = sb("act_hi", [P, G, T], F32R), sb("act_lo", [P, G, T], F32R)
        hidden = sb("hidden", [P, 2, HALF])
        x_in = sem("x_in")
        v_in, gate_in = ([sem(f"{n}{b}") for b in range(G)] for n in ("v_in", "gate_in"))
        u_turned, uT_hi_ready, uT_lo_ready = sem("u_turned"), sem("uT_hi_r"), sem("uT_lo_r")
        v_hi_ready, v_lo_ready = sem("v_hi_r"), sem("v_lo_r")
        hidden_done, gelu_done, gated = sem("hidden_done"), sem("gelu"), sem("gated")
        act_hi_ready, act_lo_ready = sem("act_hi_r"), sem("act_lo_r")
        unit_done, added = sem("unit_done"), sem("added")
        block = ctx.enter_context(nc.Block())
        uT_ps = ps[:, 0:2, :].rearrange("p b (k e) -> p (b k) e", e=P)

        @block.sync
        def _(sp):
            def load(n, b, reused):
                tile = lambda w: w[ds((n + first) * KEYS, KEYS), :]
                if reused:
                    sp.wait_ge(u_turned, n - 1)
                    sp.dma_start(u_raw[:, b, :], tile(u)).then_inc(u_in[b], 16)
                    sp.wait_ge(gated, 2 * (n - 1))
                sp.dma_start(gate[:, b, :].rearrange("j (q t) -> j q t", t=gates.shape[3]),
                             gates_of(gates, n + first)).then_inc(gate_in[b], 16)
                if reused:
                    sp.wait_ge(v_lo_ready, n - 1)
                sp.dma_start(v_raw[:, b, :], tile(v)).then_inc(v_in[b], 16)

            sp.wait_ge(part_written[1], 16 + 16 * (spread_pairs // 2))
            for b in range(G):
                load(b, b, False)
            for b in range(G):
                sp.wait_ge(hidden_stored[b], 16 * (spread_pairs + 1))
            sp.wait_ge(v_in[1], 16)
            sp.dma_start(X[:, :, :], x_spill.rearrange("(n p) d -> p n d", p=P)).then_inc(x_in, 16)
            with sp.Fori(1, GROUPS) as g:
                for b in range(G):
                    load(g * G + b, b, True)
            for b in range(G):
                load_early(sp, ee_raw, ee_in, v, gates, hidden_dram, b, b)

        @block.tensor
        def _(pe):
            def turn(n, g, b):
                pe.wait_ge(u_in[b], 16 * (g + 1))
                pe.wait_ge(uT_lo_ready, n + 1)
                for k in range(KD):
                    ins = pe.transpose(uT_ps[:, k, :], u_raw[:, b, k * P:(k + 1) * P], ident[:, :])
                ins.then_inc(u_turned, 1)

            def hidden_products(n, b):
                pe.wait_ge(uT_lo_ready, n + 2)
                for half in range(2):
                    pe.wait_ge(gelu_done, 2 * n + half + 1)
                    t = slice(half * HALF, (half + 1) * HALF)
                    for k in range(KD):
                        ins = product3(pe, ps[:, 2 + half, :], (uT_hi[:, b, k, :], uT_lo[:, b, k, :]),
                                       (hT[0][:, k, t], hT[1][:, k, t]), k == 0, k == KD - 1)
                    ins.then_inc(hidden_done, 1)

            def output_part(g, unit, b):
                tt, d = unit // 2, slice((unit % 2) * HALF, (unit % 2 + 1) * HALF)
                return product3(pe, ps[:, 4 + unit % OUT_BANKS, :],
                                (act_hi[:, b, tt * P:(tt + 1) * P], act_lo[:, b, tt * P:(tt + 1) * P]),
                                (v_hi[:, b, d], v_lo[:, b, d]), b == 0, b == G - 1)

            def outputs(g):
                pe.wait_ge(v_lo_ready, g * G + 1)
                pe.wait_ge(act_lo_ready, 2 * (g * G) + 2 + 2)
                for unit in range(OUT_BANKS):
                    pe.wait_ge(added, UNITS * g + unit + 1)
                    output_part(g, unit, 0)
                pe.wait_ge(v_lo_ready, g * G + 2)
                for unit in range(UNITS):
                    if unit % 8 == 0:
                        pe.wait_ge(act_lo_ready, 2 * (g * G + 1) + unit // 8 + 1 + 2)
                    if unit >= OUT_BANKS:
                        pe.wait_ge(added, UNITS * g + unit + 1)
                        output_part(g, unit, 0)
                    output_part(g, unit, 1).then_inc(unit_done, 1)

            def group(g, last):
                turn(g * G + 1, g, 1)
                hidden_products(g * G, 0)
                if not last:
                    turn(g * G + 2, g + 1, 0)
                hidden_products(g * G + 1, 1)
                outputs(g)

            pe.sem_inc(uT_lo_ready, 1)
            pe.sem_inc(gelu_done, 2)
            pe.sem_inc(added, OUT_BANKS)
            pe.sem_inc(unit_done, UNITS)
            turn(0, 0, 0)
            with pe.Fori(0, GROUPS - 1) as g:
                group(g, False)
            group(GROUPS - 1, True)

        @block.scalar
        def _(act):
            copy = lambda o, i: act.activation(o, i, ACT.Copy)

            def u_hi(n, b):
                act.wait_ge(u_turned, n + 1)
                copy(uT_hi[:, b, :, :], uT_ps).then_inc(uT_hi_ready, 1)

            def tile(g, b):
                n = g * G + b
                act.wait_ge(v_in[b], 16 * (g + 1))
                act.wait_ge(unit_done, UNITS * (g + 1))
                copy(v_hi[:, b, :], v_raw[:, b, :]).then_inc(v_hi_ready, 1)
                for half in range(2):
                    t = slice(half * HALF, (half + 1) * HALF)
                    act.wait_ge(hidden_done, 2 * n + half + 1)
                    act.wait_ge(act_lo_ready, 2 * n + half + 1)
                    act.activation(hidden[:, half, :], ps[:, 2 + half, :], ACT.Gelu).then_inc(gelu_done, 1)
                    act.wait_ge(gated, 2 * n + half + 1)
                    copy(act_hi[:, b, t], hidden[:, half, :]).then_inc(act_hi_ready, 1)

            u_hi(0, 0)
            with act.Fori(0, GROUPS - 1) as g:
                u_hi(g * G + 1, 1)
                tile(g, 0)
                u_hi(g * G + 2, 0)
                tile(g, 1)
            u_hi(TILES - 1, 1)
            tile(GROUPS - 1, 0)
            tile(GROUPS - 1, 1)

        @block.vector
        def _(dve):
            def u_lo(n, b):
                dve.wait_ge(uT_hi_ready, n + 1)
                dve.tensor_tensor(uT_lo[:, b, :, :], uT_ps, uT_hi[:, b, :, :].bitcast(F32), ALU.subtract).then_inc(uT_lo_ready, 1)

            def tile(g, b):
                n = g * G + b
                dve.wait_ge(v_hi_ready, n + 1)
                dve.tensor_tensor(v_lo[:, b, :], v_raw[:, b, :], v_hi[:, b, :].bitcast(F32), ALU.subtract).then_inc(v_lo_ready, 1)
                for half in range(2):
                    t = slice(half * HALF, (half + 1) * HALF)
                    if half == 0:
                        dve.wait_ge(gate_in[b], 16 * (g + 1))
                    dve.wait_ge(gelu_done, 2 * n + half + 1 + 2)
                    dve.tensor_tensor(hidden[:, half, :], hidden[:, half, :], gate[:, b, t], ALU.mult).then_inc(gated, 1)
                    dve.wait_ge(act_hi_ready, 2 * n + half + 1)
                    dve.tensor_tensor(act_lo[:, b, t], hidden[:, half, :], act_hi[:, b, t].bitcast(F32),
                                      ALU.subtract).then_inc(act_lo_ready, 1)

            def add_outputs(g):
                dve.wait_ge(x_in, 16)
                for unit in range(UNITS):
                    dve.wait_ge(unit_done, UNITS * (g + 1) + unit + 1)
                    x = X[:, unit // 2, (unit % 2) * HALF:(unit % 2 + 1) * HALF]
                    dve.tensor_tensor(x, ps[:, 4 + unit % OUT_BANKS, :], x, ALU.add).then_inc(added, 1)

            dve.sem_inc(act_lo_ready, 2)
            u_lo(0, 0)
            with dve.Fori(0, GROUPS - 1) as g:
                u_lo(g * G + 1, 1)
                tile(g, 0)
                u_lo(g * G + 2, 0)
                tile(g, 1)
                add_outputs(g)
            u_lo(TILES - 1, 1)
            tile(GROUPS - 1, 0)
            tile(GROUPS - 1, 1)
            add_outputs(GROUPS - 1)


def load_early(sp, raw, landed, v, gates, hidden_dram, n, b):
    sp.dma_start(raw[:, 0, b, :], hidden_dram[ds(n, 1), :, :].rearrange("a j t -> (a j) t")).then_inc(landed[b], 16)
    sp.dma_start(raw[:, 1, b, :].rearrange("j (q t) -> j q t", t=gates.shape[3]), gates_of(gates, n)).then_inc(landed[b], 16)
    sp.dma_start(raw[:, 2, b, :], v[ds(n * KEYS, KEYS), :]).then_inc(landed[b], 16)


def mix_early_experts(nc, v, gates, hidden_dram, hT, X, out, tiles, raw, landed):
    G = 2
    GROUPS = tiles // G
    UNITS = 16
    OUT_BANKS = 8
    with ExitStack() as ctx:
        sem = lambda n: nc.alloc_semaphore(f"ee_{n}")
        sb = lambda n, s, dt=F32: ctx.enter_context(nc.sbuf_tensor(f"ee_{n}", s, dt))
        ps = banks(nc, ctx, "ee_ps")
        hidden, gate, v_raw = (raw[:, a, :, :] for a in range(3))
        act_hi, act_lo = (h[:, 0:4, :].rearrange("p (s g) t -> p s g t", s=2) for h in hT)
        v_hi, v_lo = (h[:, 4:8, :].rearrange("p (s g) t -> p s g t", s=2) for h in hT)
        v_hi_ready, v_lo_ready, gated = sem("v_hi_r"), sem("v_lo_r"), sem("gated")
        act_hi_ready, act_lo_ready = sem("act_hi_r"), sem("act_lo_r")
        unit_done, added, stored = sem("unit_done"), sem("added"), sem("stored")
        block = ctx.enter_context(nc.Block())

        @block.sync
        def _(sp):
            with sp.Fori(1, GROUPS) as g:
                for b in range(G):
                    n = g * G + b
                    sp.wait_ge(act_lo_ready, n - 1)
                    load_early(sp, raw, landed, v, gates, hidden_dram, n, b)
            for tt in range(NT):
                sp.wait_ge(added, OUT_BANKS + UNITS * (GROUPS - 1) + 2 * tt + 2)
                sp.dma_start(out[tt * P:(tt + 1) * P, :], X[:, tt, :]).then_inc(stored, 16)
            sp.wait_ge(stored, 16 * NT)

        @block.tensor
        def _(pe):
            pe.sem_inc(unit_done, 2 * UNITS)
            pe.sem_inc(added, OUT_BANKS)
            with pe.Fori(0, GROUPS // 2) as two:
                for slot in range(2):
                    g = 2 * two + slot
                    pe.wait_ge(act_lo_ready, G * (g + 1))
                    pe.wait_ge(v_lo_ready, G * (g + 1))
                    for unit in range(UNITS):
                        tt, d = unit // 2, slice((unit % 2) * HALF, (unit % 2 + 1) * HALF)
                        pe.wait_ge(added, UNITS * g + unit + 1)
                        for b in range(G):
                            ins = product3(pe, ps[:, unit % OUT_BANKS, :],
                                           (act_hi[:, slot, b, tt * P:(tt + 1) * P], act_lo[:, slot, b, tt * P:(tt + 1) * P]),
                                           (v_hi[:, slot, b, d], v_lo[:, slot, b, d]), b == 0, b == G - 1)
                        ins.then_inc(unit_done, 1)

        @block.scalar
        def _(act):
            with act.Fori(0, GROUPS // 2) as two:
                for slot in range(2):
                    g = 2 * two + slot
                    for b in range(G):
                        act.wait_ge(landed[b], 48 * (g + 1))
                        act.wait_ge(unit_done, UNITS * (g + 1))
                        act.activation(v_hi[:, slot, b, :], v_raw[:, b, :], ACT.Copy).then_inc(v_hi_ready, 1)
                        act.wait_ge(gated, G * g + b + 1)
                        act.activation(act_hi[:, slot, b, :], hidden[:, b, :], ACT.Copy).then_inc(act_hi_ready, 1)

        @block.vector
        def _(dve):
            def prepare(g, slot):
                for b in range(G):
                    n = G * g + b
                    dve.wait_ge(landed[b], 48 * (g + 1))
                    dve.tensor_tensor(hidden[:, b, :], hidden[:, b, :], gate[:, b, :], ALU.mult).then_inc(gated, 1)
                    dve.wait_ge(v_hi_ready, n + 1)
                    dve.tensor_tensor(v_lo[:, slot, b, :], v_raw[:, b, :], v_hi[:, slot, b, :].bitcast(F32),
                                      ALU.subtract).then_inc(v_lo_ready, 1)
                    dve.wait_ge(act_hi_ready, n + 1)
                    dve.tensor_tensor(act_lo[:, slot, b, :], hidden[:, b, :], act_hi[:, slot, b, :].bitcast(F32),
                                      ALU.subtract).then_inc(act_lo_ready, 1)

            def add_outputs(g):
                for unit in range(UNITS):
                    dve.wait_ge(unit_done, UNITS * (g + 2) + unit + 1)
                    x = X[:, unit // 2, (unit % 2) * HALF:(unit % 2 + 1) * HALF]
                    dve.tensor_tensor(x, ps[:, unit % OUT_BANKS, :], x, ALU.add).then_inc(added, 1)

            prepare(0, 0)
            with dve.Fori(0, GROUPS // 2 - 1) as two:
                for slot in range(2):
                    prepare(2 * two + slot + 1, 1 - slot)
                    add_outputs(2 * two + slot)
            prepare(GROUPS - 1, 1)
            add_outputs(GROUPS - 2)
            add_outputs(GROUPS - 1)


def hybrid_block(nc, x, w_in, pool_w, w_out, w_query, sub_keys, u, v, attn_g, q_g, k_g, pool_scale, ffn_g,
                 ident_d, cos_d, sin_d, mask_d, inv_count_d, iota_d, out):
    x_spill = nc.dram_tensor("x_spill", (T, D), F32).ap()
    gates = nc.dram_tensor("gates", (T // 64, KEYS, KEYS, 64), F32).ap()
    search_pairs, spread_pairs = 12, 16
    early = 2 * (search_pairs + spread_pairs)
    hidden_dram = nc.dram_tensor("hidden", (early, P, T), F32).ap()
    with ExitStack() as whole:
        sb = lambda ctx, n, s, dt=F32: ctx.enter_context(nc.sbuf_tensor(n, s, dt))
        ident = sb(whole, "ident", [P, P])
        X = sb(whole, "X", [P, NT, D])
        with ExitStack() as mixing:
            mixing.enter_context(nc.cleanup_on_exit())
            QKV = sb(mixing, "QKV", [P, NT, 3 * DA])
            poolT = sb(mixing, "poolT", [P, NG, PAD + T])
            OT = sb(mixing, "OT", [P, HEADS // 2, T])
            inv_sum = sb(mixing, "inv_sum", [P, NT, HEADS])
            with ExitStack() as ctx:
                hT = [sb(ctx, f"hT1_{n}", [P, KD, T], F32R) for n in ("hi", "lo")]
                scratch = OT[:, :, :].rearrange("p n d -> p (n d)")
                norm_and_transpose(nc, "n1", X, x, attn_g, scratch, *hT, ident, ident_d, None)
                project_inputs(nc, w_in, *hT, QKV, poolT)
            with ExitStack() as ctx:
                QT = sb(ctx, "QT", [P, 8, T])
                inv_count = sb(ctx, "inv_count", [P, NG, PAD])
                with ExitStack() as inner:
                    cos, sin = sb(inner, "cos", [P, NT, HD // 2]), sb(inner, "sin", [P, NT, HD // 2])
                    gains = sb(inner, "gains", [P, 2, HD])
                    consts = [(cos[:, :, :], cos_d.rearrange("(n p) d -> p n d", p=P)),
                              (sin[:, :, :], sin_d.rearrange("(n p) d -> p n d", p=P)),
                              (gains[:, 0, :], q_g.partition_broadcast(P)), (gains[:, 1, :], k_g.partition_broadcast(P)),
                              (inv_count[:, :, :], inv_count_d)]
                    prepare_heads(nc, QKV, QT, cos, sin, gains, ident, consts)
                pooled = attend(nc, QKV, QT, OT, inv_sum, poolT, inv_count, mask_d, ident)
            with ExitStack() as ctx:
                mixT = [sb(ctx, f"mixT_{n}", [P, KD, T], F32R) for n in ("hi", "lo")]
                mix(nc, OT, inv_sum, pooled, pool_w, pool_scale, *mixT, ident)
                project_output(nc, w_out, *mixT, X)
        iota = sb(whole, "iota", [P, KEYS])
        hT = [sb(whole, f"hT2_{n}", [P, KD, T], F32R) for n in ("hi", "lo")]
        with ExitStack() as ctx:
            scratch = sb(ctx, "scratch", [P, 4 * D])
            norm_and_transpose(nc, "n2", X, None, ffn_g, scratch[:, :], *hT, ident, None, x_spill, (iota[:, :], iota_d))
        W = Weights(nc, whole, "rt_w")
        flat = X[:, :, :].rearrange("p n d -> p (n d)")
        scores = flat.rearrange("p (b t g n) -> p b t g n", b=2, t=NT, g=4)
        picksT = flat[:, 4 * D:8 * D].rearrange("p (a t) -> p a t", a=4)
        with ExitStack() as ctx:
            picks = sb(ctx, "picks", [P, NT, 3, KEYS])
            retrieve(nc, w_query, sub_keys, *hT, W, scores, picks, iota, ident, u, hidden_dram, search_pairs)
            turn_picks(nc, picks, picksT, W, ident)
        last_part = sb(whole, "last_part", [P, 32, 256])
        part_written, late_u_in = ([nc.alloc_semaphore(f"{n}{b}") for b in range(2)] for n in ("part_written", "late_u_in"))
        with ExitStack() as ctx:
            hidden_stored = spread_gates(nc, ctx, picksT, iota, ident, gates, W, X, hT, u, hidden_dram,
                                         2 * search_pairs, spread_pairs, last_part, part_written, late_u_in)
        ee_raw = last_part[:, 0:24, :].rearrange("p a n -> p (a n)").rearrange("p (a g d) -> p a g d", a=3, g=2)
        ee_in = [nc.alloc_semaphore(f"ee_in{b}") for b in range(2)]
        mix_late_experts(nc, u, v, gates, hT, x_spill, X, ident, early, W, part_written, late_u_in, hidden_stored,
                         spread_pairs, hidden_dram, ee_raw, ee_in)
        mix_early_experts(nc, v, gates, hidden_dram, hT, X, out, early, ee_raw, ee_in)


def constants():
    freqs = np.float32(10000.0) ** (-np.arange(0, HD, 2, dtype=np.float32) / np.float32(HD))
    angle = np.arange(T, dtype=np.float32)[:, None] * freqs[None, :].astype(np.float32)
    back = np.arange(P)[:, None] - np.arange(T)[None, :] + (T - P)
    count = sum(((back >= 0) & (back <= window) & (back % dil == 0)).astype(np.int64)
                for window, dil in ((128, 1), (512, 4), (2048, 16)))
    mask = np.where(count > 0, np.log(np.maximum(count, 1)), NEG).astype(np.float32)
    t = np.arange(PAD)
    inv = np.stack([1.0 / np.minimum(t + 1, w) for w in WINDOWS]).astype(np.float32)
    return {
        "ident": np.eye(P, dtype=np.float32), "cos": np.cos(angle), "sin": np.sin(angle), "mask": mask,
        "inv_count": np.ascontiguousarray(np.broadcast_to(inv, (P, NG, PAD))),
        "iota": np.ascontiguousarray(np.broadcast_to(np.arange(KEYS, dtype=np.float32), (P, KEYS))),
    }


def kernel(**inputs):
    import concourse.bacc as bacc
    from concourse.bass_utils import run_bass_kernel_spmd

    shapes = {
        "x": (T, D), "w_in": (D, 3 * DA + NG * P), "pool_w": (NG, P, P), "w_out": (D, D),
        "peer_w_query": (D, PH * 2 * P), "peer_sub_keys": (PH * 2 * KEYS, P),
        "peer_u": (KEYS * KEYS, D), "peer_v": (KEYS * KEYS, D),
        "attn_norm_g": (D,), "q_norm_g": (HD,), "k_norm_g": (HD,), "pool_scale": (NG * P,), "ffn_norm_g": (D,),
    }
    nc = bacc.Bacc("TRN2", target_bir_lowering=False, num_devices=1)
    arrays = {f"in_{n}": np.ascontiguousarray(inputs[n]).reshape(s) for n, s in shapes.items()}
    arrays["in_pool_scale"] = np.ascontiguousarray(arrays["in_pool_scale"].reshape(NG, P).T)
    arrays |= {f"const_{n}": a for n, a in constants().items()}
    args = [nc.dram_tensor(n, a.shape, mybir.dt.from_np(a.dtype), kind="ExternalInput").ap() for n, a in arrays.items()]
    out = nc.dram_tensor("out", (T, D), F32, kind="ExternalOutput").ap()
    hybrid_block(nc, *args, out)
    r = run_bass_kernel_spmd(nc, [arrays], core_ids=[0])
    return r.results[0]["out"].reshape(1, T, D)
```

```python
from contextlib import ExitStack

import numpy as np
import concourse.bass as bass
from concourse import mybir

F32 = mybir.dt.float32
F32R = mybir.dt.float32r
U32 = mybir.dt.uint32
BF16 = mybir.dt.bfloat16
ALU = mybir.AluOpType
ACT = mybir.ActivationFunctionType
AX = mybir.AxisListType
ds = bass.ds

P = 128
T = 1024
NT = T // P
D = 1024
KD = D // P
HALF = 512
HEADS = 8
HD = 64
DA = HEADS * HD
WINDOWS = (2, 4, 8, 16)
NG = len(WINDOWS)
PAD = max(WINDOWS)
EPS = 1e-6
KEYS = 128
PH = 8
TOPK = 16
NEG = -1e30
LOWEST = -3.0e38
RING = 4


def hold(eng, sem, value, passed):
    eng.wait_ge(sem, value)
    eng.sem_inc(passed, 1)


def banks(nc, ctx, name):
    return ctx.enter_context(nc.psum_tensor(name, [P, 8, HALF], F32))


def norm_and_transpose(nc, name, X, x_dram, gain_row, scratch, hT_hi, hT_lo, ident, ident_dram, spill, ahead):
    BATCH = NT // 2
    with ExitStack() as ctx:
        sem = lambda n: nc.alloc_semaphore(f"{name}_{n}")
        ps = banks(nc, ctx, f"{name}_ps")
        stats = ctx.enter_context(nc.sbuf_tensor(f"{name}_stats", [P, 4, NT], F32))
        ssq, mean, root, rstd = (stats[:, i, :] for i in range(4))
        slots = [scratch[:, i * D:(i + 1) * D] for i in range(4)]
        hn, gain, junk = lambda tt: slots[tt % 3], slots[3], slots[2]
        turned_ps = lambda tt: ps[:, 2 * (tt % 4):2 * (tt % 4) + 2, :].rearrange("p b (k t) -> p (b k) t", t=P)
        x_in = [sem(f"x_in{i}") for i in range(NT)]
        consts_in, spilled = sem("consts_in"), sem("spilled")
        squares, mean_ready, root_ready, rstd_ready = sem("squares"), sem("mean"), sem("root"), sem("rstd")
        hn_ready, turned, hi_ready, lo_ready = sem("hn"), sem("turned"), sem("hi"), sem("lo")
        block = ctx.enter_context(nc.Block())

        @block.sync
        def _(sp):
            if x_dram is not None:
                for tt in range(NT):
                    sp.dma_start(X[:, tt, :], x_dram[tt * P:(tt + 1) * P, :]).then_inc(x_in[tt], 16)
                sp.dma_start(ident[:, :], ident_dram).then_inc(consts_in, 16)
            sp.dma_start(gain, gain_row.partition_broadcast(P)).then_inc(consts_in, 16)
            for to, source, landed in ahead:
                sp.dma_start(to, source).then_inc(landed, 16)
            if spill is not None:
                sp.dma_start(spill.rearrange("(n p) d -> p n d", p=P), X[:, :, :]).then_inc(spilled, 16)
                sp.wait_ge(spilled, 16)

        @block.scalar
        def _(act):
            for tt in range(NT):
                if x_dram is not None:
                    act.wait_ge(x_in[tt], 16)
                if tt:
                    act.wait_ge(squares, tt)
                act.activation(junk, X[:, tt, :], ACT.Square, accum_out=ssq[:, tt:tt + 1]).then_inc(squares, 1)
                if tt % BATCH == BATCH - 1:
                    batch = slice(tt - BATCH + 1, tt + 1)
                    act.wait_ge(mean_ready, tt // BATCH + 1)
                    act.activation(root[:, batch], mean[:, batch], ACT.Sqrt).then_inc(root_ready, 1)
            for tt in range(NT):
                act.wait_ge(turned, tt + 1)
                act.activation(hT_hi[:, :, tt * P:(tt + 1) * P], turned_ps(tt), ACT.Copy).then_inc(hi_ready, 1)

        @block.vector
        def _(dve):
            dve.wait_ge(consts_in, 32 if x_dram is not None else 16)

            def roots(n):
                batch = slice(n * BATCH, (n + 1) * BATCH)
                dve.wait_ge(squares, (n + 1) * BATCH)
                dve.tensor_scalar(mean[:, batch], ssq[:, batch], 1.0 / D, EPS, ALU.mult, ALU.add).then_inc(mean_ready, 1)
                dve.wait_ge(root_ready, n + 1)
                dve.reciprocal(rstd[:, batch], root[:, batch]).then_inc(rstd_ready, 1)
                dve.wait_ge(rstd_ready, n + 1)

            def scale_tile(tt):
                if tt >= 3:
                    dve.wait_ge(turned, tt - 2)
                dve.scalar_tensor_tensor(out=hn(tt), in0=X[:, tt, :], scalar=rstd[:, tt:tt + 1], in1=gain,
                                         op0=ALU.mult, op1=ALU.mult).then_inc(hn_ready, 1)

            roots(0)
            scale_tile(0)
            scale_tile(1)
            roots(1)
            for tt in range(NT):
                if tt + 2 < NT:
                    scale_tile(tt + 2)
                dve.wait_ge(hi_ready, tt + 1)
                dve.tensor_tensor(hT_lo[:, :, tt * P:(tt + 1) * P], turned_ps(tt),
                                  hT_hi[:, :, tt * P:(tt + 1) * P].bitcast(F32), ALU.subtract).then_inc(lo_ready, 1)

        @block.tensor
        def _(pe):
            pe.wait_ge(consts_in, 32 if x_dram is not None else 16)
            for tt in range(NT):
                pe.wait_ge(hn_ready, tt + 1)
                if tt >= 4:
                    pe.wait_ge(lo_ready, tt - 3)
                for k in range(KD):
                    ins = pe.transpose(turned_ps(tt)[:, k, :], hn(tt)[:, k * P:(k + 1) * P], ident[:, :])
                ins.then_inc(turned, 1)


class Weights:

    def __init__(self, nc, ctx, name):
        sem = lambda n: nc.alloc_semaphore(f"{name}_{n}")
        self.raw = ctx.enter_context(nc.sbuf_tensor(f"{name}_raw", [P, RING, HALF], F32))
        self.hi = ctx.enter_context(nc.sbuf_tensor(f"{name}_hi", [P, RING, HALF], F32R))
        self.lo = ctx.enter_context(nc.sbuf_tensor(f"{name}_lo", [P, RING, HALF], F32R))
        self.landed = [sem(f"landed{i}") for i in range(RING)]
        self.hi_ready, self.lo_ready, self.used = sem("hi_ready"), sem("lo_ready"), sem("used")


def product3(pe, out, left, right, first, last):
    (lh, ll), (rh, rl) = left, right
    pe.matmul(out, lh, rh, start=first, stop=False)
    pe.matmul(out, lh, rl, start=False, stop=False)
    return pe.matmul(out, ll, rh, start=False, stop=last)


def first_weights(W, source):
    return [(W.raw[:, k, :], source[k * P:(k + 1) * P, 0:HALF], W.landed[k]) for k in range(RING)]


def load_weights(eng, W, source, chunks, first=0):
    def load(c, k):
        eng.wait_ge(W.lo_ready, c * KD + k + 1)
        eng.dma_start(W.raw[:, k % RING, :], source[k * P:(k + 1) * P, ds(c * HALF, HALF)]).then_inc(
            W.landed[k % RING], 16)

    for k in range(first, KD):
        load(0, k)
    with eng.Fori(1, chunks) as c:
        for k in range(KD):
            load(c, k)


HEAD = range(RING - 1)
REST = range(RING - 1, KD)


def split_hi(act, W, c, slices=range(KD)):
    for k in slices:
        act.wait_ge(W.landed[k % RING], 16 * (2 * c + k // RING + 1))
        act.wait_ge(W.used, c * KD + k + 1)
        act.activation(W.hi[:, k % RING, :], W.raw[:, k % RING, :], ACT.Copy).then_inc(W.hi_ready, 1)


def split_lo(eng, W, c, slices=range(KD)):
    for k in slices:
        eng.wait_ge(W.hi_ready, c * KD + k + 1)
        eng.tensor_tensor(W.lo[:, k % RING, :], W.raw[:, k % RING, :],
                          W.hi[:, k % RING, :].bitcast(F32), ALU.subtract).then_inc(W.lo_ready, 1)


def wait_bank(eng, W, bank_done, c, b):
    if b < 7:
        eng.wait_ge(bank_done, c * 7 + b + 1)
    else:
        eng.wait_ge(W.used, RING + (c + 1) * KD)


def weight_chunk(pe, W, ps, c, free, bank_done, operands):
    for k in range(KD):
        pe.wait_ge(W.lo_ready, RING + c * KD + k + 1)
        for b in range(8):
            if k == 0:
                free(b)
            left, right = operands(k, b)
            ins = product3(pe, ps[:, b, :], left, right, k == 0, k == KD - 1)
            if k == KD - 1 and b < 7:
                ins.then_inc(bank_done, 1)
        ins.then_inc(W.used, 1)


def token_operands(W, hT_hi, hT_lo):
    return lambda k, b: ((hT_hi[:, k, b * P:(b + 1) * P], hT_lo[:, k, b * P:(b + 1) * P]),
                         (W.hi[:, k % RING, :], W.lo[:, k % RING, :]))


def channel_operands(W, hT_hi, hT_lo):
    def at(k, b):
        n, t = (b % 4) * P, (b // 4) * HALF
        return ((W.hi[:, k % RING, n:n + P], W.lo[:, k % RING, n:n + P]),
                (hT_hi[:, k, t:t + HALF], hT_lo[:, k, t:t + HALF]))
    return at


def project_inputs(nc, w_in, hT_hi, hT_lo, W, QKV, poolT, scratch, consts):
    NH = 2 * HEADS
    with ExitStack() as ctx:
        sem = lambda n: nc.alloc_semaphore(f"pi_{n}")
        sb = lambda n, s: ctx.enter_context(nc.sbuf_tensor(f"pi_{n}", s, F32))
        ps = banks(nc, ctx, "pi_ps")
        cos, sin, gains = sb("cos", [P, NT, HD // 2]), sb("sin", [P, NT, HD // 2]), sb("gains", [P, 2, HD])
        stats = sb("stats", [P, 3, NT, NH])
        normed, turnc, turns = (scratch[:, i * 2 * DA:(i + 1) * 2 * DA] for i in range(3))
        square = (normed, turnc)
        bank_done, even_free, odd_free, zeroed = sem("bank_done"), sem("even_free"), sem("odd_free"), sem("zeroed")
        consts_in, squared, summed = sem("consts_in"), sem("squared"), sem("summed")
        mean_ready, root_ready, rstd_ready = sem("mean"), sem("root"), sem("rstd")
        normed_ready, gained, cos_ready = sem("normed_r"), sem("gained"), sem("cos")
        sin_ready, rotated = sem("sin"), sem("rotated")
        block = ctx.enter_context(nc.Block())
        heads = lambda ap: ap.rearrange("p (h d) -> p h d", d=HD)
        halves = lambda ap: ap.rearrange("p (h s d) -> p h s d", s=2, d=HD // 2)
        later = [(2, k) for k in REST] + [(3, k) for k in HEAD] + [(3, k) for k in REST]
        BEFORE = KD

        def channel_slot(b):
            return poolT[:, b % 4, PAD + (b // 4) * HALF:PAD + (b // 4 + 1) * HALF]

        def out_slot(c, b):
            return channel_slot(b) if isinstance(c, int) and c == 3 else QKV[:, b, ds(c * HALF, HALF)]

        @block.sync
        def _(sp):
            sources = [cos_d.rearrange("(n p) d -> p n d", p=P) for cos_d in consts[:2]]
            sources += [g.partition_broadcast(P) for g in consts[2:]]
            for to, source in zip((cos[:, :, :], sin[:, :, :], gains[:, 0, :], gains[:, 1, :]), sources):
                sp.dma_start(to, source).then_inc(consts_in, 16)
            load_weights(sp, W, w_in, 4, RING)

        @block.scalar
        def _(act):
            def copy_out(c):
                for b in range(0, 8, 2):
                    wait_bank(act, W, bank_done, c, b)
                    act.activation(out_slot(c, b), ps[:, b, :], ACT.Copy).then_inc(even_free, 1)

            split_hi(act, W, 0, HEAD)
            with act.Fori(0, 2) as c:
                split_hi(act, W, c, REST)
                split_hi(act, W, c + 1, HEAD)
                copy_out(c)
            act.wait_ge(even_free, 4 + 8)
            act.wait_ge(odd_free, 4 + 8)
            for n, (c, k) in enumerate(later):
                if n == BEFORE:
                    copy_out(2)
                if n < NT // 2:
                    for tt in (2 * n, 2 * n + 1):
                        if tt >= 2:
                            act.wait_ge(summed, tt - 1)
                        act.activation(square[tt % 2], QKV[:, tt, 0:2 * DA], ACT.Square).then_inc(squared, 1)
                if n == NT // 2:
                    act.wait_ge(mean_ready, 1)
                    act.activation(stats[:, 1], stats[:, 0], ACT.Sqrt).then_inc(root_ready, 1)
                split_hi(act, W, c, (k,))
            copy_out(3)

        @block.gpsimd
        def _(pool):
            pool.wait_ge(consts_in, 16 * 4)
            with pool.Fori(0, NT) as tt:
                pool.wait_ge(gained, tt + 1)
                pool.wait_ge(rotated, tt + 1)
                s = sin[:, ds(tt, 1), :].broadcast_to([P, NH, HD // 2])
                x, o = halves(normed), halves(turns)
                pool.tensor_tensor(o[:, :, 0, :], x[:, :, 1, :], s, ALU.mult).then_inc(sin_ready, 1)
                pool.tensor_tensor(o[:, :, 1, :], x[:, :, 0, :], s, ALU.mult).then_inc(sin_ready, 1)

        @block.vector
        def _(dve):
            def copy_out(c):
                for b in range(1, 8, 2):
                    wait_bank(dve, W, bank_done, c, b)
                    dve.tensor_copy(out_slot(c, b), ps[:, b, :]).then_inc(odd_free, 1)

            def scale(tt):
                dve.wait_ge(rotated, tt + 1)
                dve.tensor_tensor(heads(turnc), heads(QKV[:, tt, 0:2 * DA]),
                                  stats[:, 2, tt, :].unsqueeze(2).broadcast_to([P, NH, HD]),
                                  ALU.mult).then_inc(normed_ready, 1)
                dve.wait_ge(normed_ready, tt + 1)
                dve.tensor_tensor(normed.rearrange("p (a h d) -> p a h d", a=2, d=HD),
                                  turnc.rearrange("p (a h d) -> p a h d", a=2, d=HD),
                                  gains[:, :, :].unsqueeze(2).broadcast_to([P, 2, HEADS, HD]),
                                  ALU.mult).then_inc(gained, 1)

            def rotate(tt):
                dve.wait_ge(gained, tt + 1)
                dve.tensor_tensor(turnc.rearrange("p (h d) -> p h d", d=HD // 2),
                                  normed.rearrange("p (h d) -> p h d", d=HD // 2),
                                  cos[:, tt:tt + 1, :].broadcast_to([P, 2 * NH, HD // 2]), ALU.mult).then_inc(cos_ready, 1)
                dve.wait_ge(cos_ready, tt + 1)
                dve.wait_ge(sin_ready, 2 * tt + 2)
                out, c, s = halves(QKV[:, tt, 0:2 * DA]), halves(turnc), halves(turns)
                dve.tensor_tensor(out[:, :, 0, :], c[:, :, 0, :], s[:, :, 0, :], ALU.subtract)
                dve.tensor_tensor(out[:, :, 1, :], c[:, :, 1, :], s[:, :, 1, :], ALU.add).then_inc(rotated, 1)

            dve.sem_inc(W.lo_ready, RING)
            dve.sem_inc(rotated, 1)
            dve.memset(poolT[:, :, 0:PAD], 0.0).then_inc(zeroed, 1)
            split_lo(dve, W, 0, HEAD)
            with dve.Fori(0, 2) as c:
                split_lo(dve, W, c, REST)
                split_lo(dve, W, c + 1, HEAD)
                copy_out(c)
            first_tile = NT // 2
            for n, (c, k) in enumerate(later):
                if n == BEFORE:
                    copy_out(2)
                if n < NT // 2:
                    for tt in (2 * n, 2 * n + 1):
                        dve.wait_ge(squared, tt + 1)
                        dve.tensor_reduce(stats[:, 2, tt, :], heads(square[tt % 2]), AX.X, ALU.add).then_inc(summed, 1)
                if n == NT // 2 - 1:
                    dve.wait_ge(summed, NT)
                    dve.tensor_scalar(stats[:, 0], stats[:, 2], 1.0 / HD, EPS, ALU.mult, ALU.add).then_inc(mean_ready, 1)
                if n == first_tile:
                    dve.wait_ge(root_ready, 1)
                    dve.reciprocal(stats[:, 2], stats[:, 1]).then_inc(rstd_ready, 1)
                    dve.wait_ge(rstd_ready, 1)
                    dve.wait_ge(consts_in, 16 * 4)
                if 0 <= n - first_tile < NT:
                    scale(n - first_tile)
                split_lo(dve, W, c, (k,))
                if 0 <= n - first_tile < NT:
                    rotate(n - first_tile)
            copy_out(3)

        @block.tensor
        def _(pe):
            pe.sem_inc(W.used, RING)
            pe.sem_inc(even_free, 4)
            pe.sem_inc(odd_free, 4)

            def free(c):
                return lambda b: pe.wait_ge((even_free, odd_free)[b % 2], c * 4 + b // 2 + 1)

            with pe.Fori(0, 3) as c:
                weight_chunk(pe, W, ps, c, free(c), bank_done, token_operands(W, hT_hi, hT_lo))
            weight_chunk(pe, W, ps, 3, free(3), bank_done, channel_operands(W, hT_hi, hT_lo))


def turn_heads(nc, QKV, QT, ident, ahead):
    with ExitStack() as ctx:
        sem = lambda n: nc.alloc_semaphore(f"th_{n}")
        ps = banks(nc, ctx, "th_ps")
        turned, q_ready, k_ready = sem("turned"), sem("q"), sem("k")
        block = ctx.enter_context(nc.Block())
        bank = lambda tt, a: ps[:, 2 * (tt % 4) + a, :].rearrange("p (n t) -> p n t", t=P)

        @block.sync
        def _(sp):
            for to, source, landed in ahead:
                sp.dma_start(to, source).then_inc(landed, 16)

        @block.tensor
        def _(pe):
            for tt in range(NT):
                if tt >= 4:
                    pe.wait_ge(q_ready, tt - 3)
                    pe.wait_ge(k_ready, tt - 3)
                for pair in range(8):
                    ins = pe.transpose(bank(tt, pair // 4)[:, pair % 4, :], QKV[:, tt, pair * P:(pair + 1) * P], ident[:, :])
                ins.then_inc(turned, 1)

        @block.scalar
        def _(act):
            for tt in range(NT):
                act.wait_ge(turned, tt + 1)
                act.activation(QT[:, 0:4, tt * P:(tt + 1) * P], bank(tt, 0), ACT.Copy, scale=HD ** -0.5).then_inc(q_ready, 1)

        @block.vector
        def _(dve):
            for tt in range(NT):
                dve.wait_ge(turned, tt + 1)
                dve.tensor_copy(QT[:, 4:8, tt * P:(tt + 1) * P], bank(tt, 1)).then_inc(k_ready, 1)


class AttentionLoads:

    def __init__(self, nc, ctx, QKV, mask_dram, inv_count_dram):
        sb = lambda n, s: ctx.enter_context(nc.sbuf_tensor(f"at_{n}", s, F32))
        self.mask, self.inv_count = sb("mask", [P, T]), sb("inv_count", [P, NG, PAD])
        self.values = sb("values", [P, 2, NT, P])
        self.mask_in, self.counts_in = nc.alloc_semaphore("at_mask_in"), nc.alloc_semaphore("at_counts_in")
        self.values_in = [nc.alloc_semaphore(f"at_values_in{s}") for s in range(2)]
        self.QKV = QKV
        self.first = [(self.mask[:, :], mask_dram, self.mask_in), (self.inv_count[:, :, :], inv_count_dram, self.counts_in)]
        self.first += [self.values_load(pair, pair) for pair in range(2)]

    def values_load(self, pair, s):
        return self.values[:, s, :, :], self.QKV[:, :, ds(2 * DA + pair * P, P)], self.values_in[s]


def attend(nc, QKV, QT, OT, inv_sum, poolT, loads, ident):
    stage = [QKV[:, 0:2, 0:T], QKV[:, 2:4, 0:T]]
    pooled = QKV[:, 4:8, 0:T]
    PAIR = 2 * NT
    UNITS = 2 * PAIR
    ORDER = (7, 6, 5, 0, 2, 1, 3, 4)
    assert sorted(ORDER) == list(range(NT))
    tile = lambda u: ORDER[u % NT]
    with ExitStack() as ctx:
        sem = lambda n: nc.alloc_semaphore(f"at_{n}")
        sb = lambda n, s: ctx.enter_context(nc.sbuf_tensor(f"at_{n}", s, F32))
        ps = banks(nc, ctx, "at_ps")
        mask, values, inv_count = loads.mask, loads.values, loads.inv_count
        masked, probs, probsT = sb("masked", [P, 2, T]), sb("probs", [P, 2, T]), sb("probsT", [P, 2, T])
        small = sb("small", [P, 3, 2])
        windows = sb("windows", [P, 2, PAD + T])
        mask_in, counts_in, staged = loads.mask_in, loads.counts_in, [sem("staged0"), sem("staged1")]
        scores_ready, masked_ready = sem("scores"), sem("masked_r")
        negmax_ready, probs_ready, turned = sem("negmax"), sem("probs_r"), sem("turned")
        left_ready, right_ready, pv_done = sem("left"), sem("right"), sem("pv")
        inv_ready, out_ready, pool_step = sem("inv"), sem("out"), sem("pool_step")
        passed = sem("passed")
        block = ctx.enter_context(nc.Block())
        scores = lambda u: ps[:, 2 * (u % 2):2 * (u % 2) + 2, :].rearrange("p b n -> p (b n)")
        psT = ps[:, 4:6, :].rearrange("p b n -> p (b n)")
        psO = lambda u: ps[:, 6 + u % 2, 0:P]
        cols = lambda u: (tile(u) + 1) * P

        def rights(u):
            return sum(cols(w) > HALF for w in range(u + 1))

        RIGHTS = rights(UNITS - 1)

        @block.sync
        def _(sp):
            def load(two, s):
                pair = 2 * two + s
                sp.dma_start(stage[s][:, 0, :], QT[:, ds(pair, 1), :].rearrange("p a t -> p (a t)")).then_inc(staged[s], 16)
                sp.dma_start(stage[s][:, 1, :], QT[:, ds(pair + 4, 1), :].rearrange("p a t -> p (a t)")).then_inc(staged[s], 16)

            load(0, 0)
            sp.wait_ge(staged[0], 32)
            load(0, 1)
            with sp.Fori(1, HEADS // 4) as two:
                for s in range(2):
                    sp.wait_ge(pv_done, UNITS * two + PAIR * (s - 1))
                    load(two, s)
                    to, source, landed = loads.values_load(2 * two + s, s)
                    sp.dma_start(to, source).then_inc(landed, 16)

        @block.tensor
        def _(pe):
            with pe.Fori(0, HEADS // 4) as two:
                for step in range(UNITS + 2):
                    if step < UNITS:
                        u, s, rows = step, step // PAIR, slice(step // NT % 2 * HD, (step // NT % 2 + 1) * HD)
                        if u % PAIR == 0:
                            pe.wait_ge(staged[s], 32 * two + 32)
                        if u >= 2:
                            pe.wait_ge(masked_ready, UNITS * two + u - 1)
                        for c0 in range(0, cols(u), HALF):
                            c1 = min(c0 + HALF, cols(u))
                            ins = pe.matmul(scores(u)[:, c0:c1], stage[s][rows, 0, tile(u) * P:(tile(u) + 1) * P],
                                            stage[s][rows, 1, c0:c1], start=True, stop=True)
                        ins.then_inc(scores_ready, 1)
                    if 0 < step <= UNITS:
                        u = step - 1
                        pe.wait_ge(probs_ready, UNITS * two + u + 1)
                        if u >= 1:
                            pe.wait_ge(left_ready, UNITS * two + u)
                            if cols(u - 1) > HALF:
                                pe.wait_ge(right_ready, RIGHTS * two + rights(u - 1))
                        for b in range(tile(u) + 1):
                            ins = pe.transpose(psT[:, b * P:(b + 1) * P], probs[:, u % 2, b * P:(b + 1) * P], ident[:, :])
                        ins.then_inc(turned, 1)
                    if step >= 2:
                        u = step - 2
                        if u % PAIR == 0:
                            pe.wait_ge(loads.values_in[u // PAIR], 16 * two + 16)
                        pe.wait_ge(left_ready, UNITS * two + u + 1)
                        if cols(u) > HALF:
                            pe.wait_ge(right_ready, RIGHTS * two + rights(u))
                        if u >= 2:
                            pe.wait_ge(out_ready, UNITS * two + u - 1)
                        n = tile(u) + 1
                        for b in range(n):
                            ins = pe.matmul(psO(u), values[:, u // PAIR, b, :], probsT[:, u % 2, b * P:(b + 1) * P],
                                            start=b == 0, stop=b == n - 1)
                        ins.then_inc(pv_done, 1)

        @block.scalar
        def _(act):
            with act.Fori(0, HEADS // 4) as two:
                for step in range(UNITS + 1):
                    if step < UNITS:
                        u, n = step, cols(step)
                        act.wait_ge(negmax_ready, UNITS * two + u + 1)
                        if u >= 2:
                            act.wait_ge(turned, UNITS * two + u - 1)
                            act.wait_ge(inv_ready, UNITS * two + u - 1)
                        act.activation(probs[:, u % 2, 0:n], masked[:, u % 2, 0:n], ACT.Exp,
                                       bias=small[:, 1, u % 2:u % 2 + 1],
                                       accum_out=small[:, 2, u % 2:u % 2 + 1]).then_inc(probs_ready, 1)
                    if step >= 1:
                        u = step - 1
                        act.wait_ge(turned, UNITS * two + u + 1)
                        if u >= 2:
                            act.wait_ge(pv_done, UNITS * two + u - 1)
                        n = min(cols(u), HALF)
                        act.activation(probsT[:, u % 2, 0:n], psT[:, 0:n], ACT.Copy).then_inc(left_ready, 1)

        @block.vector
        def _(dve):
            dve.wait_ge(mask_in, 16)
            with dve.Fori(0, HEADS // 4) as two:
                for step in range(UNITS + 2):
                    if step < UNITS:
                        u, n = step, cols(step)
                        if u >= 2:
                            dve.wait_ge(probs_ready, UNITS * two + u - 1)
                        hold(dve, scores_ready, UNITS * two + u + 1, passed)
                        dve.tensor_tensor_reduce(masked[:, u % 2, 0:n], scores(u)[:, 0:n], mask[:, T - n:T],
                                                 1.0, LOWEST, ALU.add, ALU.max,
                                                 small[:, 0, u % 2:u % 2 + 1]).then_inc(masked_ready, 1)
                        dve.wait_ge(masked_ready, UNITS * two + u + 1)
                        dve.tensor_scalar(small[:, 1, u % 2:u % 2 + 1], small[:, 0, u % 2:u % 2 + 1], -1.0, None,
                                          ALU.mult).then_inc(negmax_ready, 1)
                    if 0 < step <= UNITS:
                        u = step - 1
                        if cols(u) > HALF:
                            dve.wait_ge(turned, UNITS * two + u + 1)
                            if u >= 2:
                                dve.wait_ge(pv_done, UNITS * two + u - 1)
                            dve.tensor_copy(probsT[:, u % 2, HALF:cols(u)], psT[:, HALF:cols(u)]).then_inc(right_ready, 1)
                    if step >= 2:
                        u = step - 2
                        rows = slice(u // NT % 2 * HD, (u // NT % 2 + 1) * HD)
                        dve.wait_ge(pv_done, UNITS * two + u + 1)
                        dve.tensor_copy(OT[rows, ds(2 * two + u // PAIR, 1), tile(u) * P:(tile(u) + 1) * P].rearrange("p a t -> p (a t)"),
                                        psO(u)[rows, :]).then_inc(out_ready, 1)
                    if 0 < step <= UNITS:
                        u = step - 1
                        dve.wait_ge(probs_ready, UNITS * two + u + 1)
                        dve.reciprocal(inv_sum[:, tile(u), ds(4 * two + u // NT, 1)], small[:, 2, u % 2:u % 2 + 1]).then_inc(inv_ready, 1)

        @block.gpsimd
        def _(pool):
            pool.memset(windows[:, :, 0:PAD], 0.0).then_inc(pool_step, 1)
            n = 1

            def step(ins):
                nonlocal n
                ins.then_inc(pool_step, 1)
                n += 1
                pool.wait_ge(pool_step, n)

            pool.wait_ge(pool_step, 1)
            pool.wait_ge(counts_in, 16)
            for g, w in enumerate(WINDOWS):
                source, reach = poolT[:, g, :], 1
                while reach < w:
                    to = windows[:, reach.bit_length() % 2, :]
                    step(pool.tensor_tensor(to[:, PAD:], source[:, PAD:], source[:, PAD - reach:PAD + T - reach], ALU.add))
                    source, reach = to, 2 * reach
                step(pool.tensor_tensor(pooled[:, g, 0:PAD], source[:, PAD:2 * PAD], inv_count[:, g, :], ALU.mult))
                step(pool.tensor_scalar(pooled[:, g, PAD:T], source[:, 2 * PAD:], 1.0 / w, None, ALU.mult))
                step(pool.tensor_tensor(pooled[:, g, :], pooled[:, g, :], poolT[:, g, PAD:], ALU.subtract))
    return pooled


def mix(nc, OT, inv_sum, pooled, pool_w, pool_scale, mixT_hi, mixT_lo, ident):
    with ExitStack() as ctx:
        sem = lambda n: nc.alloc_semaphore(f"mx_{n}")
        sb = lambda n, s: ctx.enter_context(nc.sbuf_tensor(f"mx_{n}", s, F32))
        ps = banks(nc, ctx, "mx_ps")
        inv = sb("inv", [P, 2, HEADS, HD])
        inv_ready, divided = sem("inv"), sem("divided")
        w, scale, scaled = sb("w", [P, NG, P]), sb("scale", [P, NG]), sb("scaled", [P, 8, HALF])
        w_in, pooled_done, scaled_ready = sem("w_in"), sem("pooled_done"), sem("scaled")
        hi_ready, lo_ready, turned, oT_hi, oT_lo = sem("hi"), sem("lo"), sem("turned"), sem("oT_hi"), sem("oT_lo")
        block = ctx.enter_context(nc.Block())
        at = lambda m, n: m[:, NG + n // 2, (n % 2) * HALF:(n % 2 + 1) * HALF]
        att = lambda m, tt: m[:, 0:4, tt * P:(tt + 1) * P]
        turned_ps = lambda tt: ps[:, tt, :].rearrange("p (k t) -> p k t", t=P)

        @block.sync
        def _(sp):
            sp.dma_start(w[:, :, :], pool_w.rearrange("g c d -> c g d")).then_inc(w_in, 16)
            sp.dma_start(scale[:, :], pool_scale).then_inc(w_in, 16)

        @block.tensor
        def _(pe):
            pe.wait_ge(w_in, 32)
            for n in range(8):
                pe.matmul(ps[:, n, :], w[:, n // 2, :], pooled[:, n // 2, (n % 2) * HALF:(n % 2 + 1) * HALF],
                          start=True, stop=True).then_inc(pooled_done, 1)
            for tt in range(NT):
                pe.wait_ge(scaled_ready, tt + 1)
                pe.wait_ge(inv_ready, tt + 1)
                for k in range(4):
                    ins = pe.transpose(ps[:, tt, k * P:(k + 1) * P],
                                       inv[:, tt % 2, 2 * k:2 * k + 2, :].rearrange("p h d -> p (h d)"), ident[:, :])
                ins.then_inc(turned, 1)

        @block.scalar
        def _(act):
            act.wait_ge(w_in, 32)
            for n in range(8):
                act.wait_ge(pooled_done, n + 1)
                act.activation(scaled[:, n, :], ps[:, n, :], ACT.Copy, scale=scale[:, n // 2:n // 2 + 1]).then_inc(scaled_ready, 1)
                act.wait_ge(scaled_ready, n + 1)
                act.activation(at(mixT_hi, n), scaled[:, n, :], ACT.Copy).then_inc(hi_ready, 1)
            for tt in range(NT):
                act.wait_ge(divided, tt + 1)
                act.activation(att(mixT_hi, tt), att(OT, tt), ACT.Copy).then_inc(oT_hi, 1)

        @block.vector
        def _(dve):
            for n in range(8):
                dve.wait_ge(hi_ready, n + 1)
                dve.tensor_tensor(at(mixT_lo, n), scaled[:, n, :], at(mixT_hi, n).bitcast(F32), ALU.subtract).then_inc(lo_ready, 1)
            def divide(tt):
                dve.wait_ge(turned, tt + 1)
                dve.tensor_tensor(att(OT, tt), att(OT, tt), turned_ps(tt), ALU.mult).then_inc(divided, 1)

            divide(0)
            for tt in range(NT):
                if tt + 1 < NT:
                    divide(tt + 1)
                dve.wait_ge(oT_hi, tt + 1)
                dve.tensor_tensor(att(mixT_lo, tt), att(OT, tt), att(mixT_hi, tt).bitcast(F32), ALU.subtract).then_inc(oT_lo, 1)

        @block.gpsimd
        def _(pool):
            for tt in range(NT):
                if tt >= 2:
                    pool.wait_ge(turned, tt - 1)
                pool.tensor_copy(inv[:, tt % 2, :, :], inv_sum[:, tt, :].unsqueeze(2).broadcast_to([P, HEADS, HD])).then_inc(inv_ready, 1)


def project_output(nc, w_out, mixT_hi, mixT_lo, X):
    with ExitStack() as ctx:
        sem = lambda n: nc.alloc_semaphore(f"po_{n}")
        ps = banks(nc, ctx, "po_ps")
        W = Weights(nc, ctx, "po_w")
        bank_done, added = sem("bank_done"), sem("added")
        block = ctx.enter_context(nc.Block())
        chunks = D // HALF

        @block.sync
        def _(sp):
            load_weights(sp, W, w_out, chunks)

        @block.scalar
        def _(act):
            with act.Fori(0, chunks) as c:
                split_hi(act, W, c)

        @block.vector
        def _(dve):
            dve.sem_inc(W.lo_ready, RING)

            def add_banks(c):
                for b in range(8):
                    wait_bank(dve, W, bank_done, c, b)
                    x = X[:, b, ds(c * HALF, HALF)]
                    dve.tensor_tensor(x, ps[:, b, :], x, ALU.add).then_inc(added, 1)

            split_lo(dve, W, 0, HEAD)
            with dve.Fori(0, chunks - 1) as c:
                split_lo(dve, W, c, REST)
                split_lo(dve, W, c + 1, HEAD)
                add_banks(c)
            split_lo(dve, W, chunks - 1, REST)
            add_banks(chunks - 1)

        @block.tensor
        def _(pe):
            pe.sem_inc(W.used, RING)
            pe.sem_inc(added, 8)
            with pe.Fori(0, chunks) as c:
                weight_chunk(pe, W, ps, c, lambda b: pe.wait_ge(added, 8 * c + b + 1), bank_done,
                             token_operands(W, mixT_hi, mixT_lo))


class EarlyTiles:

    def __init__(self, nc, ctx, name, u, hidden_dram, first, hT, ps, ident, u_raw, uT_f, uT_hi, uT_lo, hidden, u_in=None):
        sem = lambda n: nc.alloc_semaphore(f"{name}_{n}")
        self.u, self.hidden_dram, self.first, self.hT, self.ps, self.ident = u, hidden_dram, first, hT, ps, ident
        self.u_raw, self.uT_f, self.uT_hi, self.uT_lo, self.hidden = u_raw, uT_f, uT_hi, uT_lo, hidden
        self.u_in = u_in or [sem("u_in0"), sem("u_in1")]
        self.stored = [sem("stored0"), sem("stored1")]
        self.turned, self.copied, self.lo_ready = sem("turned"), sem("copied"), sem("lo_ready")
        self.hidden_done, self.gelu_done = sem("hidden_done"), sem("gelu_done")
        self.uT_ps = ps[:, 0:2, :].rearrange("p b (k e) -> p (b k) e", e=P)

    def load(self, sp, pair, s, landed=None):
        m = 2 * pair + s
        sp.wait_ge(self.turned, m + 1)
        sp.dma_start(self.u_raw[:, s, :], self.u[ds((m + self.first) * KEYS, KEYS), :]).then_inc(
            landed or self.u_in[s], 16)

    def credit_tensor(self, pe):
        pe.sem_inc(self.turned, 2)
        pe.sem_inc(self.copied, 2)
        pe.sem_inc(self.gelu_done, 2)

    def credit_sync(self, sp):
        for s in range(2):
            sp.sem_inc(self.stored[s], 16)

    def turn(self, pe, pair, s):
        m = 2 * pair + s
        pe.wait_ge(self.u_in[s], 16 * (pair + 1))
        pe.wait_ge(self.copied, 2 * m + 2)
        for k in range(KD):
            ins = pe.transpose(self.uT_ps[:, k, :], self.u_raw[:, s, k * P:(k + 1) * P], self.ident[:, :])
        ins.then_inc(self.turned, 1)

    def products(self, pe, pair, s, between=None):
        m = 2 * pair + s
        pe.wait_ge(self.lo_ready, m + 1)
        for half in range(2):
            pe.wait_ge(self.gelu_done, 2 * m + half + 1)
            t = slice(half * HALF, (half + 1) * HALF)
            for k in range(KD):
                ins = product3(pe, self.ps[:, 2 + half, :], (self.uT_hi[:, s, k, :], self.uT_lo[:, s, k, :]),
                               (self.hT[0][:, k, t], self.hT[1][:, k, t]), k == 0, k == KD - 1)
                if k == KD - 1:
                    ins.then_inc(self.hidden_done, 1)
                if between is not None:
                    between(half * KD + k)

    def copy(self, act, pair, s):
        m = 2 * pair + s
        act.wait_ge(self.turned, m + 1 + 2)
        act.activation(self.uT_f[:, s, :, :], self.uT_ps, ACT.Copy).then_inc(self.copied, 1)
        act.activation(self.uT_hi[:, s, :, :], self.uT_ps, ACT.Copy).then_inc(self.copied, 1)

    def gelu(self, act, pair, s, half):
        m = 2 * pair + s
        act.wait_ge(self.hidden_done, 2 * m + half + 1)
        if half == 0:
            act.wait_ge(self.stored[s], 16 * (pair + 1))
        act.activation(self.hidden[:, s, half * HALF:(half + 1) * HALF], self.ps[:, 2 + half, :],
                       ACT.Gelu).then_inc(self.gelu_done, 1)

    def store(self, act, pair, s):
        m = 2 * pair + s
        act.wait_ge(self.gelu_done, 2 * m + 2 + 2)
        act.dma_start(self.hidden_dram[ds(m + self.first, 1), :, :].rearrange("a j t -> (a j) t"),
                      self.hidden[:, s, :]).then_inc(self.stored[s], 16)

    def split(self, pool, pair, s):
        m = 2 * pair + s
        pool.wait_ge(self.copied, 2 * m + 2 + 2)
        pool.tensor_tensor(self.uT_lo[:, s, :, :], self.uT_f[:, s, :, :], self.uT_hi[:, s, :, :].bitcast(F32),
                           ALU.subtract).then_inc(self.lo_ready, 1)

    def finish(self, eng, pairs):
        for s in range(2):
            eng.wait_ge(self.stored[s], 16 * (pairs + 1))


def retrieve(nc, w_query, sub_keys, hT_hi, hT_lo, W, scores, picks, iota, iota_in, raw_keys, keys_in, ident, u,
             hidden_dram, early_pairs, picksT, gate_rest, next_u_in):
    HC = 2
    CHUNKS = PH // HC
    LISTS = NT * HC
    with ExitStack() as ctx:
        sem = lambda n: nc.alloc_semaphore(f"rt_{n}")
        sb = lambda n, s, dt=F32: ctx.enter_context(nc.sbuf_tensor(f"rt_{n}", s, dt))
        ps = banks(nc, ctx, "rt_ps")
        queryT, keysT = sb("queryT", [P, 2 * HC, T]), sb("keysT", [P, 2 * PH, KEYS])
        top, top_i = sb("top", [P, NT, 2 * HC, TOPK]), sb("top_i", [P, NT, 2 * HC, TOPK], U32)
        best, best_i = sb("best", [P, NT, HC, TOPK]), sb("best_i", [P, NT, HC, TOPK], U32)
        rest, cand = sb("rest", [P, 2 * HC, KEYS]), sb("cand", [P, 2, HC, TOPK * TOPK])
        rest2 = sb("rest2", [P, HC, TOPK * TOPK])
        match = raw_keys[:, :, :].rearrange("p a b -> p (a b)").rearrange("p (l q a) -> p l q a", q=TOPK, a=TOPK)
        ab, ab_i = sb("ab", [P, 2, NT, HC, TOPK]), sb("ab_i", [P, 2, NT, HC, TOPK], U32)
        topf, total = sb("topf", [P, NT, 2 * HC, TOPK]), sb("total", [P, 2, NT, PH])
        early = EarlyTiles(nc, ctx, "re", u, hidden_dram, 0, (hT_hi, hT_lo), ps, ident,
                           W.raw[:, :, :].rearrange("p (s a) n -> p s (a n)", s=2),
                           queryT[:, 0:2, :].rearrange("p s (k e) -> p s k e", e=P),
                           W.hi[:, :, :].rearrange("p (s a) (k e) -> p s (a k) e", s=2, e=P),
                           W.lo[:, :, :].rearrange("p (s a) (k e) -> p s (a k) e", s=2, e=P), queryT[:, 2:4, :])
        bank_done, keys_turned, keys_ready = sem("bank_done"), sem("keys_turned"), sem("keys")
        query_ready, scored, scores_ready = sem("query"), sem("scored"), sem("scores_r")
        scores_free, passed = sem("scores_free"), sem("passed")
        dec, shifted, exped, normed = sem("decode"), sem("shifted"), sem("exped"), sem("normed")
        picks_turned, gate_step = sem("picks_turned"), sem("gate_step")
        picks_ps = lambda a: ps[:, (6, 4, 4)[a]:(6, 4, 4)[a] + 2, :].rearrange("p b t -> p (b t)")
        block = ctx.enter_context(nc.Block())

        @block.sync
        def _(sp):
            load_weights(sp, W, w_query, CHUNKS, RING)
            early.credit_sync(sp)
            sp.wait_ge(W.lo_ready, RING + CHUNKS * KD)
            with sp.Fori(0, early_pairs) as pair:
                for s in range(2):
                    early.load(sp, pair, s)
            for s in range(2):
                early.load(sp, early_pairs, s, next_u_in[s])

        @block.tensor
        def _(pe):
            pe.wait_ge(keys_in, 16)
            for n in range(2 * PH // 4):
                for g in range(4):
                    ins = pe.transpose(ps[:, n, g * P:(g + 1) * P], raw_keys[:, 4 * n + g, :], ident[:, :])
                ins.then_inc(keys_turned, 1)
            pe.wait_ge(keys_ready, 4)
            pe.sem_inc(W.used, RING)
            pe.sem_inc(scores_ready, 8)
            with pe.Fori(0, CHUNKS) as c:
                weight_chunk(pe, W, ps, c, lambda b: pe.wait_ge(scores_ready, 8 * c + b + 1), bank_done,
                             channel_operands(W, hT_hi, hT_lo))
                for tt in range(NT):
                    pe.wait_ge(query_ready, 8 * c + max(4 * (tt // 4) + 4, tt + 1))
                    for g in range(2 * HC):
                        ins = pe.matmul(ps[:, tt, g * KEYS:(g + 1) * KEYS], queryT[:, g, tt * P:(tt + 1) * P],
                                        keysT[:, ds(c * 2 * HC + g, 1), :].rearrange("p a n -> p (a n)"),
                                        start=True, stop=True)
                    ins.then_inc(scored, 1)
            pe.wait_ge(scores_ready, 8 * (CHUNKS + 1))
            early.credit_tensor(pe)
            early.turn(pe, 0, 0)
            with pe.Fori(0, early_pairs - 1) as pair:
                early.turn(pe, pair, 1)
                early.products(pe, pair, 0)
                early.turn(pe, pair + 1, 0)
                early.products(pe, pair, 1)
            early.turn(pe, early_pairs - 1, 1)

            def turn_picks(a):
                for tt in range(NT):
                    ins = pe.transpose(picks_ps(a)[:, tt * P:(tt + 1) * P], picks[:, tt, a, :], ident[:, :])
                ins.then_inc(picks_turned, 1)

            pe.wait_ge(normed, 3)
            turn_picks(2)
            turn_picks(0)
            early.products(pe, early_pairs - 1, 0)
            pe.wait_ge(gate_step, 2)
            turn_picks(1)
            early.products(pe, early_pairs - 1, 1)

        @block.scalar
        def _(act):
            for n in range(2 * PH // 4):
                act.wait_ge(keys_turned, n + 1)
                act.activation(keysT[:, 4 * n:4 * n + 4, :], ps[:, n, :].rearrange("p (g c) -> p g c", c=P),
                               ACT.Copy).then_inc(keys_ready, 1)

            def chunk(c, buffer, last=False):
                split_hi(act, W, c, REST)
                if not last:
                    split_hi(act, W, c + 1, HEAD)
                for b in range(8):
                    wait_bank(act, W, bank_done, c, b)
                    act.activation(queryT[:, b % 4, (b // 4) * HALF:(b // 4 + 1) * HALF], ps[:, b, :],
                                   ACT.Copy).then_inc(query_ready, 1)
                for tt in range(NT):
                    act.wait_ge(scored, 8 * c + tt + 1)
                    act.wait_ge(scores_free, 8 * c + tt + 1)
                    act.activation(scores[:, buffer, tt, :, :], ps[:, tt, :].rearrange("p (g n) -> p g n", n=KEYS),
                                   ACT.Copy).then_inc(scores_ready, 1)

            split_hi(act, W, 0, HEAD)
            with act.Fori(0, CHUNKS // 2 - 1) as cc:
                chunk(2 * cc, 0)
                chunk(2 * cc + 1, 1)
            chunk(CHUNKS - 2, 0)
            chunk(CHUNKS - 1, 1, last=True)

            def tile(pair, s):
                for half in range(2):
                    early.gelu(act, pair, s, half)
                early.store(act, pair, s)

            def two_tiles(pair):
                early.copy(act, pair, 1)
                tile(pair, 0)
                early.copy(act, pair + 1, 0)
                tile(pair, 1)

            early.copy(act, 0, 0)
            with act.Fori(0, early_pairs - 2) as pair:
                two_tiles(pair)
            act.wait_ge(shifted, CHUNKS)
            act.activation(picks[:, :, 2, :], picks[:, :, 2, :], ACT.Exp).then_inc(exped, 1)
            two_tiles(early_pairs - 2)
            early.copy(act, early_pairs - 1, 1)
            for s in range(2):
                act.wait_ge(picks_turned, 2 + s)
                act.activation(picksT[:, s, :], picks_ps(s), ACT.Copy)
                tile(early_pairs - 1, s)
            early.finish(act, early_pairs)

        @block.gpsimd
        def _(pool):
            pool.sem_inc(W.lo_ready, RING)
            with pool.Fori(0, CHUNKS) as c:
                split_lo(pool, W, c)
            with pool.Fori(0, early_pairs) as pair:
                for s in range(2):
                    early.split(pool, pair, s)

        @block.vector
        def _(dve):
            dve.sem_inc(scores_free, 2 * NT)
            dve.wait_ge(iota_in, 16)

            def search_keys(c, buffer, tt):
                hold(dve, scores_ready, 8 * c + tt + 1 + 8, passed)
                s = scores[:, buffer, tt, :, :]
                for g in range(4):
                    dve.max(top[:, tt, g, 0:8], s[:, g, :])
                dve.drain()
                for g in range(4):
                    dve.match_replace(rest[:, g, :], top[:, tt, g, 0:8], s[:, g, :], LOWEST)
                for g in range(4):
                    ins = dve.max_index(top_i[:, tt, g, 0:8], top[:, tt, g, 0:8], s[:, g, :])
                ins.then_inc(scores_free, 1)
                dve.drain()
                for g in range(4):
                    dve.max(top[:, tt, g, 8:16], rest[:, g, :])
                dve.drain()
                for g in range(4):
                    dve.max_index(top_i[:, tt, g, 8:16], top[:, tt, g, 8:16], rest[:, g, :])

            def search_pairs(tt):
                sums = cand[:, tt % 2, :, :]
                for h in range(HC):
                    dve.tensor_tensor(sums[:, h, :].rearrange("p (a b) -> p a b", b=TOPK),
                                      top[:, tt, 2 * h, :].unsqueeze(2).broadcast_to([P, TOPK, TOPK]),
                                      top[:, tt, 2 * h + 1, :].unsqueeze(1).broadcast_to([P, TOPK, TOPK]), ALU.add)
                dve.drain()
                for h in range(HC):
                    dve.max(best[:, tt, h, 0:8], sums[:, h, :])
                dve.drain()
                for h in range(HC):
                    dve.match_replace(rest2[:, h, :], best[:, tt, h, 0:8], sums[:, h, :], LOWEST)
                for h in range(HC):
                    dve.max_index(best_i[:, tt, h, 0:8], best[:, tt, h, 0:8], sums[:, h, :])
                dve.drain()
                for h in range(HC):
                    dve.max(best[:, tt, h, 8:16], rest2[:, h, :])
                dve.drain()
                for h in range(HC):
                    dve.max_index(best_i[:, tt, h, 8:16], best[:, tt, h, 8:16], rest2[:, h, :])

            STEPS = 4 + 2 * (2 * 3)

            def decode(c):
                count = 0

                def step(ins):
                    nonlocal count
                    count += 1
                    ins.then_inc(dec, 1)
                    dve.wait_ge(dec, STEPS * c + count)

                dve.drain()
                dve.tensor_tensor(picks[:, :, 2, ds(c * HC * TOPK, HC * TOPK)].rearrange("p t (h r) -> p t h r", r=TOPK),
                                  best[:, :, :, :],
                                  best[:, :, :, 0:1].broadcast_to([P, NT, HC, TOPK]), ALU.subtract).then_inc(shifted, 1)
                step(dve.tensor_scalar(ab_i[:, 0], best_i[:, :, :, :], 4, None, ALU.logical_shift_right))
                step(dve.tensor_scalar(ab_i[:, 1], best_i[:, :, :, :], TOPK - 1, None, ALU.bitwise_and))
                step(dve.tensor_copy(ab[:, :, :, :, :].rearrange("p a t h r -> p (a t h r)"),
                                     ab_i[:, :, :, :, :].rearrange("p a t h r -> p (a t h r)")))
                step(dve.tensor_copy(topf[:, :, :, :], top_i[:, :, :, :]))
                for part in range(2):
                    for half in range(2):
                        tts = slice(half * NT // 2, (half + 1) * NT // 2)
                        position = ab[:, part, tts, :, :].rearrange("p t h r -> p (t h) r")
                        step(dve.tensor_tensor(match[:, :, :, :], position.unsqueeze(3).broadcast_to([P, LISTS // 2, TOPK, TOPK]),
                                               iota[:, 0:TOPK].unsqueeze(1).unsqueeze(1).broadcast_to([P, LISTS // 2, TOPK, TOPK]),
                                               ALU.is_equal))
                        lists = topf[:, tts, :, :].rearrange("p t (h q) a -> p (t h) q a", q=2)[:, :, part, :]
                        step(dve.tensor_tensor(match[:, :, :, :], match[:, :, :, :],
                                               lists.unsqueeze(2).broadcast_to([P, LISTS // 2, TOPK, TOPK]), ALU.mult))
                        out = picks[:, tts, part, ds(c * HC * TOPK, HC * TOPK)].rearrange("p t (h r) -> p t h r", r=TOPK)
                        step(dve.tensor_reduce(out, match[:, :, :, :].rearrange("p (t h) r a -> p t h r a", h=HC), AX.X, ALU.add))
                assert count == STEPS

            with dve.Fori(0, CHUNKS // 2) as cc:
                for half in range(2):
                    c = 2 * cc + half
                    for tt in range(NT):
                        search_keys(c, half, tt)
                        search_pairs(tt)
                    decode(c)
            gates = picks[:, :, 2, :].rearrange("p t (h r) -> p t h r", r=TOPK)
            dve.wait_ge(exped, 1)
            dve.tensor_reduce(total[:, 0, :, :], gates, AX.X, ALU.add).then_inc(normed, 1)
            dve.wait_ge(normed, 1)
            dve.reciprocal(total[:, 1, :, :], total[:, 0, :, :]).then_inc(normed, 1)
            dve.wait_ge(normed, 2)
            dve.tensor_tensor(gates, gates, total[:, 1, :, :].unsqueeze(3).broadcast_to([P, NT, PH, TOPK]),
                              ALU.mult).then_inc(normed, 1)
            dve.wait_ge(picks_turned, 1)
            count, source = 0, picks_ps(2)
            for part in range(3):
                dve.tensor_copy(picksT[:, 2 + part, :], source).then_inc(gate_step, 1)
                count += 1
                dve.wait_ge(gate_step, count)
                if part < 2:
                    dve.tensor_tensor(gate_rest[:, part, :], source, picksT[:, 2 + part, :], ALU.subtract).then_inc(gate_step, 1)
                    count += 1
                    dve.wait_ge(gate_step, count)
                    source = gate_rest[:, part, :]


def spread_gates(nc, ctx, picksT, iota, ident, gates, W, X, hT, u, hidden_dram, first, early_pairs, last_part,
                 written, u_in, late_u_in):
    BATCH = 4
    HOTS = 8
    PART = 64
    SLOTS = 4
    BATCHES = PART // BATCH
    PER_TILE = 8
    assert T // PART == early_pairs and BATCHES == 2 * PER_TILE
    sem = lambda n: nc.alloc_semaphore(f"sg_{n}")
    sb = lambda n, s, dt=F32: ctx.enter_context(nc.sbuf_tensor(f"sg_{n}", s, dt))
    ps = banks(nc, ctx, "sg_ps")
    flat = X[:, :, :].rearrange("p n d -> p (n d)")
    slots = lambda a: flat[:, a * 2 * D:(a + 1) * 2 * D].rearrange("p (s d) -> p s d", s=2)
    early = EarlyTiles(nc, ctx, "se", u, hidden_dram, first, hT, ps, ident,
                       W.raw[:, :, :].rearrange("p (s a) n -> p s (a n)", s=2),
                       slots(0).rearrange("p s (k e) -> p s k e", e=P),
                       W.hi[:, :, :].rearrange("p (s a) (k e) -> p s (a k) e", s=2, e=P),
                       W.lo[:, :, :].rearrange("p (s a) (k e) -> p s (a k) e", s=2, e=P), slots(1), u_in)
    keys = sb("keys", [P, KEYS, HOTS], BF16)
    rows, column_hot = sb("rows", [P, 2, KEYS, HOTS], BF16), sb("columns", [P, 2, KEYS, HOTS], BF16)
    row_gates = sb("row_gates", [P, 2, 3, KEYS, HOTS], BF16)
    part = [sb("part", [P, KEYS, PART])[:, :, :],
            last_part[:, :, :].rearrange("p a n -> p (a n)").rearrange("p (i t) -> p i t", t=PART)]
    keys_ready, rows_ready, hots_ready = sem("keys"), sem("rows_r"), sem("hots")
    spread, copied = sem("spread"), sem("copied")
    block = ctx.enter_context(nc.Block())

    @block.tensor
    def _(pe):
        pe.sem_inc(copied, SLOTS)
        early.credit_tensor(pe)

        def batch(part_i, j):
            n = part_i * BATCHES + j
            slot = j * BATCH // HOTS % 2
            if j * BATCH % HOTS == 0:
                pe.wait_ge(hots_ready, part_i * (PART // HOTS) + j * BATCH // HOTS + 1)
            pe.wait_ge(copied, n + 1)
            for q in range(BATCH):
                t = j * BATCH % HOTS + q
                for gate in range(3):
                    ins = pe.matmul(ps[:, 4 + j % SLOTS, q * KEYS:(q + 1) * KEYS], column_hot[:, slot, :, t],
                                    row_gates[:, slot, gate, :, t], start=gate == 0, stop=gate == 2)
            ins.then_inc(spread, 1)

        def between(pair, s):
            return lambda step: step % 2 and batch(pair, s * PER_TILE + step // 2)

        early.turn(pe, 0, 0)
        with pe.Fori(0, early_pairs - 1) as pair:
            early.turn(pe, pair, 1)
            early.products(pe, pair, 0, between(pair, 0))
            early.turn(pe, pair + 1, 0)
            early.products(pe, pair, 1, between(pair, 1))
        early.turn(pe, early_pairs - 1, 1)
        early.products(pe, early_pairs - 1, 0, lambda step: batch(early_pairs - 1, step))
        early.products(pe, early_pairs - 1, 1)

    @block.vector
    def _(dve):
        PER_HOTS = HOTS // BATCH
        dve.tensor_copy(keys[:, :, :], iota[:, :].unsqueeze(2).broadcast_to([P, KEYS, HOTS])).then_inc(keys_ready, 1)
        dve.sem_inc(spread, 2 * PER_HOTS)
        dve.wait_ge(keys_ready, 1)
        with dve.Fori(0, early_pairs) as pair:
            for m in range(PART // HOTS):
                n, slot = pair * (PART // HOTS) + m, m % 2
                of = lambda a: picksT[:, a, ds(n * HOTS, HOTS)].unsqueeze(1).broadcast_to([P, KEYS, HOTS])
                dve.wait_ge(spread, PER_HOTS * (n + 1))
                dve.tensor_tensor(rows[:, slot, :, :], keys[:, :, :], of(0), ALU.is_equal).then_inc(rows_ready, 1)
                dve.tensor_tensor(column_hot[:, slot, :, :], keys[:, :, :], of(1), ALU.is_equal)
                dve.wait_ge(rows_ready, n + 1)
                for gate in range(3):
                    ins = dve.tensor_tensor(row_gates[:, slot, gate, :, :], rows[:, slot, :, :], of(2 + gate), ALU.mult)
                ins.then_inc(hots_ready, 1)

    @block.gpsimd
    def _(pool):
        with pool.Fori(0, early_pairs) as pair:
            for s in range(2):
                early.split(pool, pair, s)

    @block.scalar
    def _(act):
        def copy_out(pair, b, j):
            n = pair * BATCHES + j
            act.wait_ge(spread, n + 1 + 2 * HOTS // BATCH)
            act.activation(part[b][:, :, j * BATCH:(j + 1) * BATCH],
                           ps[:, 4 + j % SLOTS, :].rearrange("p (t i) -> p i t", i=KEYS), ACT.Copy).then_inc(copied, 1)

        def tile(pair, b, s, batches):
            for half in range(2):
                for j in range(batches // 2):
                    copy_out(pair, b, s * PER_TILE + half * batches // 2 + j)
                early.gelu(act, pair, s, half)
            early.store(act, pair, s)

        def both(two, b, last=False):
            pair = 2 * two + b
            act.wait_ge(written[b], 16 * two + 16)
            early.copy(act, pair, 1)
            tile(pair, b, 0, BATCHES if last else PER_TILE)
            if not last:
                early.copy(act, pair + 1, 0)
            tile(pair, b, 1, 0 if last else PER_TILE)

        early.copy(act, 0, 0)
        with act.Fori(0, early_pairs // 2 - 1) as two:
            both(two, 0)
            both(two, 1)
        both(early_pairs // 2 - 1, 0)
        both(early_pairs // 2 - 1, 1, last=True)

    @block.sync
    def _(sp):
        early.credit_sync(sp)
        for b in range(2):
            sp.sem_inc(written[b], 16)

        def store_part(n, b):
            sp.wait_ge(copied, SLOTS + (n + 1) * BATCHES)
            sp.dma_start(gates[ds(n, 1), :, :, :].rearrange("q j i t -> (q j) i t"), part[b]).then_inc(written[b], 16)

        with sp.Fori(0, early_pairs // 2 - 1) as two:
            for b in range(2):
                n = 2 * two + b
                for s in range(2):
                    early.load(sp, n + 1, s)
                store_part(n, b)
        for s in range(2):
            early.load(sp, early_pairs - 1, s)
        store_part(early_pairs - 2, 0)
        early.load(sp, early_pairs, 0, late_u_in[0])
        store_part(early_pairs - 1, 1)
        early.load(sp, early_pairs, 1, late_u_in[1])
        sp.wait_ge(written[0], 16 + 16 * (early_pairs // 2))
    return early.stored


def gates_of(gates, i):
    return gates[:, :, ds(i, 1), :].rearrange("q j i t -> j q (i t)")


def mix_late_experts(nc, u, v, gates, hT, x_spill, X, ident, first, W, part_written, u_in, hidden_stored, spread_pairs,
                     hidden_dram, ee_raw, ee_in):
    G = 2
    TILES = KEYS - first
    GROUPS = TILES // G
    UNITS = 16
    OUT_BANKS = 4
    with ExitStack() as ctx:
        sem = lambda n: nc.alloc_semaphore(f"me_{n}")
        sb = lambda n, s, dt=F32: ctx.enter_context(nc.sbuf_tensor(f"me_{n}", s, dt))
        ps = banks(nc, ctx, "me_ps")
        v_raw, gate = sb("v_raw", [P, G, D]), sb("gate", [P, G, T])
        u_raw = W.raw[:, :, :].rearrange("p (s a) n -> p s (a n)", s=2)
        uT_hi, uT_lo = (w[:, :, :].rearrange("p (s a) (k e) -> p s (a k) e", s=2, e=P) for w in (W.hi, W.lo))
        v_hi, v_lo = sb("v_hi", [P, G, D], F32R), sb("v_lo", [P, G, D], F32R)
        act_hi, act_lo = sb("act_hi", [P, G, T], F32R), sb("act_lo", [P, G, T], F32R)
        hidden = sb("hidden", [P, 2, HALF])
        x_in = sem("x_in")
        v_in, gate_in = ([sem(f"{n}{b}") for b in range(G)] for n in ("v_in", "gate_in"))
        u_turned, uT_hi_ready, uT_lo_ready = sem("u_turned"), sem("uT_hi_r"), sem("uT_lo_r")
        v_hi_ready, v_lo_ready = sem("v_hi_r"), sem("v_lo_r")
        hidden_done, gelu_done, gated = sem("hidden_done"), sem("gelu"), sem("gated")
        act_hi_ready, act_lo_ready = sem("act_hi_r"), sem("act_lo_r")
        unit_done, added = sem("unit_done"), sem("added")
        block = ctx.enter_context(nc.Block())
        uT_ps = ps[:, 0:2, :].rearrange("p b (k e) -> p (b k) e", e=P)

        @block.sync
        def _(sp):
            tile = lambda w, n: w[ds((n + first) * KEYS, KEYS), :]

            def load_u(n, b):
                sp.wait_ge(u_turned, n - 1)
                sp.dma_start(u_raw[:, b, :], tile(u, n)).then_inc(u_in[b], 16)

            def load_gate(n, b, reused=True):
                if reused:
                    sp.wait_ge(gated, 2 * (n - 1))
                sp.dma_start(gate[:, b, :].rearrange("j (q t) -> j q t", t=gates.shape[3]),
                             gates_of(gates, n + first)).then_inc(gate_in[b], 16)

            def load_v(n, b, reused=True):
                if reused:
                    sp.wait_ge(v_lo_ready, n - 1)
                sp.dma_start(v_raw[:, b, :], tile(v, n)).then_inc(v_in[b], 16)

            for b in range(G):
                load_v(b, b, False)
            sp.wait_ge(part_written[1], 16 + 16 * (spread_pairs // 2))
            for b in range(G):
                load_gate(b, b, False)
            for b in range(G):
                load_u(G + b, b)
            for b in range(G):
                sp.wait_ge(hidden_stored[b], 16 * (spread_pairs + 1))
            sp.dma_start(X[:, :, :], x_spill.rearrange("(n p) d -> p n d", p=P)).then_inc(x_in, 16)
            for b in range(G):
                load_gate(G + b, b)
                load_v(G + b, b)
            with sp.Fori(2, GROUPS) as g:
                for b in range(G):
                    load_u(g * G + b, b)
                    load_gate(g * G + b, b)
                    load_v(g * G + b, b)
            for b in range(G):
                load_early(sp, ee_raw, ee_in, v, gates, hidden_dram, b, b)

        @block.tensor
        def _(pe):
            def turn(n, g, b):
                pe.wait_ge(u_in[b], 16 * (g + 1))
                pe.wait_ge(uT_lo_ready, n + 1)
                for k in range(KD):
                    ins = pe.transpose(uT_ps[:, k, :], u_raw[:, b, k * P:(k + 1) * P], ident[:, :])
                ins.then_inc(u_turned, 1)

            def hidden_products(n, b):
                pe.wait_ge(uT_lo_ready, n + 2)
                for half in range(2):
                    pe.wait_ge(gelu_done, 2 * n + half + 1)
                    t = slice(half * HALF, (half + 1) * HALF)
                    for k in range(KD):
                        ins = product3(pe, ps[:, 2 + half, :], (uT_hi[:, b, k, :], uT_lo[:, b, k, :]),
                                       (hT[0][:, k, t], hT[1][:, k, t]), k == 0, k == KD - 1)
                    ins.then_inc(hidden_done, 1)

            def output_part(g, unit, b):
                tt, d = unit // 2, slice((unit % 2) * HALF, (unit % 2 + 1) * HALF)
                return product3(pe, ps[:, 4 + unit % OUT_BANKS, :],
                                (act_hi[:, b, tt * P:(tt + 1) * P], act_lo[:, b, tt * P:(tt + 1) * P]),
                                (v_hi[:, b, d], v_lo[:, b, d]), b == 0, b == G - 1)

            def outputs(g):
                pe.wait_ge(v_lo_ready, g * G + 1)
                pe.wait_ge(act_lo_ready, 2 * (g * G) + 2 + 2)
                for unit in range(OUT_BANKS):
                    pe.wait_ge(added, UNITS * g + unit + 1)
                    output_part(g, unit, 0)
                pe.wait_ge(v_lo_ready, g * G + 2)
                for unit in range(UNITS):
                    if unit % 8 == 0:
                        pe.wait_ge(act_lo_ready, 2 * (g * G + 1) + unit // 8 + 1 + 2)
                    if unit >= OUT_BANKS:
                        pe.wait_ge(added, UNITS * g + unit + 1)
                        output_part(g, unit, 0)
                    output_part(g, unit, 1).then_inc(unit_done, 1)

            def group(g, last):
                turn(g * G + 1, g, 1)
                hidden_products(g * G, 0)
                if not last:
                    turn(g * G + 2, g + 1, 0)
                hidden_products(g * G + 1, 1)
                outputs(g)

            pe.sem_inc(uT_lo_ready, 1)
            pe.sem_inc(gelu_done, 2)
            pe.sem_inc(added, OUT_BANKS)
            pe.sem_inc(unit_done, UNITS)
            turn(0, 0, 0)
            with pe.Fori(0, GROUPS - 1) as g:
                group(g, False)
            group(GROUPS - 1, True)

        @block.scalar
        def _(act):
            copy = lambda o, i: act.activation(o, i, ACT.Copy)

            def u_hi(n, b):
                act.wait_ge(u_turned, n + 1)
                copy(uT_hi[:, b, :, :], uT_ps).then_inc(uT_hi_ready, 1)

            def tile(g, b):
                n = g * G + b
                act.wait_ge(v_in[b], 16 * (g + 1))
                act.wait_ge(unit_done, UNITS * (g + 1))
                copy(v_hi[:, b, :], v_raw[:, b, :]).then_inc(v_hi_ready, 1)
                for half in range(2):
                    t = slice(half * HALF, (half + 1) * HALF)
                    act.wait_ge(hidden_done, 2 * n + half + 1)
                    act.wait_ge(act_lo_ready, 2 * n + half + 1)
                    act.activation(hidden[:, half, :], ps[:, 2 + half, :], ACT.Gelu).then_inc(gelu_done, 1)
                    act.wait_ge(gated, 2 * n + half + 1)
                    copy(act_hi[:, b, t], hidden[:, half, :]).then_inc(act_hi_ready, 1)

            u_hi(0, 0)
            with act.Fori(0, GROUPS - 1) as g:
                u_hi(g * G + 1, 1)
                tile(g, 0)
                u_hi(g * G + 2, 0)
                tile(g, 1)
            u_hi(TILES - 1, 1)
            tile(GROUPS - 1, 0)
            tile(GROUPS - 1, 1)

        @block.vector
        def _(dve):
            def u_lo(n, b):
                dve.wait_ge(uT_hi_ready, n + 1)
                dve.tensor_tensor(uT_lo[:, b, :, :], uT_ps, uT_hi[:, b, :, :].bitcast(F32), ALU.subtract).then_inc(uT_lo_ready, 1)

            def tile(g, b):
                n = g * G + b
                dve.wait_ge(v_hi_ready, n + 1)
                dve.tensor_tensor(v_lo[:, b, :], v_raw[:, b, :], v_hi[:, b, :].bitcast(F32), ALU.subtract).then_inc(v_lo_ready, 1)
                for half in range(2):
                    t = slice(half * HALF, (half + 1) * HALF)
                    if half == 0:
                        dve.wait_ge(gate_in[b], 16 * (g + 1))
                    dve.wait_ge(gelu_done, 2 * n + half + 1 + 2)
                    dve.tensor_tensor(hidden[:, half, :], hidden[:, half, :], gate[:, b, t], ALU.mult).then_inc(gated, 1)
                    dve.wait_ge(act_hi_ready, 2 * n + half + 1)
                    dve.tensor_tensor(act_lo[:, b, t], hidden[:, half, :], act_hi[:, b, t].bitcast(F32),
                                      ALU.subtract).then_inc(act_lo_ready, 1)

            def add_outputs(g):
                dve.wait_ge(x_in, 16)
                for unit in range(UNITS):
                    dve.wait_ge(unit_done, UNITS * (g + 1) + unit + 1)
                    x = X[:, unit // 2, (unit % 2) * HALF:(unit % 2 + 1) * HALF]
                    dve.tensor_tensor(x, ps[:, 4 + unit % OUT_BANKS, :], x, ALU.add).then_inc(added, 1)

            dve.sem_inc(act_lo_ready, 2)
            u_lo(0, 0)
            with dve.Fori(0, GROUPS - 1) as g:
                u_lo(g * G + 1, 1)
                tile(g, 0)
                u_lo(g * G + 2, 0)
                tile(g, 1)
                add_outputs(g)
            u_lo(TILES - 1, 1)
            tile(GROUPS - 1, 0)
            tile(GROUPS - 1, 1)
            add_outputs(GROUPS - 1)


def load_early(sp, raw, landed, v, gates, hidden_dram, n, b):
    sp.dma_start(raw[:, 0, b, :], hidden_dram[ds(n, 1), :, :].rearrange("a j t -> (a j) t")).then_inc(landed[b], 16)
    sp.dma_start(raw[:, 1, b, :].rearrange("j (q t) -> j q t", t=gates.shape[3]), gates_of(gates, n)).then_inc(landed[b], 16)
    sp.dma_start(raw[:, 2, b, :], v[ds(n * KEYS, KEYS), :]).then_inc(landed[b], 16)


def mix_early_experts(nc, v, gates, hidden_dram, hT, X, out, tiles, raw, landed):
    G = 2
    GROUPS = tiles // G
    UNITS = 16
    OUT_BANKS = 8
    with ExitStack() as ctx:
        sem = lambda n: nc.alloc_semaphore(f"ee_{n}")
        sb = lambda n, s, dt=F32: ctx.enter_context(nc.sbuf_tensor(f"ee_{n}", s, dt))
        ps = banks(nc, ctx, "ee_ps")
        hidden, gate, v_raw = (raw[:, a, :, :] for a in range(3))
        act_hi, act_lo = (h[:, 0:4, :].rearrange("p (s g) t -> p s g t", s=2) for h in hT)
        v_hi, v_lo = (h[:, 4:8, :].rearrange("p (s g) t -> p s g t", s=2) for h in hT)
        v_hi_ready, v_lo_ready, gated = sem("v_hi_r"), sem("v_lo_r"), sem("gated")
        act_hi_ready, act_lo_ready = sem("act_hi_r"), sem("act_lo_r")
        unit_done, added, stored = sem("unit_done"), sem("added"), sem("stored")
        block = ctx.enter_context(nc.Block())

        @block.sync
        def _(sp):
            with sp.Fori(1, GROUPS) as g:
                for b in range(G):
                    n = g * G + b
                    sp.wait_ge(act_lo_ready, n - 1)
                    load_early(sp, raw, landed, v, gates, hidden_dram, n, b)
            for tt in range(NT):
                sp.wait_ge(added, OUT_BANKS + UNITS * (GROUPS - 1) + 2 * tt + 2)
                sp.dma_start(out[tt * P:(tt + 1) * P, :], X[:, tt, :]).then_inc(stored, 16)
            sp.wait_ge(stored, 16 * NT)

        @block.tensor
        def _(pe):
            pe.sem_inc(unit_done, 2 * UNITS)
            pe.sem_inc(added, OUT_BANKS)
            with pe.Fori(0, GROUPS // 2) as two:
                for slot in range(2):
                    g = 2 * two + slot
                    pe.wait_ge(act_lo_ready, G * (g + 1))
                    pe.wait_ge(v_lo_ready, G * (g + 1))
                    for unit in range(UNITS):
                        tt, d = unit // 2, slice((unit % 2) * HALF, (unit % 2 + 1) * HALF)
                        pe.wait_ge(added, UNITS * g + unit + 1)
                        for b in range(G):
                            ins = product3(pe, ps[:, unit % OUT_BANKS, :],
                                           (act_hi[:, slot, b, tt * P:(tt + 1) * P], act_lo[:, slot, b, tt * P:(tt + 1) * P]),
                                           (v_hi[:, slot, b, d], v_lo[:, slot, b, d]), b == 0, b == G - 1)
                        ins.then_inc(unit_done, 1)

        @block.scalar
        def _(act):
            with act.Fori(0, GROUPS // 2) as two:
                for slot in range(2):
                    g = 2 * two + slot
                    for b in range(G):
                        act.wait_ge(landed[b], 48 * (g + 1))
                        act.wait_ge(unit_done, UNITS * (g + 1))
                        act.activation(v_hi[:, slot, b, :], v_raw[:, b, :], ACT.Copy).then_inc(v_hi_ready, 1)
                        act.wait_ge(gated, G * g + b + 1)
                        act.activation(act_hi[:, slot, b, :], hidden[:, b, :], ACT.Copy).then_inc(act_hi_ready, 1)

        @block.vector
        def _(dve):
            def prepare(g, slot):
                for b in range(G):
                    n = G * g + b
                    dve.wait_ge(landed[b], 48 * (g + 1))
                    dve.tensor_tensor(hidden[:, b, :], hidden[:, b, :], gate[:, b, :], ALU.mult).then_inc(gated, 1)
                    dve.wait_ge(v_hi_ready, n + 1)
                    dve.tensor_tensor(v_lo[:, slot, b, :], v_raw[:, b, :], v_hi[:, slot, b, :].bitcast(F32),
                                      ALU.subtract).then_inc(v_lo_ready, 1)
                    dve.wait_ge(act_hi_ready, n + 1)
                    dve.tensor_tensor(act_lo[:, slot, b, :], hidden[:, b, :], act_hi[:, slot, b, :].bitcast(F32),
                                      ALU.subtract).then_inc(act_lo_ready, 1)

            def add_outputs(g):
                for unit in range(UNITS):
                    dve.wait_ge(unit_done, UNITS * (g + 2) + unit + 1)
                    x = X[:, unit // 2, (unit % 2) * HALF:(unit % 2 + 1) * HALF]
                    dve.tensor_tensor(x, ps[:, unit % OUT_BANKS, :], x, ALU.add).then_inc(added, 1)

            prepare(0, 0)
            with dve.Fori(0, GROUPS // 2 - 1) as two:
                for slot in range(2):
                    prepare(2 * two + slot + 1, 1 - slot)
                    add_outputs(2 * two + slot)
            prepare(GROUPS - 1, 1)
            add_outputs(GROUPS - 2)
            add_outputs(GROUPS - 1)


def hybrid_block(nc, x, w_in, pool_w, w_out, w_query, sub_keys, u, v, attn_g, q_g, k_g, pool_scale, ffn_g,
                 ident_d, cos_d, sin_d, mask_d, inv_count_d, iota_d, out):
    x_spill = nc.dram_tensor("x_spill", (T, D), F32).ap()
    gates = nc.dram_tensor("gates", (T // 64, KEYS, KEYS, 64), F32).ap()
    search_pairs, spread_pairs = 12, 16
    early = 2 * (search_pairs + spread_pairs)
    hidden_dram = nc.dram_tensor("hidden", (early, P, T), F32).ap()
    with ExitStack() as whole:
        sb = lambda ctx, n, s, dt=F32: ctx.enter_context(nc.sbuf_tensor(n, s, dt))
        ident = sb(whole, "ident", [P, P])
        X = sb(whole, "X", [P, NT, D])
        with ExitStack() as mixing:
            mixing.enter_context(nc.cleanup_on_exit())
            QKV = sb(mixing, "QKV", [P, NT, 3 * DA])
            poolT = sb(mixing, "poolT", [P, NG, PAD + T])
            OT = sb(mixing, "OT", [P, HEADS // 2, T])
            inv_sum = sb(mixing, "inv_sum", [P, NT, HEADS])
            with ExitStack() as ctx:
                hT = [sb(ctx, f"hT1_{n}", [P, KD, T], F32R) for n in ("hi", "lo")]
                scratch = OT[:, :, :].rearrange("p n d -> p (n d)")
                W = Weights(nc, ctx, "pi_w")
                norm_and_transpose(nc, "n1", X, x, attn_g, scratch, *hT, ident, ident_d, None, first_weights(W, w_in))
                project_inputs(nc, w_in, *hT, W, QKV, poolT, scratch, (cos_d, sin_d, q_g, k_g))
            with ExitStack() as ctx:
                QT = sb(ctx, "QT", [P, 8, T])
                loads = AttentionLoads(nc, ctx, QKV, mask_d, inv_count_d)
                turn_heads(nc, QKV, QT, ident, loads.first)
                pooled = attend(nc, QKV, QT, OT, inv_sum, poolT, loads, ident)
            with ExitStack() as ctx:
                mixT = [sb(ctx, f"mixT_{n}", [P, KD, T], F32R) for n in ("hi", "lo")]
                mix(nc, OT, inv_sum, pooled, pool_w, pool_scale, *mixT, ident)
                project_output(nc, w_out, *mixT, X)
        iota = sb(whole, "iota", [P, KEYS])
        hT = [sb(whole, f"hT2_{n}", [P, KD, T], F32R) for n in ("hi", "lo")]
        W = Weights(nc, whole, "rt_w")
        ahead = whole.enter_context(ExitStack())
        raw_keys, keys_in = sb(ahead, "raw_keys", [P, 2 * PH, P]), nc.alloc_semaphore("keys_in")
        iota_in = nc.alloc_semaphore("iota_in")
        with ExitStack() as ctx:
            scratch = sb(ctx, "scratch", [P, 4 * D])
            loads = [(raw_keys[:, :, :], sub_keys.rearrange("(g n) c -> n g c", n=KEYS), keys_in)]
            loads += first_weights(W, w_query) + [(iota[:, :], iota_d, iota_in)]
            norm_and_transpose(nc, "n2", X, None, ffn_g, scratch[:, :], *hT, ident, None, x_spill, loads)
        flat = X[:, :, :].rearrange("p n d -> p (n d)")
        scores = flat.rearrange("p (b t g n) -> p b t g n", b=2, t=NT, g=4)
        picksT = flat[:, 4 * D:4 * D + 5 * T // 2].bitcast(BF16).rearrange("p (a t) -> p a t", a=5)
        rest = flat[:, 0:2 * T].rearrange("p (a t) -> p a t", a=2)
        spread_u_in = [nc.alloc_semaphore(f"spread_u_in{s}") for s in range(2)]
        with ExitStack() as ctx:
            picks = sb(ctx, "picks", [P, NT, 3, KEYS])
            retrieve(nc, w_query, sub_keys, *hT, W, scores, picks, iota, iota_in, raw_keys, keys_in, ident, u,
                     hidden_dram, search_pairs, picksT, rest, spread_u_in)
        ahead.close()
        last_part = sb(whole, "last_part", [P, 32, 256])
        part_written, late_u_in = ([nc.alloc_semaphore(f"{n}{b}") for b in range(2)] for n in ("part_written", "late_u_in"))
        with ExitStack() as ctx:
            hidden_stored = spread_gates(nc, ctx, picksT, iota, ident, gates, W, X, hT, u, hidden_dram,
                                         2 * search_pairs, spread_pairs, last_part, part_written, spread_u_in, late_u_in)
        ee_raw = last_part[:, 0:24, :].rearrange("p a n -> p (a n)").rearrange("p (a g d) -> p a g d", a=3, g=2)
        ee_in = [nc.alloc_semaphore(f"ee_in{b}") for b in range(2)]
        mix_late_experts(nc, u, v, gates, hT, x_spill, X, ident, early, W, part_written, late_u_in, hidden_stored,
                         spread_pairs, hidden_dram, ee_raw, ee_in)
        mix_early_experts(nc, v, gates, hidden_dram, hT, X, out, early, ee_raw, ee_in)


def constants():
    freqs = np.float32(10000.0) ** (-np.arange(0, HD, 2, dtype=np.float32) / np.float32(HD))
    angle = np.arange(T, dtype=np.float32)[:, None] * freqs[None, :].astype(np.float32)
    back = np.arange(P)[:, None] - np.arange(T)[None, :] + (T - P)
    count = sum(((back >= 0) & (back <= window) & (back % dil == 0)).astype(np.int64)
                for window, dil in ((128, 1), (512, 4), (2048, 16)))
    mask = np.where(count > 0, np.log(np.maximum(count, 1)), NEG).astype(np.float32)
    t = np.arange(PAD)
    inv = np.stack([1.0 / np.minimum(t + 1, w) for w in WINDOWS]).astype(np.float32)
    return {
        "ident": np.eye(P, dtype=np.float32), "cos": np.cos(angle), "sin": np.sin(angle), "mask": mask,
        "inv_count": np.ascontiguousarray(np.broadcast_to(inv, (P, NG, PAD))),
        "iota": np.ascontiguousarray(np.broadcast_to(np.arange(KEYS, dtype=np.float32), (P, KEYS))),
    }


def kernel(**inputs):
    import concourse.bacc as bacc
    from concourse.bass_utils import run_bass_kernel_spmd

    shapes = {
        "x": (T, D), "w_in": (D, 3 * DA + NG * P), "pool_w": (NG, P, P), "w_out": (D, D),
        "peer_w_query": (D, PH * 2 * P), "peer_sub_keys": (PH * 2 * KEYS, P),
        "peer_u": (KEYS * KEYS, D), "peer_v": (KEYS * KEYS, D),
        "attn_norm_g": (D,), "q_norm_g": (HD,), "k_norm_g": (HD,), "pool_scale": (NG * P,), "ffn_norm_g": (D,),
    }
    nc = bacc.Bacc("TRN2", target_bir_lowering=False, num_devices=1)
    arrays = {f"in_{n}": np.ascontiguousarray(inputs[n]).reshape(s) for n, s in shapes.items()}
    arrays["in_pool_scale"] = np.ascontiguousarray(arrays["in_pool_scale"].reshape(NG, P).T)
    arrays |= {f"const_{n}": a for n, a in constants().items()}
    args = [nc.dram_tensor(n, a.shape, mybir.dt.from_np(a.dtype), kind="ExternalInput").ap() for n, a in arrays.items()]
    out = nc.dram_tensor("out", (T, D), F32, kind="ExternalOutput").ap()
    hybrid_block(nc, *args, out)
    r = run_bass_kernel_spmd(nc, [arrays], core_ids=[0])
    return r.results[0]["out"].reshape(1, T, D)
```
